# Optimizing a Trainium2 kernel written in Bass

```python
import jax, jax.numpy as jnp
from jax import lax
import numpy as np

D_MODEL = 1024
BATCH = 1
SEQ = 256
DEPTH = 1

N_HEADS_A = 8
N_KV_HEADS_A = 2
HEAD_DIM_A = 64
IDX_HEADS = 8
IDX_DIM = 64
TOPK_MAX = 256
Q_BLOCK = 128
CONV_CH = 512
CONV_WIDTH = 31
N_MEM = 256
MEM_HEADS = 4
MEM_HEAD_DIM = 128
N_BRANCHES = 3
N_GROUPS = 4
EXPERTS_PER_GROUP = 8
N_EXPERTS = N_GROUPS * EXPERTS_PER_GROUP
TOP_K_INNER = 2
D_FF_EXPERT = 256

ROPE_THETA = 10000.0
EPS = 1e-6

SPLIT_SIZES = (
    N_HEADS_A * HEAD_DIM_A,
    N_KV_HEADS_A * HEAD_DIM_A,
    N_KV_HEADS_A * HEAD_DIM_A,
    IDX_HEADS * IDX_DIM,
    IDX_DIM,
    IDX_HEADS,
    2 * CONV_CH,
    MEM_HEADS * MEM_HEAD_DIM,
    N_BRANCHES * D_MODEL,
)
IN_COLS = sum(SPLIT_SIZES)


def rmsnorm(x, g):
    xf = x.astype(jnp.float32)
    y = xf * lax.rsqrt(jnp.mean(xf * xf, axis=-1, keepdims=True) + EPS)
    return (y * g.astype(jnp.float32)).astype(x.dtype)

def layernorm(x, g, b):
    xf = x.astype(jnp.float32)
    mu = jnp.mean(xf, axis=-1, keepdims=True)
    var = jnp.mean(jnp.square(xf - mu), axis=-1, keepdims=True)
    y = (xf - mu) * lax.rsqrt(var + EPS)
    return (y * g.astype(jnp.float32) + b.astype(jnp.float32)).astype(x.dtype)

def rope(x, pos):
    d = x.shape[-1]
    half = d // 2
    inv = ROPE_THETA ** (-jnp.arange(half, dtype=jnp.float32) / half)
    ang = pos.astype(jnp.float32)[:, None] * inv[None, :]
    cos = jnp.cos(ang)[None, :, None, :]
    sin = jnp.sin(ang)[None, :, None, :]
    xf = x.astype(jnp.float32)
    x1, x2 = xf[..., :half], xf[..., half:]
    out = jnp.concatenate([x1 * cos - x2 * sin, x2 * cos + x1 * sin], axis=-1)
    return out.astype(x.dtype)

def dsa_attention(q, k, v, q_idx, k_idx, w_idx, topk):
    B, S = q.shape[0], q.shape[1]
    G = N_HEADS_A // N_KV_HEADS_A
    n_blocks = S // Q_BLOCK
    key_pos = jnp.arange(S)
    w_idx = w_idx.astype(jnp.float32) * (IDX_HEADS ** -0.5)
    scale = HEAD_DIM_A ** -0.5

    def block(i):
        start = i * Q_BLOCK
        qb = lax.dynamic_slice_in_dim(q, start, Q_BLOCK, axis=1)
        qib = lax.dynamic_slice_in_dim(q_idx, start, Q_BLOCK, axis=1)
        wib = lax.dynamic_slice_in_dim(w_idx, start, Q_BLOCK, axis=1)
        tpos = start + jnp.arange(Q_BLOCK)
        logits = jnp.einsum('bqhd,bsd->bqhs', qib, k_idx,
                            preferred_element_type=jnp.float32) * (IDX_DIM ** -0.5)
        score = jnp.einsum('bqh,bqhs->bqs', wib, jax.nn.relu(logits))
        causal = key_pos[None, :] <= tpos[:, None]
        score = jnp.where(causal[None], score, -jnp.inf)
        _, sel = lax.top_k(score, topk)
        valid = sel <= tpos[None, :, None]
        kg = jax.vmap(lambda kk, ii: kk[ii])(k, sel)
        vg = jax.vmap(lambda vv, ii: vv[ii])(v, sel)
        qg = qb.reshape(B, Q_BLOCK, N_KV_HEADS_A, G, HEAD_DIM_A)
        s = jnp.einsum('bqhgd,bqkhd->bqhgk', qg, kg,
                       preferred_element_type=jnp.float32) * scale
        s = jnp.where(valid[:, :, None, None, :], s, -jnp.inf)
        p = jax.nn.softmax(s, axis=-1)
        o = jnp.einsum('bqhgk,bqkhd->bqhgd', p.astype(vg.dtype), vg)
        return o.reshape(B, Q_BLOCK, N_HEADS_A * HEAD_DIM_A)

    out = lax.map(block, jnp.arange(n_blocks))
    return jnp.moveaxis(out, 0, 1).reshape(B, S, N_HEADS_A * HEAD_DIM_A)

def conformer_conv(conv_in, conv_w, conv_b, ln_g, ln_b):
    a, gte = jnp.split(conv_in, 2, axis=-1)
    u = a * jax.nn.sigmoid(gte)
    y = lax.conv_general_dilated(
        u, conv_w, window_strides=(1,), padding=[(CONV_WIDTH - 1, 0)],
        dimension_numbers=('NWC', 'WIO', 'NWC'), feature_group_count=CONV_CH)
    y = y + conv_b
    return jax.nn.silu(layernorm(y, ln_g, ln_b))

def memory_attention(q_m, mem, g_mem, w_mem_kv, g_qm, g_km):
    B, S = q_m.shape[0], q_m.shape[1]
    M = mem.shape[1]
    kv = jnp.einsum('bmd,dc->bmc', rmsnorm(mem, g_mem), w_mem_kv)
    k_m, v_m = jnp.split(kv, 2, axis=-1)
    k_m = rmsnorm(k_m.reshape(B, M, MEM_HEADS, MEM_HEAD_DIM), g_km)
    v_m = v_m.reshape(B, M, MEM_HEADS, MEM_HEAD_DIM)
    q = rmsnorm(q_m.reshape(B, S, MEM_HEADS, MEM_HEAD_DIM), g_qm)
    s = jnp.einsum('bshd,bmhd->bhsm', q, k_m,
                   preferred_element_type=jnp.float32) * (MEM_HEAD_DIM ** -0.5)
    p = jax.nn.softmax(s, axis=-1)
    o = jnp.einsum('bhsm,bmhd->bshd', p.astype(v_m.dtype), v_m)
    return o.reshape(B, S, MEM_HEADS * MEM_HEAD_DIM)

def hier_moe(h, w_rg, b_rg, w_re, b_re, w_up, w_down):
    T = h.shape[0]
    g_logits = (h @ w_rg + b_rg).astype(jnp.float32)
    p_g = jax.nn.softmax(g_logits, axis=-1)
    g_sel = jnp.argmax(g_logits, axis=-1)
    p_sel = jnp.take_along_axis(p_g, g_sel[:, None], axis=1)
    e_logits = (h @ w_re + b_re).astype(jnp.float32).reshape(T, N_GROUPS, EXPERTS_PER_GROUP)
    e_in = jnp.take_along_axis(e_logits, g_sel[:, None, None], axis=1)[:, 0]
    top_v, top_i = lax.top_k(e_in, TOP_K_INNER)
    w2 = jax.nn.softmax(top_v, axis=-1) * p_sel
    expert_id = g_sel[:, None] * EXPERTS_PER_GROUP + top_i
    combine = jnp.sum(jax.nn.one_hot(expert_id, N_EXPERTS, dtype=jnp.float32)
                      * w2[..., None], axis=1).astype(h.dtype)
    out = jnp.zeros_like(h)
    for n in range(N_EXPERTS):
        a, b = jnp.split(h @ w_up[n], 2, axis=-1)
        out = out + combine[:, n:n + 1] * ((jax.nn.silu(a) * b) @ w_down[n])
    return out

def first_inputs(seed: int = 0) -> dict:
    key = jax.random.key(seed)
    ks = jax.random.split(key, 28)
    f32 = jnp.float32
    L = DEPTH

    def nrm(k, shape, fan_in):
        return jax.random.normal(k, shape, f32) * (fan_in ** -0.5)

    def gain(k, shape):
        return 1.0 + 0.05 * jax.random.normal(k, shape, f32)

    def small(k, shape, s):
        return s * jax.random.normal(k, shape, f32)

    return {
        "x": jax.random.normal(ks[0], (BATCH, SEQ, D_MODEL), f32),
        "mem": jax.random.normal(ks[1], (BATCH, N_MEM, D_MODEL), f32),
        "g_mix": gain(ks[2], (L, D_MODEL)),
        "w_in": nrm(ks[3], (L, D_MODEL, IN_COLS), D_MODEL),
        "b_gate": small(ks[4], (L, N_BRANCHES * D_MODEL), 0.02),
        "g_qa": gain(ks[5], (L, HEAD_DIM_A)),
        "g_ka": gain(ks[6], (L, HEAD_DIM_A)),
        "g_idx_k": gain(ks[7], (L, IDX_DIM)),
        "conv_w": nrm(ks[8], (L, CONV_WIDTH, 1, CONV_CH), CONV_WIDTH),
        "conv_b": small(ks[9], (L, CONV_CH), 0.02),
        "ln_g": gain(ks[10], (L, CONV_CH)),
        "ln_b": small(ks[11], (L, CONV_CH), 0.02),
        "g_mem": gain(ks[12], (L, D_MODEL)),
        "w_mem_kv": nrm(ks[13], (L, D_MODEL, 2 * MEM_HEADS * MEM_HEAD_DIM), D_MODEL),
        "g_qm": gain(ks[14], (L, MEM_HEAD_DIM)),
        "g_km": gain(ks[15], (L, MEM_HEAD_DIM)),
        "w_br_a": nrm(ks[16], (L, N_HEADS_A * HEAD_DIM_A, D_MODEL), N_HEADS_A * HEAD_DIM_A),
        "w_br_b": nrm(ks[17], (L, CONV_CH, D_MODEL), CONV_CH),
        "w_br_m": nrm(ks[18], (L, MEM_HEADS * MEM_HEAD_DIM, D_MODEL), MEM_HEADS * MEM_HEAD_DIM),
        "w_o": nrm(ks[19], (L, D_MODEL, D_MODEL), D_MODEL),
        "g_ffn": gain(ks[20], (L, D_MODEL)),
        "w_rg": nrm(ks[21], (L, D_MODEL, N_GROUPS), D_MODEL),
        "b_rg": small(ks[22], (L, N_GROUPS), 0.01),
        "w_re": nrm(ks[23], (L, D_MODEL, N_EXPERTS), D_MODEL),
        "b_re": small(ks[24], (L, N_EXPERTS), 0.01),
        "w_up": nrm(ks[25], (L, N_EXPERTS, D_MODEL, 2 * D_FF_EXPERT), D_MODEL),
        "w_down": nrm(ks[26], (L, N_EXPERTS, D_FF_EXPERT, D_MODEL), D_FF_EXPERT),
    }

def first_block(x, mem, g_mix, w_in, b_gate, g_qa, g_ka, g_idx_k, conv_w, conv_b, ln_g, ln_b,
              g_mem, w_mem_kv, g_qm, g_km, w_br_a, w_br_b, w_br_m, w_o, g_ffn,
              w_rg, b_rg, w_re, b_re, w_up, w_down):
    B, S, D = x.shape
    topk = min(TOPK_MAX, S // 4)
    pos = jnp.arange(S, dtype=jnp.int32)
    split_points = []
    acc = 0
    for sz in SPLIT_SIZES[:-1]:
        acc += sz
        split_points.append(acc)

    for l in range(DEPTH):
        h = rmsnorm(x, g_mix[l])
        proj = jnp.einsum('bsd,dc->bsc', h, w_in[l])
        q_a, k_a, v_a, q_i, k_i, w_i, conv_in, q_m, gate_logits = jnp.split(
            proj, split_points, axis=-1)

        q_a = rope(rmsnorm(q_a.reshape(B, S, N_HEADS_A, HEAD_DIM_A), g_qa[l]), pos)
        k_a = rope(rmsnorm(k_a.reshape(B, S, N_KV_HEADS_A, HEAD_DIM_A), g_ka[l]), pos)
        v_a = v_a.reshape(B, S, N_KV_HEADS_A, HEAD_DIM_A)
        q_i = rope(q_i.reshape(B, S, IDX_HEADS, IDX_DIM), pos)
        k_i = rope(rmsnorm(k_i, g_idx_k[l])[:, :, None, :], pos)[:, :, 0, :]
        o_a = dsa_attention(q_a, k_a, v_a, q_i, k_i, w_i, topk)

        o_b = conformer_conv(conv_in, conv_w[l], conv_b[l], ln_g[l], ln_b[l])

        o_m = memory_attention(q_m, mem, g_mem[l], w_mem_kv[l], g_qm[l], g_km[l])

        gates = jax.nn.sigmoid((gate_logits + b_gate[l]).astype(jnp.float32)).astype(x.dtype)
        gates = gates.reshape(B, S, N_BRANCHES, D)
        merged = (gates[:, :, 0] * (o_a @ w_br_a[l])
                  + gates[:, :, 1] * (o_b @ w_br_b[l])
                  + gates[:, :, 2] * (o_m @ w_br_m[l]))
        x = x + merged @ w_o[l]

        h2 = rmsnorm(x, g_ffn[l]).reshape(B * S, D)
        moe = hier_moe(h2, w_rg[l], b_rg[l], w_re[l], b_re[l], w_up[l], w_down[l])
        x = x + moe.reshape(B, S, D)
    return x


DEPTH_2 = 2

HEAD_DIM = 64
MIX_WIDTH = D_MODEL
ATT_Q_HEADS = (MIX_WIDTH // 2) // HEAD_DIM
ATT_KV_HEADS = 2
ATT_GROUP = ATT_Q_HEADS // ATT_KV_HEADS
ATT_WIDTH = ATT_Q_HEADS * HEAD_DIM
ATT_KV_WIDTH = ATT_KV_HEADS * HEAD_DIM
WINDOW = 128
BLOCK = 128
RWKV_HEADS = (MIX_WIDTH // 4) // HEAD_DIM
RWKV_WIDTH = RWKV_HEADS * HEAD_DIM
DECAY_LORA = 64
ICLR_LORA = 64
GATE_LORA = 128
RWKV_GN_EPS = 64e-5
CONV_WIDTH_2 = MIX_WIDTH - ATT_WIDTH - RWKV_WIDTH
CONV_K = 3
ATT_PROJ_WIDTH = ATT_WIDTH + 2 * ATT_KV_WIDTH
RWKV_SIZES = (RWKV_WIDTH, RWKV_WIDTH, RWKV_WIDTH, DECAY_LORA, ICLR_LORA, GATE_LORA)
RWKV_PROJ_WIDTH = 3 * RWKV_WIDTH + DECAY_LORA + ICLR_LORA + GATE_LORA
CONV_PROJ_WIDTH = 3 * CONV_WIDTH_2
PROJ_WIDTH = ATT_PROJ_WIDTH + RWKV_PROJ_WIDTH + CONV_PROJ_WIDTH
D_FF = 2816
N_MOD = 9


def rms_norm(x, gain):
    xf = x.astype(jnp.float32)
    y = xf * lax.rsqrt(jnp.mean(xf * xf, axis=-1, keepdims=True) + EPS)
    return (y * gain.astype(jnp.float32)).astype(x.dtype)

def swiglu(x, w_in, w_out):
    gate, up = jnp.split(x @ w_in, 2, axis=-1)
    return (jax.nn.silu(gate) * up) @ w_out

def token_shift(p):
    return jnp.pad(p, ((0, 0), (1, 0), (0, 0)))[:, :-1]

def sliding_window_sink_attention(qkv, q_gain, k_gain, sinks):
    B, T, _ = qkv.shape
    nb = T // BLOCK
    q, k, v = jnp.split(qkv, [ATT_WIDTH, ATT_WIDTH + ATT_KV_WIDTH], axis=-1)
    q = rms_norm(q.reshape(B, T, ATT_Q_HEADS, HEAD_DIM), q_gain)
    k = rms_norm(k.reshape(B, T, ATT_KV_HEADS, HEAD_DIM), k_gain)
    v = v.reshape(B, T, ATT_KV_HEADS, HEAD_DIM)
    qb = q.reshape(B, nb, BLOCK, ATT_KV_HEADS, ATT_GROUP, HEAD_DIM)

    def band(z):
        zb = z.reshape(B, nb, BLOCK, ATT_KV_HEADS, HEAD_DIM)
        prev = jnp.pad(zb, ((0, 0), (1, 0), (0, 0), (0, 0), (0, 0)))[:, :-1]
        return jnp.concatenate([prev, zb], axis=2)

    kb, vb = band(k), band(v)
    scores = jnp.einsum('bnqhgd,bnkhd->bnhgqk', qb, kb).astype(jnp.float32) * (HEAD_DIM ** -0.5)
    blk = jnp.arange(nb)[:, None, None] * BLOCK
    q_pos = blk + jnp.arange(BLOCK)[None, :, None]
    k_pos = blk - BLOCK + jnp.arange(2 * BLOCK)[None, None, :]
    diff = q_pos - k_pos
    mask = (k_pos >= 0) & (diff >= 0) & (diff < WINDOW)
    scores = jnp.where(mask[None, :, None, None], scores, -jnp.inf)
    sink = sinks.astype(jnp.float32).reshape(ATT_KV_HEADS, ATT_GROUP)[None, None, :, :, None, None]
    sink = jnp.broadcast_to(sink, scores.shape[:-1] + (1,))
    probs = jax.nn.softmax(jnp.concatenate([scores, sink], axis=-1), axis=-1)[..., :-1]
    out = jnp.einsum('bnhgqk,bnkhd->bnqhgd', probs.astype(v.dtype), vb)
    return out.reshape(B, T, ATT_WIDTH)

def rwkv7_time_mix(p, mu, w0, w_w2, a0, w_a2, w_g2, k_k, k_a, r_k, gn_w, gn_b):
    B, T, _ = p.shape
    f32 = jnp.float32
    p = p + mu * (token_shift(p) - p)
    r, k, v, wd, ad, gd = jnp.split(p, np.cumsum(RWKV_SIZES)[:-1].tolist(), axis=-1)
    r, k, v = r.astype(f32), k.astype(f32), v.astype(f32)
    w_log = -jax.nn.softplus(-(w0 + jnp.tanh(wd) @ w_w2).astype(f32)) - 0.5
    decay = jnp.exp(-jnp.exp(w_log))
    a = jax.nn.sigmoid((a0 + ad @ w_a2).astype(f32))
    g = (jax.nn.sigmoid(gd) @ w_g2).astype(f32)
    kk = (k * k_k).reshape(B, T, RWKV_HEADS, HEAD_DIM)
    kk = kk / jnp.maximum(jnp.linalg.norm(kk, axis=-1, keepdims=True), 1e-12)
    k = k * (1.0 + (a - 1.0) * k_a)
    hs = lambda z: z.reshape(B, T, RWKV_HEADS, HEAD_DIM)
    r, k, v, a, decay = hs(r), hs(k), hs(v), hs(a), hs(decay)

    def step(S, inp):
        r_t, w_t, k_t, v_t, kk_t, a_t = inp
        s_kk = jnp.einsum('bhvk,bhk->bhv', S, kk_t)
        S = (S * w_t[:, :, None, :] - s_kk[..., None] * (kk_t * a_t)[:, :, None, :]
             + v_t[..., None] * k_t[:, :, None, :])
        return S, jnp.einsum('bhvk,bhk->bhv', S, r_t)

    xs = tuple(jnp.swapaxes(z, 0, 1) for z in (r, decay, k, v, kk, a))
    S0 = jnp.zeros((B, RWKV_HEADS, HEAD_DIM, HEAD_DIM), f32)
    _, y = lax.scan(step, S0, xs)
    y = jnp.swapaxes(y, 0, 1)
    mean = jnp.mean(y, axis=-1, keepdims=True)
    var = jnp.mean(jnp.square(y - mean), axis=-1, keepdims=True)
    y = ((y - mean) * lax.rsqrt(var + RWKV_GN_EPS)).reshape(B, T, RWKV_WIDTH) * gn_w + gn_b
    bonus = jnp.sum(r * k * r_k, axis=-1, keepdims=True) * v
    y = (y + bonus.reshape(B, T, RWKV_WIDTH)) * g
    return y.astype(p.dtype)

def short_conv_mix(p, conv_w):
    b_gate, c_gate, h = jnp.split(p, [CONV_WIDTH_2, 2 * CONV_WIDTH_2], axis=-1)
    u = c_gate * h
    y = lax.conv_general_dilated(u, conv_w[:, None, :].astype(u.dtype), window_strides=(1,),
                                 padding=[(CONV_K - 1, 0)], dimension_numbers=('NWC', 'WIO', 'NWC'),
                                 feature_group_count=CONV_WIDTH_2)
    return b_gate * y

def second_inputs(seed: int = 0) -> dict:
    key = jax.random.key(seed)
    ks = iter(jax.random.split(key, 32))
    nrm = lambda shape, s: jax.random.normal(next(ks), shape, jnp.float32) * s
    L, D = DEPTH_2, D_MODEL
    return {
        'x': nrm((BATCH, SEQ, D), 1.0),
        'c': nrm((BATCH, D), 1.0),
        'w_ada': nrm((L, D, N_MOD * D), 0.1 * D ** -0.5),
        'b_ada': nrm((L, N_MOD * D), 0.01),
        'g_ffn1': 1.0 + nrm((L, D), 0.05),
        'w_ffn1_in': nrm((L, D, 2 * D_FF), D ** -0.5),
        'w_ffn1_out': nrm((L, D_FF, D), D_FF ** -0.5),
        'g_mix': 1.0 + nrm((L, D), 0.05),
        'w_mix_in': nrm((L, D, PROJ_WIDTH), D ** -0.5),
        'w_mix_out': nrm((L, MIX_WIDTH, D), MIX_WIDTH ** -0.5),
        'att_q_gain': 1.0 + nrm((L, HEAD_DIM), 0.05),
        'att_k_gain': 1.0 + nrm((L, HEAD_DIM), 0.05),
        'att_sinks': nrm((L, ATT_Q_HEADS), 1.0),
        'rwkv_mu': jax.random.uniform(next(ks), (L, RWKV_PROJ_WIDTH), jnp.float32),
        'rwkv_w0': jax.random.uniform(next(ks), (L, RWKV_WIDTH), jnp.float32, -6.0, -1.0),
        'rwkv_w_w2': nrm((L, DECAY_LORA, RWKV_WIDTH), 0.1 * DECAY_LORA ** -0.5),
        'rwkv_a0': nrm((L, RWKV_WIDTH), 0.1),
        'rwkv_a_w2': nrm((L, ICLR_LORA, RWKV_WIDTH), 0.1 * ICLR_LORA ** -0.5),
        'rwkv_g_w2': nrm((L, GATE_LORA, RWKV_WIDTH), GATE_LORA ** -0.5),
        'rwkv_k_k': 1.0 + nrm((L, RWKV_WIDTH), 0.1),
        'rwkv_k_a': 1.0 + nrm((L, RWKV_WIDTH), 0.1),
        'rwkv_r_k': nrm((L, RWKV_HEADS, HEAD_DIM), 0.1),
        'rwkv_gn_w': 1.0 + nrm((L, RWKV_WIDTH), 0.05),
        'rwkv_gn_b': nrm((L, RWKV_WIDTH), 0.01),
        'conv_w': nrm((L, CONV_K, CONV_WIDTH_2), CONV_K ** -0.5),
        'g_ffn2': 1.0 + nrm((L, D), 0.05),
        'w_ffn2_in': nrm((L, D, 2 * D_FF), D ** -0.5),
        'w_ffn2_out': nrm((L, D_FF, D), D_FF ** -0.5),
    }

def second_block(x, c, w_ada, b_ada, g_ffn1, w_ffn1_in, w_ffn1_out, g_mix, w_mix_in, w_mix_out,
              att_q_gain, att_k_gain, att_sinks, rwkv_mu, rwkv_w0, rwkv_w_w2, rwkv_a0, rwkv_a_w2,
              rwkv_g_w2, rwkv_k_k, rwkv_k_a, rwkv_r_k, rwkv_gn_w, rwkv_gn_b, conv_w,
              g_ffn2, w_ffn2_in, w_ffn2_out):
    h = x
    B = x.shape[0]
    c_act = jax.nn.silu(c)
    for l in range(DEPTH_2):
        mod = (c_act @ w_ada[l] + b_ada[l]).reshape(B, N_MOD, D_MODEL)
        sh1, sc1, gt1, sh2, sc2, gt2, sh3, sc3, gt3 = [mod[:, i, None, :] for i in range(N_MOD)]
        hn = rms_norm(h, g_ffn1[l]) * (1.0 + sc1) + sh1
        h = h + 0.5 * (1.0 + gt1) * swiglu(hn, w_ffn1_in[l], w_ffn1_out[l])
        hn = rms_norm(h, g_mix[l]) * (1.0 + sc2) + sh2
        proj = hn @ w_mix_in[l]
        p_att, p_rwkv, p_conv = jnp.split(proj, [ATT_PROJ_WIDTH, ATT_PROJ_WIDTH + RWKV_PROJ_WIDTH], axis=-1)
        y_att = sliding_window_sink_attention(p_att, att_q_gain[l], att_k_gain[l], att_sinks[l])
        y_rwkv = rwkv7_time_mix(p_rwkv, rwkv_mu[l], rwkv_w0[l], rwkv_w_w2[l], rwkv_a0[l], rwkv_a_w2[l],
                                rwkv_g_w2[l], rwkv_k_k[l], rwkv_k_a[l], rwkv_r_k[l], rwkv_gn_w[l], rwkv_gn_b[l])
        y_conv = short_conv_mix(p_conv, conv_w[l])
        mixed = jnp.concatenate([y_att, y_rwkv, y_conv], axis=-1) @ w_mix_out[l]
        h = h + (1.0 + gt2) * mixed
        hn = rms_norm(h, g_ffn2[l]) * (1.0 + sc3) + sh3
        h = h + 0.5 * (1.0 + gt3) * swiglu(hn, w_ffn2_in[l], w_ffn2_out[l])
    return h


def setup_inputs(seed=0):
    out = dict(first_inputs(seed))
    for name, value in second_inputs(seed + 1).items():
        if name != "x":
            out[name + "_2"] = value
    return out


def reference(
    x, mem, g_mix, w_in, b_gate, g_qa, g_ka, g_idx_k, conv_w, conv_b, ln_g, ln_b, g_mem,
    w_mem_kv, g_qm, g_km, w_br_a, w_br_b, w_br_m, w_o, g_ffn, w_rg, b_rg, w_re, b_re, w_up,
    w_down, c_2, w_ada_2, b_ada_2, g_ffn1_2, w_ffn1_in_2, w_ffn1_out_2, g_mix_2, w_mix_in_2,
    w_mix_out_2, att_q_gain_2, att_k_gain_2, att_sinks_2, rwkv_mu_2, rwkv_w0_2, rwkv_w_w2_2,
    rwkv_a0_2, rwkv_a_w2_2, rwkv_g_w2_2, rwkv_k_k_2, rwkv_k_a_2, rwkv_r_k_2, rwkv_gn_w_2,
    rwkv_gn_b_2, conv_w_2, g_ffn2_2, w_ffn2_in_2, w_ffn2_out_2,
):
    x = first_block(
        x, mem, g_mix, w_in, b_gate, g_qa, g_ka, g_idx_k, conv_w, conv_b, ln_g, ln_b, g_mem,
        w_mem_kv, g_qm, g_km, w_br_a, w_br_b, w_br_m, w_o, g_ffn, w_rg, b_rg, w_re, b_re, w_up,
        w_down,
    )
    return second_block(
        x, c_2, w_ada_2, b_ada_2, g_ffn1_2, w_ffn1_in_2, w_ffn1_out_2, g_mix_2, w_mix_in_2,
        w_mix_out_2, att_q_gain_2, att_k_gain_2, att_sinks_2, rwkv_mu_2, rwkv_w0_2, rwkv_w_w2_2,
        rwkv_a0_2, rwkv_a_w2_2, rwkv_g_w2_2, rwkv_k_k_2, rwkv_k_a_2, rwkv_r_k_2, rwkv_gn_w_2,
        rwkv_gn_b_2, conv_w_2, g_ffn2_2, w_ffn2_in_2, w_ffn2_out_2,
    )


_drawn_inputs = setup_inputs


def setup_inputs(seed=0):
    import zlib

    import numpy as np

    out = dict(_drawn_inputs(seed))
    spreads = {}
    factors = {'b_gate': 8.0,
     'ln_b': 4.933,
     'g_mem': 3.443,
     'g_qm': 8.0,
     'g_km': 3.572,
     'b_re': 8.0,
     'att_q_gain_2': 7.604,
     'att_k_gain_2': 7.569,
     'att_sinks_2': 12.271,
     'rwkv_w_w2_2': 8.0,
     'rwkv_a0_2': 3.63,
     'rwkv_a_w2_2': 4.054,
     'rwkv_k_k_2': 2.67,
     'rwkv_gn_w_2': 3.482,
     'rwkv_gn_b_2': 21.868}
    for name, (base, spread) in spreads.items():
        noise = np.random.default_rng([zlib.crc32(name.encode()), seed]).standard_normal(out[name].shape)
        drawn = base * np.exp(spread * noise) if base else spread * noise
        out[name] = __import__('jax').numpy.asarray(drawn.astype(out[name].dtype))
    for name, factor in factors.items():
        out[name] = (out[name] * factor).astype(out[name].dtype)
    return out
```

```python
import math
from contextlib import ExitStack

import numpy as np
import concourse.bass as bass
from concourse import mybir

P = 128
D = 1024
KD = D // P
T = 256
NT = T // P
EPS = 1e-6
NEG = -1e30
PAD = -3e38
TAKEN1 = 3e38
TAKEN2 = 2e38
TOPK = 64
HEADS = 8
N_EXP = 32
N_GROUP = 4
PER_GROUP = N_EXP // N_GROUP
TAPS = 31
LAYERS = 2
D_FF = 2816
CHUNK = 64
SLOTS = 6
SLAB = 2048
RING = 7
ADA_COLS = 576
ADA_SLABS = 9 * D // ADA_COLS
DECAY_C = math.exp(-0.5)
KK_SHIFT = 24

def _constants():
    eye = np.eye(P, dtype=np.float32)
    ones = np.ones((P, P), np.float32)
    p = np.arange(P)
    half = (p[:, None] // 64 == p[None, :] // 64).astype(np.float32)
    rot = np.zeros((P, P), np.float32)
    for m in range(P):
        if m % 64 < 32:
            rot[m + 32, m] = -1.0
        else:
            rot[m - 32, m] = 1.0
    dup0 = (p[:, None] == p[None, :] % 64).astype(np.float32)
    dup1 = (p[:, None] == 64 + p[None, :] % 64).astype(np.float32)
    inv = np.float32(10000.0) ** (-np.arange(32, dtype=np.float32) / np.float32(32))
    ang = np.arange(T, dtype=np.float32)[None, :] * inv[p % 32][:, None].astype(np.float32)
    cos, sin = np.cos(ang).astype(np.float32), np.sin(ang).astype(np.float32)
    key = np.arange(T)
    causal0 = np.where(key[None, :P] <= p[:, None], 0.0, NEG).astype(np.float32)
    causal1 = np.where(key[None, :] <= P + p[:, None], 0.0, NEG).astype(np.float32)
    gap = P + p[:, None] - key[None, :]
    window1 = np.where((gap >= 0) & (gap < 128), 0.0, NEG).astype(np.float32)
    same = p[:, None] // CHUNK == p[None, :] // CHUNK
    strict = (same & (p[:, None] < p[None, :])).astype(np.float32)
    incl = (same & (p[:, None] <= p[None, :])).astype(np.float32)
    levels = []
    for m in (1, 2, 4, 8, 16, 32):
        blk = p[:, None] // (2 * m) == p[None, :] // (2 * m)
        levels.append((blk & (p[:, None] % (2 * m) < m) & (p[None, :] % (2 * m) >= m)).astype(np.float32))
    reset = np.tile((np.arange(T) % CHUNK != 0).astype(np.float32), (P, 1))
    small = np.zeros((P, 8), np.float32)
    small[:, 0] = EPS
    small[:, 1] = 64e-5
    small[:, 2] = 0.5 * KK_SHIFT * math.log(2.0)
    parts = dict(eye=eye, ones=ones, half=half, rot=rot, dup0=dup0, dup1=dup1, small=small, cos=cos,
                 sin=sin, causal0=causal0, causal1=causal1, window1=window1, strict=strict, incl=incl,
                 reset=reset, **{f"level{n}": v for n, v in enumerate(levels)})
    at, where = 0, {}
    for name, v in parts.items():
        where[name] = (at, v.shape[1])
        at += v.shape[1]
    return np.ascontiguousarray(np.concatenate(list(parts.values()), axis=1)), where


ROWS_1 = [("g_mix", 8), ("g_mem", 8), ("g_ffn", 8), ("b_gate", 24), ("conv_b", 4), ("ln_g", 4),
          ("ln_b", 4), ("g_qa", 1), ("g_ka", 1), ("g_idx_k", 1), ("g_qm", 1), ("g_km", 1), ("c_2", 8)]
ROWS_2 = [("g_ffn1_2", 8), ("g_mix_2", 8), ("g_ffn2_2", 8), ("att_q_gain_2", 1), ("att_k_gain_2", 1),
          ("rwkv_mu_2", 8), ("rwkv_w0_2", 2), ("rwkv_a0_2", 2), ("rwkv_k_k_2", 2), ("rwkv_k_a_2", 2),
          ("rwkv_r_k_2", 2), ("rwkv_gn_w_2", 2), ("rwkv_gn_b_2", 2), ("conv_w_2", 6)]

SEMAPHORES = {
    "const_in": "constants", "x_in": "tokens", "mem_in": "memory tokens", "rows_in": "the small inputs",
    **{f"slab{s}_in": "a weight slab in this slot" for s in range(SLOTS)},
    **{f"ada{s}_in": "a slab of w_ada" for s in range(2)}, "out_written": "the result is in DRAM",
    "for_act": "a product for ScalarE", "for_dve": "a product for VectorE",
    "read_by_act": "ScalarE has read one and written what came of it",
    "read_by_dve": "VectorE has read one and written what came of it",
    "up_done": "gate|up of 128 hidden features", "down_done": "a unit's part of the output",
    "comb_done": "an expert's combine weights on every partition", "ada_sum": "adaLN sums over partitions",
    "y_done": "the recurrence's output is complete",
    "act_step": "a step of its own chain", "params": "parameter columns", "c_act": "silu(c)",
    "sq": "four chunks of squares", "rs": "reciprocal norms", "ki_sq": "squares of the index key",
    "qka_sq": "squares of attention queries and key", "qkm_sq": "squares of memory queries and keys",
    "rl_ready": "rectified index logits", "glu_in": "conv value and gate", "att_exp": "exponentials and sums",
    "att_pT": "transposed probabilities", "oa_ready": "sparse attention output", "om_ready": "memory attention output",
    "swa_ready": "window attention output", "ob_ready": "conv branch output", "router_exp": "the router's exponentials",
    "silu_ready": "silu of a gate block", "praw_ready": "RWKV projections", "lora_in": "low-rank inputs",
    "sw_ready": "decay and rate sigmoids", "kk_sq": "squares of the removal key", "att_sq": "squares of q and k",
    "w_ready": "decay products", "sconv_in": "short conv inputs", "m1_ready": "first half of a doubling",
    "r_ready": "a chunk's right-hand side", "yc_sq": "squares of the centred output",
    "kdup_ready": "keys on both partition halves",
    "dve_step": "a step of its own chains", "hn": "a chunk of the normalised residual",
    "memh": "a chunk of the normalised memory", "memh_all": "all of it, its source is free",
    "rs_used": "the reciprocal norms are used", "ki_normed": "index key, normed", "idx_roped": "index queries and key",
    "qka_normed": "queries and key, normed", "rl_used": "rectified logits are used", "qa_roped": "queries, rotated",
    "ka_roped": "key, rotated", "dsa_mask": "the mask of selected keys", "qkm_normed": "memory queries and keys, normed",
    "conv_y": "convolution output", "att_max": "scaled scores and their maxima", "att_p": "probabilities",
    "yc_ready": "centred output", "yn_ready": "scaled output", "merged": "gated sum of the branches",
    "x_ready": "a chunk of the residual", "x_ready_pe": "the last residual", "router_max": "the groups' maximum",
    "router_top2": "the two best experts' logits", "comb_ready": "combine weights", "b1_done": "block 1's region is free",
    "zero": "a zero operand", "sel": "an expert's row of the combine weights", "gut": "silu times combine weight",
    "gu_ready": "a block of hidden activations", "ada_step": "one chunk of an adaLN slab added",
    "ada_done": "a pair of adaLN slabs added up", "ada_ready": "nine adaLN columns", "state_ready": "the recurrent state",
    "pm_ready": "token-shifted projections", "kk_raw": "removal key before its norm", "cs_ready": "summed log decays",
    "kk_sum": "its clamped squared norm", "bonus_in": "r k r_k", "rwkv_in": "the recurrence's operands",
    "att_normed": "q and k, normed", "off_ready": "off-diagonal blocks", "solve_ready": "the inverses",
    "u_ready": "a chunk's solution", "y_ready": "the output on chip", "mix_ready": "RWKV and conv outputs",
}


class Seen:

    def __init__(self):
        self.n, self.i, self.per, self.at = {}, None, {}, {}

    def __call__(self, name, k=1):
        self.n[name] = self.n.get(name, 0) + k
        if self.i is not None:
            return self.i * self.per[name] + self.n[name]
        return self.n[name]

    def enter(self, i, per):
        self.i, self.per, self.at = i, per, dict(self.n)

    def leave(self, turns):
        for name, v in self.n.items():
            grew = v - self.at.get(name, 0)
            if grew:
                assert grew == self.per[name], (name, grew, self.per[name])
                self.n[name] = self.at.get(name, 0) + grew * turns
        self.i = None


def build(nc, a, out, dbg=None):
    F = mybir.dt.float32
    ALU = mybir.AluOpType
    ACT = mybir.ActivationFunctionType
    AX = mybir.AxisListType.X
    _, CW = _constants()
    n_const = sum(w for _, w in CW.values())

    ctx = ExitStack()
    with ctx:
        def sb(name, shape):
            return ctx.enter_context(nc.sbuf_tensor(name, shape, F))

        S = {name: ctx.enter_context(nc.semaphore(name)) for name in SEMAPHORES}

        const = sb("const", [P, n_const])
        slab = [sb(f"slab{i}", [P, SLAB]) for i in range(SLOTS)]
        par1 = sb("par1", [P, sum(n for _, n in ROWS_1)])
        par2 = sb("par2", [P, LAYERS * sum(n for _, n in ROWS_2)])
        taps = sb("taps", [P, TAPS * 4])
        b_ada = sb("b_ada", [P, LAYERS * 72])
        ada = sb("ada", [P, LAYERS * 72])
        brow = sb("brow", [1, 52])
        bbc = sb("bbc", [P, 52])
        router = sb("router", [P, KD, 36])
        lora_wa = sb("lora_wa", [P, LAYERS, T])
        lora_g = sb("lora_g", [P, LAYERS, T])
        c_act = sb("c_act", [P, KD])
        modg = sb("modg", [P, LAYERS * 6, KD])
        xT = sb("xT", [P, KD, T])
        hT = sb("hT", [P, KD, T])
        sq = sb("sq", [P, KD, T])
        rows = sq[:, :, :].rearrange("p a b -> p (a b)")[:, 0:5 * P].rearrange("p (a b) -> p a b", a=5)
        lnt = sb("lnt", [P, 512])
        rsB = sb("rsB", [P, 512])
        silu = sb("silu", [P, 2, T])
        gu = sb("gu", [P, 2, T])
        sel = sb("sel", [P, 2, T])
        combT = sb("combT", [P, T])
        tiny = sb("tiny", [P, 160])
        region_n = 25700
        region = sb("region", [P, region_n])
        bank = [ctx.enter_context(nc.psum_tensor(f"bank{i}", [P, 512], F)) for i in range(8)]

        def C(name, lo=0, hi=None):
            at, w = CW[name]
            return const[:, at + lo:at + (w if hi is None else hi)]

        def layout(start, **sizes):
            views, at = {}, start
            for name, shape in sizes.items():
                n = int(np.prod(shape))
                v = region[:, at:at + n]
                if len(shape) == 2:
                    v = v.rearrange("p (a b) -> p a b", a=shape[0])
                elif len(shape) == 3:
                    v = v.rearrange("p (a b c) -> p a b c", a=shape[0], b=shape[1])
                views[name] = v
                at += n
            assert at <= region_n, at
            return views

        B1 = layout(0, qi=(4, T), ki=(T,), wi=(NT, 8), ka=(T,), kdup=(2, T), va=(NT, P), qa=(4, T),
                    u=(4, 30 + T), ug=(4, T), y=(4, T), qm=(4, T), km=(4, T), vm=(NT, 512),
                    memh=(8, T), gate=(24, T), oa=(4, T), score=(NT, T), pick=(NT, T), amask=(NT, T),
                    sc=(2, 512), pr=(2, 512), pT=(2, 512), tmp=(512,), tmp2=(512,))
        B1["om"], B1["ob"], B1["merged"] = B1["qi"], B1["ug"], B1["memh"]
        B1["rl"] = B1["sc"].rearrange("p a (b c) -> p a b c", b=2)
        xin = B1["gate"][:, 0:8, :].rearrange("p a b -> p (a b)").rearrange("p (t d) -> p t d", t=NT)
        memin = B1["gate"][:, 8:16, :].rearrange("p a b -> p (a b)").rearrange("p (t d) -> p t d", t=NT)
        memT = B1["gate"][:, 16:24, :]
        M = layout(0, ada_in=(2, KD, ADA_COLS), ada_acc=(2, ADA_COLS))
        B2 = layout(0, q=(4, T), k=(T,), kdup=(2, T), v=(NT, P), o=(4, T), praw=(8, 1 + T), pm=(8, T),
                    sw=(2, T), cs=(2, T), csp=(2, T), W=(2, T), Winv=(2, T), Wprev=(2, T), aa=(2, T),
                    gB=(2, T), kk=(2, T), al=(2, T), be=(2, T), kap=(2, T), rho=(2, T), bon=(2, T),
                    ysh=(8, T), AT=(2, 512), BT=(2, 512), Tm=(2, 512), TT=(2, 512), off=(2, 512),
                    M1=(2, 512), R=(T,), state=(2, P), cb=(2, T), cc=(2, T), ch=(2, T), cu=(2, 2 + T),
                    cy=(2, T))
        for n, name in enumerate(("vt", "bt", "kt", "negU")):
            B2[name] = B2["ysh"][:, 2 * n:2 * n + 2, :]
        flat_praw = B2["praw"].rearrange("p a b -> p (a b)")
        B2["C1T"] = flat_praw[:, 0:1024].rearrange("p (a b) -> p a b", a=2)
        B2["C2T"] = flat_praw[:, 1024:2048].rearrange("p (a b) -> p a b", a=2)
        B2["sc"], B2["pr"], B2["pT"] = B2["AT"], B2["M1"], B2["off"]
        B2["th"], B2["yr"] = B2["R"], B2["cs"]

        def par_at(name, layer=None):
            spec, tile = (ROWS_1, par1) if layer is None else (ROWS_2, par2)
            at = 0 if layer is None else layer * sum(n for _, n in ROWS_2)
            for nm, n in spec:
                if nm == name:
                    return tile, at, n
                at += n
            raise KeyError(name)

        def col(name, j=0, layer=None):
            tile, at, _ = par_at(name, layer)
            return tile[:, at + j:at + j + 1]

        ROUTE = {}
        for nm, n in (("gpad", 16), ("epad", 48), ("list1", 8), ("list2", 8), ("lg", 36), ("g8", 8), ("e8", 8),
                      ("ngmax", 1), ("nv1", 1), ("gsum", 1), ("e21", 1), ("d", 1), ("w1", 1), ("w2", 1),
                      ("goh", 4), ("gneg", 4), ("ge", 4)):
            ROUTE[nm] = sum(k for _, k in ROUTE.values()), n
        rscratch = sb("rscratch", [P, NT, sum(k for _, k in ROUTE.values())])

        def route(name, t, n):
            at = ROUTE[name][0]
            return rscratch[:, t, at:at + n]

        def row_loads():
            at = 0
            for name, n in ROWS_1:
                yield from one_row(0, at, n, a[name][0])
                at += n
            at = 0
            for l in range(LAYERS):
                for name, n in ROWS_2:
                    src = a[name][l]
                    if len(src.shape) == 2:
                        src = src.rearrange("a b -> (a b)")
                    yield from one_row(1, at, n, src)
                    at += n
            yield rows[0:TAPS * 4, 2, :], a["conv_w"][0, :, 0, :].rearrange("k (c p) -> (k c) p", p=P)
            for l in range(LAYERS):
                yield rows[0:72, 3 + l, :], a["b_ada_2"][l].rearrange("(c p) -> c p", p=P)
                yield lora_wa[0:64, l, :], a["rwkv_w_w2_2"][l]
                yield lora_wa[64:128, l, :], a["rwkv_a_w2_2"][l]
                yield lora_g[:, l, :], a["rwkv_g_w2_2"][l]
            yield brow[0:1, 0:4], a["b_rg"]
            yield brow[0:1, 4:36], a["b_re"]
            yield brow[0:1, 36:52], a["att_sinks_2"].rearrange("(o l) h -> o (l h)", o=1)
            yield router[:, :, 0:4], a["w_rg"][0].rearrange("(k p) c -> p k c", p=P)
            yield router[:, :, 4:36], a["w_re"][0].rearrange("(k p) c -> p k c", p=P)

        def one_row(tile, at, n, src):
            if src.shape[0] == 64:
                for half in range(2):
                    yield rows[at:at + 1, tile, half * 64:half * 64 + 64], src.rearrange("(o p) -> o p", o=1)
            else:
                yield rows[at:at + n, tile, :], src.rearrange("(c p) -> c p", p=P)

        def b3(ap, n):
            return ap.unsqueeze(1).to_broadcast([ap.shape[0], n, ap.shape[1]])

        slab_end = []
        ring = []
        for_act, for_dve = [], []

        block = ctx.enter_context(nc.Block())

        GROUPS = [(t, h) for t in range(NT) for h in (0, 1, 4, 5)]
        MEM_GROUPS = [(t, h) for t in range(NT) for h in (0, 2)]

        @block.tensor
        def _(pe):
            w = Seen()
            n_slab = [0]
            made = {"up_done": 0, "down_done": 0}

            def mm(o, lhsT, rhs, start=False):
                return nc.tensor.matmul(o, lhsT, rhs, start=start, stop=True, skip_group_check=True)

            def product(consumer):
                n = len(ring)
                if n >= RING:
                    who, k = ring[n - RING]
                    pe.wait_ge(S["read_by_" + who], k)
                b = n % RING
                ring.append((consumer, sum(r == consumer for r, _ in ring) + 1))
                (for_act if consumer == "act" else for_dve).append(b)
                return bank[b]

            def quiet():
                for who in ("act", "dve"):
                    k = sum(r == who for r, _ in ring)
                    if k:
                        pe.wait_ge(S["read_by_" + who], k)

            def arrive(k=16):
                s = n_slab[0] % SLOTS
                n_slab[0] += 1
                pe.wait_ge(S[f"slab{s}_in"], w(f"slab{s}_in", k))
                return slab[s]

            def used(name):
                count = {"for_act": len(for_act), "for_dve": len(for_dve), **made}
                slab_end.append((name, count[name]))

            def transpose(o, in_, last=None):
                k = in_.shape[0]
                return nc.tensor.transpose(o, in_, C("eye")[0:k, 0:k])

            def project(rhs, nblocks, consumer, kc=KD, k=16, first=None, per_slab=None):
                per = per_slab or SLAB // (kc * P)
                for b in range(nblocks):
                    if b % per == 0:
                        s = arrive(k).rearrange("p (k c) -> p k c", k=kc)
                    ps = product(consumer)
                    for j in range(kc):
                        if first and b == 0:
                            pe.wait_ge(S[first], w(first))
                        m = mm(ps[:, 0:T], s[:, j, (b % per) * P:(b % per + 1) * P], rhs[:, j, :], j == 0)
                    m.then_inc(S["for_" + consumer], 1)
                    if b % per == per - 1 or b == nblocks - 1:
                        used("for_" + consumer)

            def norm_sum(kc=KD):
                ps = product("act")
                for j in range(kc):
                    if j % 4 == 0:
                        pe.wait_ge(S["sq"], w("sq"))
                    m = mm(ps[:, 0:T], C("ones"), sq[:, j, :], j == 0)
                m.then_inc(S["for_act"], 1)

            def pair_sum(src, mat="half", consumer="act"):
                ps = product(consumer)
                n = src.shape[-1] if len(src.shape) == 2 else 2 * T
                mm(ps[:, 0:n], C(mat), src, True).then_inc(S["for_" + consumer], 1)

            def attend(groups, q, kdup, v, pr, pT, mem=False):
                width = [P * (t + 1) for t in range(NT)] if not mem else [T, T]
                for g in range(len(groups) + 1):
                    if g < len(groups):
                        t, h = groups[g]
                        ps = product("dve")
                        for j in range(2):
                            o = ps[:, j * width[t]:(j + 1) * width[t]]
                            if mem:
                                m = mm(o, q[:, h + j, t * P:(t + 1) * P], kdup[:, h + j, :], j == 0)
                            else:
                                r = (h % 2) * 64
                                m = mm(o, q[r:r + 64, h // 2 + j, t * P:(t + 1) * P],
                                       kdup[r:r + 64, h // 4, 0:width[t]], j == 0)
                        m.then_inc(S["for_dve"], 1)
                    if g:
                        t, h = groups[g - 1]
                        nk = width[t] // P
                        pe.wait_ge(S["att_p"], w("att_p"))
                        ps = product("act")
                        for x in range(2 * nk):
                            m = transpose(ps[:, x * P:(x + 1) * P], pr[:, (g - 1) % 2, x * P:(x + 1) * P])
                        m.then_inc(S["for_act"], 1)
                        pe.wait_ge(S["att_pT"], w("att_pT"))
                        ps = product("act")
                        for j in range(2):
                            for kt in range(nk):
                                x = pT[:, (g - 1) % 2, (j * nk + kt) * P:(j * nk + kt + 1) * P]
                                if mem:
                                    m = mm(ps[:, j * P:(j + 1) * P], v[:, kt, (h + j) * P:(h + j + 1) * P], x,
                                           j == 0 and kt == 0)
                                else:
                                    r = (h % 2) * 64
                                    m = mm(ps[r:r + 64, j * P:(j + 1) * P],
                                           v[:, kt, (h // 4) * 64:(h // 4) * 64 + 64], x, j == 0 and kt == 0)
                        m.then_inc(S["for_act"], 1)

            def glu_unit(u, moe, first=None):
                if moe:
                    pe.wait_ge(S["sel"], w("sel"))
                    mm(bank[2][:, 0:T], C("ones")[0:N_EXP, :], sel[0:N_EXP, u, :], True).then_inc(S["comb_done"], 1)
                for j in range(2):
                    s = arrive(32).rearrange("p (k c) -> p k c", k=KD)
                    for ab in range(2):
                        for kc in range(KD):
                            m = mm(bank[j][:, ab * T:(ab + 1) * T], s[:, kc, ab * P:(ab + 1) * P],
                                   hT[:, kc, :], kc == 0)
                    m.then_inc(S["up_done"], 1)
                    made["up_done"] += 1
                    used("up_done")
                s = arrive().rearrange("p (j d) -> p j d", j=2)
                for j in range(2):
                    pe.wait_ge(S["gu_ready"], w("gu_ready"))
                    for d in range(KD):
                        m = mm(bank[4 + d // 2][:, (d % 2) * T:(d % 2 + 1) * T], s[:, j, d * P:(d + 1) * P],
                               gu[:, j, :])
                m.then_inc(S["down_done"], 1)
                made["down_done"] += 1
                used("down_done")

            def glu(turns, tail, moe):
                quiet()
                for i in range(KD):
                    pe.wait_ge(S["hn"], w("hn"))
                for b in range(4, 8):
                    mm(bank[b][:, :], zero[:, 0:P], zero[:, :], True)
                with pe.Fori(0, turns) as i:
                    n0, up0, dn0 = len(slab_end), made["up_done"], made["down_done"]
                    per = {f"slab{s}_in": 80 for s in range(SLOTS)}
                    at = n_slab[0] % SLOTS
                    per = {f"slab{(at + x) % SLOTS}_in": (32, 32, 16)[x % 3] for x in range(6)}
                    per |= {"gu_ready": 4, "sel": 2, "ada_done": 1}
                    w.enter(i, per)
                    for u in range(2):
                        glu_unit(u, moe)
                    if moe:
                        pe.wait_ge(S["ada_done"], w("ada_done"))
                        for b in range(9):
                            m = mm(bank[3][:, b:b + 1], ada_acc[:, b * P:(b + 1) * P], C("ones")[:, 0:1], b == 0)
                        m.then_inc(S["ada_sum"], 1)
                    w.leave(turns)
                n_slab[0] += 6 * (turns - 1)
                body = slab_end[n0:]
                for r in range(1, turns):
                    for name, k in body:
                        slab_end.append((name, k + r * (4 if name == "up_done" else 2)))
                made["up_done"], made["down_done"] = up0 + 4 * turns, dn0 + 2 * turns
                for u in range(tail):
                    glu_unit(u, moe)

            zero = lnt[:, :].bitcast(mybir.dt.bfloat16)[:, 0:512]
            ada_acc = M["ada_acc"].rearrange("p a c -> p (a c)")

            pe.wait_ge(S["const_in"], w("const_in", 16))
            for src, sem in ((xin, "x_in"), (memin, "mem_in")):
                pe.wait_ge(S[sem], w(sem, 16))
                for kc in range(0, KD, 2):
                    ps = product("act")
                    for x in range(4):
                        m = transpose(ps[:, x * P:(x + 1) * P],
                                      src[:, x % 2, (kc + x // 2) * P:(kc + x // 2 + 1) * P])
                    m.then_inc(S["for_act"], 1)
            pe.wait_ge(S["rows_in"], 16 * sum(1 for _ in row_loads()))
            for n, r in enumerate(ROW_COUNTS):
                ps = product("act")
                transpose(ps[:, 0:r], rows[0:r, n, :]).then_inc(S["for_act"], 1)
            ps = product("act")
            mm(ps[:, 0:52], C("ones")[0:1, :], brow[0:1, :], True).then_inc(S["for_act"], 1)

            norm_sum()
            project(hT, 4, "act", first="hn")
            s = arrive(48).rearrange("p (k c) -> p k c", k=KD)
            ps = product("act")
            for kc in range(KD):
                m = mm(ps[:, 0:T], s[:, kc, 0:P], hT[:, kc, :], kc == 0)
            m.then_inc(S["for_act"], 1)
            ps = product("act")
            for t in range(NT):
                for kc in range(KD):
                    m = mm(ps[:, t * 8:(t + 1) * 8], hT[:, kc, t * P:(t + 1) * P], s[:, kc, P:P + 8],
                           t == 0 and kc == 0)
            m.then_inc(S["for_act"], 1)
            used("for_act")

            def key_value():
                s = arrive().rearrange("p (k c) -> p k c", k=KD)
                ps = product("act")
                for kc in range(KD):
                    m = mm(ps[:, 0:T], s[:, kc, 0:P], hT[:, kc, :], kc == 0)
                m.then_inc(S["for_act"], 1)
                ps = product("act")
                for t in range(NT):
                    for kc in range(KD):
                        m = mm(ps[:, t * P:(t + 1) * P], hT[:, kc, t * P:(t + 1) * P], s[:, kc, P:2 * P],
                               t == 0 and kc == 0)
                m.then_inc(S["for_act"], 1)
                used("for_act")
            key_value()
            project(hT, 4, "act")
            pe.wait_ge(S["ki_sq"], w("ki_sq"))
            pair_sum(sq[:, 0, :])
            for x in range(2):
                pair_sum(B1["qi"][:, 2 * x:2 * x + 2, :], "rot", "dve")
            pe.wait_ge(S["ki_normed"], w("ki_normed"))
            pair_sum(B1["ki"], "rot", "dve")
            pe.wait_ge(S["qka_sq"], w("qka_sq"))
            pair_sum(sq[:, 1:3, :])
            pair_sum(sq[:, 3:5, :])
            pair_sum(sq[:, 5, :])
            pe.wait_ge(S["idx_roped"], w("idx_roped"))
            for t, h in GROUPS:
                r, wd = (h % 2) * 64, P * (t + 1)
                ps = product("act")
                for j in range(2):
                    m = mm(ps[:, j * wd:(j + 1) * wd], B1["qi"][r:r + 64, h // 2 + j, t * P:(t + 1) * P],
                           B1["ki"][r:r + 64, 0:wd], j == 0)
                m.then_inc(S["for_act"], 1)
            pe.wait_ge(S["qka_normed"], w("qka_normed"))
            for x in range(2):
                pair_sum(B1["qa"][:, 2 * x:2 * x + 2, :], "rot", "dve")
            pair_sum(B1["ka"], "rot", "dve")
            project(hT, 8, "act")
            pe.wait_ge(S["ka_roped"], w("ka_roped"))
            for x in range(2):
                pair_sum(B1["ka"], f"dup{x}")
            project(hT, 4, "act")
            norm_sum()
            for i in range(4):
                pe.wait_ge(S["memh"], w("memh"))
            for i in range(4):
                pe.wait_ge(S["memh"], w("memh"))
            project(B1["memh"], 4, "act")
            vslab = [arrive().rearrange("p (k c) -> p k c", k=KD) for _ in range(2)]
            for t in range(NT):
                ps = product("act")
                for x in range(2):
                    for kc in range(KD):
                        m = mm(ps[:, x * T:(x + 1) * T], B1["memh"][:, kc, t * P:(t + 1) * P],
                               vslab[x][:, kc, :], x == 0 and kc == 0)
                m.then_inc(S["for_act"], 1)
            used("for_act")
            used("for_act")
            pe.wait_ge(S["qkm_sq"], w("qkm_sq"))
            for x in range(4):
                pair_sum(sq[:, 2 * x:2 * x + 2, :], "ones")
            project(hT, 24, "act")
            pe.wait_ge(S["qa_roped"], w("qa_roped"))
            pe.wait_ge(S["dsa_mask"], w("dsa_mask"))
            attend(GROUPS, B1["qa"], B1["kdup"], B1["va"], B1["pr"], B1["pT"])
            pe.wait_ge(S["qkm_normed"], w("qkm_normed"))
            attend(MEM_GROUPS, B1["qm"], B1["km"], B1["vm"], B1["pr"], B1["pT"], mem=True)
            pe.wait_ge(S["conv_y"], w("conv_y"))
            ps = product("dve")
            for j in range(4):
                m = mm(ps[:, 0:T], C("ones"), B1["y"][:, j, :], j == 0)
            m.then_inc(S["for_dve"], 1)
            norm_sum(4)
            for src, sem in (("oa", "oa_ready"), ("om", "om_ready"), ("ob", "ob_ready")):
                pe.wait_ge(S[sem], w(sem))
                project(B1[src], 8, "dve", kc=4)
            pe.wait_ge(S["merged"], w("merged"))
            project(B1["merged"], 8, "dve")
            norm_sum()
            for i in range(KD):
                pe.wait_ge(S["hn"], w("hn"))
            ps = product("dve")
            for t in range(NT):
                for kc in range(KD):
                    m = mm(ps[:, t * 64:t * 64 + 36], hT[:, kc, t * P:(t + 1) * P], router[:, kc, :],
                           t == 0 and kc == 0)
            m.then_inc(S["for_dve"], 1)
            pe.wait_ge(S["comb_ready"], w("comb_ready"))
            ps = product("dve")
            for t in range(NT):
                m = transpose(ps[0:N_EXP, t * P:(t + 1) * P], tiny[:, 96 + t * N_EXP:96 + (t + 1) * N_EXP])
            m.then_inc(S["for_dve"], 1)
            w.n["hn"] -= KD
            pe.wait_ge(S["zero"], w("zero"))
            glu(N_EXP // 2, 0, True)

            for l in range(LAYERS):
                for part in range(2):
                    norm_sum()
                    if part == 0:
                        pe.wait_ge(S["zero"], w("zero"))
                        glu(5, 1, False)
                        continue
                    V = B2
                    project(hT, 8, "act", first="hn")
                    project(hT, 4, "act")
                    key_value()
                    pe.wait_ge(S["lora_in"], w("lora_in"))
                    ps = product("act")
                    for c in range(2):
                        m = mm(ps[:, c * T:(c + 1) * T], lora_wa[0:64, l, c * P:(c + 1) * P],
                               V["th"][0:64, :], c == 0)
                    m.then_inc(S["for_act"], 1)
                    ps = product("act")
                    for c in range(2):
                        m = mm(ps[:, c * T:(c + 1) * T], lora_wa[64:128, l, c * P:(c + 1) * P],
                               V["pm"][64:128, 6, :], c == 0)
                    m.then_inc(S["for_act"], 1)
                    ps = product("act")
                    for c in range(2):
                        m = mm(ps[:, c * T:(c + 1) * T], lora_g[:, l, c * P:(c + 1) * P],
                               V["pm"][:, 7, :], c == 0)
                    m.then_inc(S["for_act"], 1)
                    pe.wait_ge(S["kk_sq"], w("kk_sq"))
                    pair_sum(sq[:, 0:2, :], consumer="dve")
                    pe.wait_ge(S["att_sq"], w("att_sq"))
                    pair_sum(sq[:, 2:4, :])
                    pair_sum(sq[:, 4:6, :])
                    pair_sum(sq[:, 6, :])
                    project(hT, 6, "act")
                    pe.wait_ge(S["bonus_in"], w("bonus_in"))
                    pair_sum(V["ysh"][:, 0:2, :], consumer="dve")
                    pe.wait_ge(S["rwkv_in"], w("rwkv_in"))
                    for src in (V["pm"][:, 4:6, :], V["be"], V["kap"]):
                        ps = product("act")
                        for x in range(4):
                            t, c = x // 2, x % 2
                            m = transpose(ps[:, x * P:(x + 1) * P], src[:, c, t * P:(t + 1) * P])
                        m.then_inc(S["for_act"], 1)
                    for left, right in (("be", "al"), ("kap", "al"), ("be", "rho"), ("kap", "rho")):
                        for g in range(2):
                            r = g * 64
                            ps = product("dve")
                            for x in range(4):
                                t, c = x // 2, x % 2
                                m = mm(ps[:, x * P:(x + 1) * P], V[left][r:r + 64, c, t * P:(t + 1) * P],
                                       V[right][r:r + 64, c, t * P:(t + 1) * P], x == 0)
                            m.then_inc(S["for_dve"], 1)
                    for lev in range(6):
                        for g in range(2):
                            pe.wait_ge(S["off_ready"], w("off_ready"))
                            ps = product("act")
                            for x in range(4):
                                X = slice(x * P, (x + 1) * P)
                                m = mm(ps[:, X], V["off"][:, g, X], V["Tm"][:, g, X], x == 0)
                            m.then_inc(S["for_act"], 1)
                        for g in range(2):
                            pe.wait_ge(S["m1_ready"], w("m1_ready"))
                            if lev < 5:
                                ps = product("dve")
                                for x in range(4):
                                    X = slice(x * P, (x + 1) * P)
                                    m = mm(ps[:, X], V["TT"][:, g, X], V["M1"][:, g, X], x == 0)
                                m.then_inc(S["for_dve"], 1)
                            ps = product("dve")
                            for x in range(4):
                                X = slice(x * P, (x + 1) * P)
                                m = mm(ps[:, X], V["M1"][:, g, X], V["TT"][:, g, X], x == 0)
                            m.then_inc(S["for_dve"], 1)
                    for c4 in range(T // CHUNK):
                        t, r0 = c4 // 2, (c4 % 2) * CHUNK
                        if c4 == 0:
                            pe.wait_ge(S["solve_ready"], w("solve_ready"))
                        pe.wait_ge(S["state_ready"], w("state_ready"))
                        ps = product("act")
                        for h in range(4):
                            X = slice((2 * t + h // 2) * P, (2 * t + h // 2 + 1) * P)
                            mm(ps[:, h * 64:(h + 1) * 64], V["BT"][:, h % 2, X],
                               V["vt"][:, t, h * 64:(h + 1) * 64], h == 0)
                        for c in range(2):
                            m = mm(ps[:, c * P:(c + 1) * P], V["al"][:, c, t * P:(t + 1) * P],
                                   V["state"][:, c, :])
                        m.then_inc(S["for_act"], 1)
                        for c in range(2):
                            tok = slice(c4 * CHUNK, (c4 + 1) * CHUNK)
                            mm(bank[7][:, c * T + c4 * CHUNK:c * T + (c4 + 1) * CHUNK], V["state"][:, c, :],
                               V["rho"][:, c, tok], c4 == 0 and c == 0)
                        pe.wait_ge(S["r_ready"], w("r_ready"))
                        ps = product("dve")
                        for h in range(4):
                            X = slice((2 * t + h // 2) * P, (2 * t + h // 2 + 1) * P)
                            m = mm(ps[:, h * 64:(h + 1) * 64], V["TT"][:, h % 2, X],
                                   V["R"][:, h * 64:(h + 1) * 64], h == 0)
                        m.then_inc(S["for_dve"], 1)
                        pe.wait_ge(S["u_ready"], w("u_ready"))
                        if c4 < 3:
                            ps = product("dve")
                            for c in range(2):
                                mm(ps[:, c * P:(c + 1) * P], V["bt"][r0:r0 + CHUNK, t, c * P:(c + 1) * P],
                                   V["negU"][r0:r0 + CHUNK, t, c * P:(c + 1) * P], c == 0)
                                m = mm(ps[:, c * P:(c + 1) * P], V["kt"][r0:r0 + CHUNK, t, c * P:(c + 1) * P],
                                       V["vt"][r0:r0 + CHUNK, t, c * P:(c + 1) * P])
                            m.then_inc(S["for_dve"], 1)
                        if c4 % 2:
                            for h in range(4):
                                X = slice((2 * t + h // 2) * P, (2 * t + h // 2 + 1) * P)
                                o = bank[7][(h % 2) * 64:(h % 2) * 64 + 64,
                                            (h // 2) * T + t * P:(h // 2) * T + (t + 1) * P]
                                mm(o, V["vt"][:, t, h * 64:(h + 1) * 64], V["C2T"][:, h % 2, X])
                                m = mm(o, V["negU"][:, t, h * 64:(h + 1) * 64], V["C1T"][:, h % 2, X])
                            if c4 == 3:
                                m.then_inc(S["y_done"], 1)
                    pe.wait_ge(S["y_ready"], w("y_ready"))
                    pair_sum(V["W"], consumer="dve")
                    pe.wait_ge(S["yc_sq"], w("yc_sq"))
                    pair_sum(sq[:, 0:2, :])
                    pe.wait_ge(S["att_normed"], w("att_normed"))
                    for x in range(2):
                        pair_sum(V["k"], f"dup{x}")
                    pe.wait_ge(S["kdup_ready"], w("kdup_ready"))
                    attend(GROUPS, V["q"], V["kdup"], V["v"], V["pr"], V["pT"])
                    pe.wait_ge(S["mix_ready"], w("mix_ready"))
                    pe.wait_ge(S["swa_ready"], w("swa_ready"))
                    parts = [V["o"][:, j, :] for j in range(4)] + [V["yr"][:, j, :] for j in range(2)] \
                        + [V["cy"][:, j, :] for j in range(2)]
                    for b in range(KD):
                        if b % 2 == 0:
                            s = arrive().rearrange("p (k c) -> p k c", k=KD)
                        ps = product("dve")
                        for j in range(KD):
                            m = mm(ps[:, 0:T], s[:, j, (b % 2) * P:(b % 2 + 1) * P], parts[j], j == 0)
                        m.then_inc(S["for_dve"], 1)
                        if b % 2:
                            used("for_dve")
                norm_sum()
                pe.wait_ge(S["zero"], w("zero"))
                glu(5, 1, False)
            for i in range(KD):
                pe.wait_ge(S["x_ready_pe"], w("x_ready_pe"))
            for t in range(NT):
                for x in range(2):
                    ps = product("act")
                    for j in range(4):
                        kc = 4 * x + j
                        m = transpose(ps[:, j * P:(j + 1) * P], xT[:, kc, t * P:(t + 1) * P])
                    m.then_inc(S["for_act"], 1)

        @block.scalar
        def _(act):
            w = Seen()
            banks = iter(for_act)
            table = [None]
            started = set()

            def tables(name):
                if table[0] != name:
                    nc.scalar.preload_act_table_set(name)
                    table[0] = name
            LNEXP, SIG, SILU = "natural_log_exp_and_others", "sigmoid_and_others", "silu_and_others"

            def take():
                act.wait_ge(S["for_act"], w("for_act"))
                return bank[next(banks)]

            def read(ins):
                ins.then_inc(S["read_by_act"], 1)
                w("read_by_act")

            def link(ins):
                ins.then_inc(S["act_step"], 1)
                act.wait_ge(S["act_step"], w("act_step"))

            def evac(dst, src_cols=None, func=ACT.Copy, shape=None, **kw):
                ps = take()
                src = ps[:, 0:src_cols or T]
                if shape:
                    src = src.rearrange("p (a b) -> p a b", a=shape)
                read(nc.scalar.activation(dst, src, func, **kw))

            def rsqrt_of(ps_ap, dst, scale, bias, sem=None):
                n = ps_ap.shape[-1]
                if "rs" in w.n:
                    act.wait_ge(S["rs"], w.n["rs"])
                w("rs")
                ins = nc.scalar.activation(lnt[:, 0:n], ps_ap, ACT.Ln, scale=scale, bias=bias)
                read(ins)
                act.wait_ge(S["read_by_act"], w.n["read_by_act"])
                if "rs" in started:
                    act.wait_ge(S["rs_used"], w("rs_used"))
                started.add("rs")
                nc.scalar.activation(dst, lnt[:, 0:n], ACT.Exp, scale=-0.5).then_inc(S[sem], 1)

            def squares(src, dst=None):
                n = src.shape[1]
                for x in range(0, n, 4):
                    nc.scalar.activation(sq[:, x:x + 4, :], src[:, x:x + 4, :], ACT.Square)\
                        .then_inc(S["sq"], 1)

            def norm(src, own=False, n=KD, bias=None, scale=1.0 / D):
                if not own:
                    for i in range(KD):
                        act.wait_ge(S["x_ready"], w("x_ready"))
                squares(src)
                tables(LNEXP)
                rsqrt_of(take()[:, 0:T], rsB[:, 0:T], scale, C("small", 0, 1), "rs")

            def attend(groups, sc, pr, pT, o, sem, mem=False, sink=None):
                width = [P * (t + 1) for t in range(NT)] if not mem else [T, T]
                nm, rsum, es = tiny[:, 0:4], tiny[:, 4:8], tiny[:, 8:12]
                for g in range(len(groups) + 1):
                    if g < len(groups):
                        t, h = groups[g]
                        act.wait_ge(S["att_max"], w("att_max"))
                        for j in range(2):
                            if sink is not None:
                                hh = h + 2 * j
                                nc.scalar.activation(es[:, (g % 2) * 2 + j:(g % 2) * 2 + j + 1],
                                                     bbc[:, 36 + 8 * sink + hh:37 + 8 * sink + hh], ACT.Exp,
                                                     bias=nm[:, (g % 2) * 2 + j:(g % 2) * 2 + j + 1])
                            m = nc.scalar.activation(pr[:, g % 2, j * width[t]:(j + 1) * width[t]],
                                                     sc[:, g % 2, j * width[t]:(j + 1) * width[t]], ACT.Exp,
                                                     bias=nm[:, (g % 2) * 2 + j:(g % 2) * 2 + j + 1],
                                                     accum_out=rsum[:, (g % 2) * 2 + j:(g % 2) * 2 + j + 1])
                        m.then_inc(S["att_exp"], 1)
                    if g:
                        t, h = groups[g - 1]
                        nk = width[t] // P
                        n = 2 * nk * P
                        ps = take()
                        read(nc.scalar.activation(pT[:, (g - 1) % 2, 0:n], ps[:, 0:n], ACT.Copy))
                        act.wait_ge(S["read_by_act"], w.n["read_by_act"])
                        act.sem_inc(S["att_pT"], 1)
                        ps = take()
                        if mem:
                            dst = o[:, h:h + 2, t * P:(t + 1) * P]
                            src = ps[:, 0:2 * P]
                        else:
                            r = (h % 2) * 64
                            dst = o[r:r + 64, h // 2:h // 2 + 2, t * P:(t + 1) * P]
                            src = ps[r:r + 64, 0:2 * P]
                        read(nc.scalar.activation(dst, src.rearrange("p (a b) -> p a b", a=2), ACT.Copy))
                act.wait_ge(S["read_by_act"], w.n["read_by_act"])
                act.sem_inc(S[sem], 1)

            def glu(turns, tail, moe):
                tables(SILU)

                def unit(u):
                    for j in range(2):
                        act.wait_ge(S["up_done"], w("up_done"))
                        nc.scalar.activation(silu[:, j, :], bank[j][:, 0:T], ACT.Silu)\
                            .then_inc(S["silu_ready"], 1)
                with act.Fori(0, turns) as i:
                    w.enter(i, {"up_done": 4})
                    for u in range(2):
                        unit(u)
                    w.leave(turns)
                for u in range(tail):
                    unit(u)

            for n, (dst, src) in enumerate(row_loads()):
                act.dma_start(dst, src).then_inc(S["rows_in"], 16)
            act.wait_ge(S["const_in"], w("const_in", 16))

            for kc in range(0, KD, 2):
                evac(xT[:, kc:kc + 2, :].rearrange("p a b -> p (a b)"), 512)
            for kc in range(0, KD, 2):
                evac(memT[:, kc:kc + 2, :].rearrange("p a b -> p (a b)"), 512)
            for dst, n in ((par1, ROW_COUNTS[0]), (par2, ROW_COUNTS[1]), (taps, ROW_COUNTS[2]),
                           (b_ada[:, 0:72], 72), (b_ada[:, 72:144], 72), (bbc, 52)):
                ps = take()
                read(nc.scalar.activation(dst[:, 0:n], ps[:, 0:n], ACT.Copy))
            act.wait_ge(S["read_by_act"], w.n["read_by_act"])
            act.sem_inc(S["params"], 1)
            tables(SILU)
            _, ca, _ = par_at("c_2")
            link(nc.scalar.activation(c_act[:, :], par1[:, ca:ca + KD], ACT.Silu))
            act.sem_inc(S["c_act"], 1)
            norm(xT, own=True)
            for c in range(4):
                evac(B1["qi"][:, c, :])
            evac(B1["ki"])
            ps = take()
            read(nc.scalar.activation(B1["wi"], ps[:, 0:16].rearrange("p (a b) -> p a b", a=2), ACT.Copy,
                                      scale=8 ** -0.5))
            act.wait_ge(S["read_by_act"], w.n["read_by_act"])
            nc.scalar.activation(sq[:, 0, :], B1["ki"], ACT.Square).then_inc(S["ki_sq"], 1)
            evac(B1["ka"])
            evac(B1["va"], shape=2)
            for c in range(4):
                evac(B1["qa"][:, c, :])
            act.wait_ge(S["read_by_act"], w.n["read_by_act"])
            nc.scalar.activation(sq[:, 1:5, :], B1["qa"], ACT.Square)
            nc.scalar.activation(sq[:, 5, :], B1["ka"], ACT.Square).then_inc(S["qka_sq"], 1)
            rsqrt_of(take()[:, 0:T], rsB[:, 0:T], 1.0 / 64, C("small", 0, 1), "rs")
            for x in range(3):
                n = 512 if x < 2 else T
                rsqrt_of(take()[:, 0:n], rsB[:, 0:n], 1.0 / 64, C("small", 0, 1), "rs")
            for g, (t, h) in enumerate(GROUPS):
                wd = P * (t + 1)
                ps = take()
                if g >= 2:
                    act.wait_ge(S["rl_used"], w("rl_used"))
                read(nc.scalar.activation(B1["rl"][:, g % 2, :, 0:wd],
                                          ps[:, 0:2 * wd].rearrange("p (a b) -> p a b", a=2), ACT.Relu,
                                          scale=64 ** -0.5))
                act.wait_ge(S["read_by_act"], w.n["read_by_act"])
                act.sem_inc(S["rl_ready"], 1)
            for c in range(4):
                evac(B1["u"][:, c, 30:30 + T])
            tables(SIG)
            for c in range(4):
                evac(B1["ug"][:, c, :], func=ACT.Sigmoid)
            act.wait_ge(S["read_by_act"], w.n["read_by_act"])
            act.sem_inc(S["glu_in"], 1)
            for x in range(2):
                evac(B1["kdup"][:, x, :])
            for c in range(4):
                evac(B1["qm"][:, c, :])
            squares(memT)
            tables(LNEXP)
            rsqrt_of(take()[:, 0:T], rsB[:, 0:T], 1.0 / D, C("small", 0, 1), "rs")
            for c in range(4):
                evac(B1["km"][:, c, :])
            act.wait_ge(S["read_by_act"], w.n["read_by_act"])
            nc.scalar.activation(sq[:, 0:4, :], B1["qm"], ACT.Square)
            nc.scalar.activation(sq[:, 4:8, :], B1["km"], ACT.Square).then_inc(S["qkm_sq"], 1)
            for t in range(NT):
                evac(B1["vm"][:, t, :], 512)
            for x in range(4):
                rsqrt_of(take()[:, 0:512], rsB[:, 0:512], 1.0 / P, C("small", 0, 1), "rs")
            tables(SIG)
            act.wait_ge(S["memh_all"], w("memh_all"))
            for c in range(24):
                evac(B1["gate"][:, c, :], func=ACT.Sigmoid, bias=col("b_gate", c))
            tables(LNEXP)
            attend(GROUPS, B1["sc"], B1["pr"], B1["pT"], B1["oa"], "oa_ready")
            attend(MEM_GROUPS, B1["sc"], B1["pr"], B1["pT"], B1["om"], "om_ready", mem=True)
            act.wait_ge(S["yc_ready"], w("yc_ready"))
            squares(B1["y"])
            rsqrt_of(take()[:, 0:T], rsB[:, 0:T], 1.0 / 512, C("small", 0, 1), "rs")
            tables(SILU)
            act.wait_ge(S["yn_ready"], w("yn_ready"))
            for c in range(4):
                m = nc.scalar.activation(B1["ob"][:, c, :], B1["y"][:, c, :], ACT.Silu, bias=col("ln_b", c))
            m.then_inc(S["ob_ready"], 1)
            norm(xT)
            act.wait_ge(S["router_max"], w("router_max"))
            for t in range(NT):
                m = nc.scalar.activation(route("ge", t, 4), route("lg", t, 4), ACT.Exp, bias=route("ngmax", t, 1),
                                         accum_out=route("gsum", t, 1))
            m.then_inc(S["router_exp"], 1)
            act.wait_ge(S["router_top2"], w("router_top2"))
            for t in range(NT):
                m = nc.scalar.activation(route("e21", t, 1), route("e8", t, 8)[:, 1:2], ACT.Exp,
                                         bias=route("nv1", t, 1))
            m.then_inc(S["router_exp"], 1)
            glu(N_EXP // 2, 0, True)

            for l in range(LAYERS):
                V = B2
                norm(xT)
                glu(5, 1, False)
                norm(xT)
                for b in range(8):
                    evac(V["praw"][:, b, 1:1 + T])
                act.wait_ge(S["read_by_act"], w.n["read_by_act"])
                act.sem_inc(S["praw_ready"], 1)
                for c in range(4):
                    evac(V["q"][:, c, :])
                evac(V["k"])
                evac(V["v"], shape=2)
                tables(SIG)
                act.wait_ge(S["pm_ready"], w("pm_ready"))
                nc.scalar.activation(V["th"][0:64, :], V["pm"][0:64, 6, :], ACT.Tanh)
                nc.scalar.activation(V["pm"][:, 7, :], V["pm"][:, 7, :], ACT.Sigmoid).then_inc(S["lora_in"], 1)
                ps = take()
                nc.scalar.activation(V["sw"][:, 0, :], ps[:, 0:T], ACT.Sigmoid, bias=col("rwkv_w0_2", 0, l))
                read(nc.scalar.activation(V["sw"][:, 1, :], ps[:, T:2 * T], ACT.Sigmoid,
                                          bias=col("rwkv_w0_2", 1, l)))
                ps = take()
                nc.scalar.activation(V["aa"][:, 0, :], ps[:, 0:T], ACT.Sigmoid, bias=col("rwkv_a0_2", 0, l))
                read(nc.scalar.activation(V["aa"][:, 1, :], ps[:, T:2 * T], ACT.Sigmoid,
                                          bias=col("rwkv_a0_2", 1, l)))
                act.wait_ge(S["read_by_act"], w.n["read_by_act"])
                act.sem_inc(S["sw_ready"], 1)
                evac(V["gB"], 512, shape=2)
                act.wait_ge(S["kk_raw"], w("kk_raw"))
                nc.scalar.activation(sq[:, 0:2, :], V["kk"], ACT.Square).then_inc(S["kk_sq"], 1)
                nc.scalar.activation(sq[:, 2:6, :], V["q"], ACT.Square)
                nc.scalar.activation(sq[:, 6, :], V["k"], ACT.Square).then_inc(S["att_sq"], 1)
                tables(LNEXP)
                act.wait_ge(S["kk_sum"], w("kk_sum"))
                act.wait_ge(S["rs"], w.n["rs"])
                w("rs")
                link(nc.scalar.activation(lnt[:, :], rsB[:, :], ACT.Ln))
                act.wait_ge(S["rs_used"], w("rs_used"))
                nc.scalar.activation(rsB[:, :], lnt[:, :], ACT.Exp, scale=-0.5, bias=C("small", 2, 3))\
                    .then_inc(S["rs"], 1)
                act.wait_ge(S["cs_ready"], w("cs_ready"))
                nc.scalar.activation(V["W"], V["cs"], ACT.Exp, scale=-DECAY_C)
                nc.scalar.activation(V["Winv"], V["cs"], ACT.Exp, scale=DECAY_C)
                nc.scalar.activation(V["Wprev"], V["csp"], ACT.Exp, scale=-DECAY_C).then_inc(S["w_ready"], 1)
                for x in range(3):
                    n = 512 if x < 2 else T
                    rsqrt_of(take()[:, 0:n], rsB[:, 0:n], 1.0 / 64, C("small", 0, 1), "rs")
                for dst in ("cb", "cc", "ch"):
                    for c in range(2):
                        evac(V[dst][:, c, :])
                act.wait_ge(S["read_by_act"], w.n["read_by_act"])
                act.sem_inc(S["sconv_in"], 1)
                for dst in ("vt", "bt", "kt"):
                    evac(V[dst], 512, shape=2)
                for lev in range(6):
                    for g in range(2):
                        evac(V["M1"][:, g, :], 512)
                        act.wait_ge(S["read_by_act"], w.n["read_by_act"])
                        act.sem_inc(S["m1_ready"], 1)
                for c4 in range(4):
                    evac(V["R"], T)
                    act.wait_ge(S["read_by_act"], w.n["read_by_act"])
                    act.sem_inc(S["r_ready"], 1)
                act.wait_ge(S["yc_ready"], w("yc_ready"))
                nc.scalar.activation(sq[:, 0:2, :], V["W"], ACT.Square).then_inc(S["yc_sq"], 1)
                rsqrt_of(take()[:, 0:512], rsB[:, 0:512], 1.0 / 64, C("small", 1, 2), "rs")
                for x in range(2):
                    evac(V["kdup"][:, x, :])
                act.wait_ge(S["read_by_act"], w.n["read_by_act"])
                act.sem_inc(S["kdup_ready"], 1)
                attend(GROUPS, V["sc"], V["pr"], V["pT"], V["o"], "swa_ready", sink=l)
                norm(xT)
                glu(5, 1, False)
            for t in range(NT):
                for x in range(2):
                    evac(hT[:, 4 * t + 2 * x:4 * t + 2 * x + 2, :].rearrange("p a b -> p (a b)"), 512)
            act.wait_ge(S["read_by_act"], w.n["read_by_act"])
            act.dma_start(out[0].rearrange("(t p) d -> p t d", p=P),
                          hT[:, :, :].rearrange("p a b -> p (a b)").rearrange("p (t d) -> p t d", t=NT))\
                .then_inc(S["out_written"], 16)
            act.wait_ge(S["out_written"], 16)

        @block.vector
        def _(dve):
            w = Seen()
            banks = iter(for_dve)
            V_ = nc.vector

            def take():
                dve.wait_ge(S["for_dve"], w("for_dve"))
                return bank[next(banks)]

            def read(ins):
                ins.then_inc(S["read_by_dve"], 1)
                dve.wait_ge(S["read_by_dve"], w("read_by_dve"))

            def step(ins):
                ins.then_inc(S["dve_step"], 1)
                w("dve_step")

            def later(k=0):
                dve.wait_ge(S["dve_step"], w.n["dve_step"] - k)

            def link(ins):
                step(ins)
                later()

            def norm(src, gain, dst, sem="hn", bias=None, last_free=None, n=KD, own=False):
                dve.wait_ge(S["rs"], w("rs"))
                for j in range(n):
                    ins = V_.scalar_tensor_tensor(dst[:, j, :], src[:, j, :], gain(j), rsB[:, 0:T],
                                                  ALU.mult, ALU.mult)
                    if bias is None:
                        ins.then_inc(S[sem], 1)
                    else:
                        step(ins)
                if bias is None:
                    dve.wait_ge(S[sem], w(sem, n))
                    dve.sem_inc(S["rs_used"], 1)
                else:
                    for j in range(n):
                        later(n - 1 - j)
                        V_.tensor_scalar(dst[:, j, :], dst[:, j, :], bias(j), None, ALU.add)\
                            .then_inc(S[sem], 1)
                    dve.wait_ge(S[sem], w(sem, n))
                    dve.sem_inc(S["rs_used"], 1)

            def scale_rs(dst, gain_col, nb):
                dve.wait_ge(S["rs"], w("rs"))
                link(V_.scalar_tensor_tensor(dst, dst, gain_col, rsB[:, 0:nb * T].rearrange("p (a b) -> p a b", a=nb)
                                             if nb > 1 else rsB[:, 0:T], ALU.mult, ALU.mult))
                dve.sem_inc(S["rs_used"], 1)

            def rope(x, nb, tmp, tmp2):
                ps = take()
                cos, sin = C("cos"), C("sin")
                tv, t2 = tmp[:, 0:nb * T], tmp2[:, 0:nb * T]
                src = ps[:, 0:nb * T]
                if nb > 1:
                    cos, sin = b3(cos, nb), b3(sin, nb)
                    tv, t2, src = (v.rearrange("p (a b) -> p a b", a=nb) for v in (tv, t2, src))
                read(V_.tensor_tensor(tv, src, sin, ALU.mult))
                link(V_.tensor_tensor(t2, x, cos, ALU.mult))
                link(V_.tensor_tensor(x, tv, t2, ALU.add))

            def attend(groups, sc, pr, scale, mask, mem=False, sink=None):
                width = [P * (t + 1) for t in range(NT)] if not mem else [T, T]
                nm, rsum, es, rr = tiny[:, 0:4], tiny[:, 4:8], tiny[:, 8:12], tiny[:, 12:16]
                for g in range(len(groups) + 1):
                    if g < len(groups):
                        t, h = groups[g]
                        wd, b = width[t], g % 2
                        ps = take()
                        src = ps[:, 0:2 * wd].rearrange("p (a b) -> p a b", a=2)
                        dst = sc[:, b, 0:2 * wd].rearrange("p (a b) -> p a b", a=2)
                        if mask is None:
                            read(V_.tensor_scalar(dst, src, scale, None, ALU.mult))
                        else:
                            read(V_.scalar_tensor_tensor(dst, src, scale, b3(mask(t), 2), ALU.mult, ALU.add))
                        link(V_.tensor_reduce(nm[:, 2 * b:2 * b + 2], dst, AX, ALU.max, negate=True))
                        if sink is not None:
                            for j in range(2):
                                sk = bbc[:, 36 + 8 * sink + h + 2 * j:37 + 8 * sink + h + 2 * j]
                                link(V_.tensor_scalar(rr[:, 2 * b + j:2 * b + j + 1], sk, -1.0, None, ALU.mult))
                                link(V_.tensor_tensor(nm[:, 2 * b + j:2 * b + j + 1], nm[:, 2 * b + j:2 * b + j + 1],
                                                      rr[:, 2 * b + j:2 * b + j + 1], ALU.min))
                        dve.sem_inc(S["att_max"], 1)
                    if g:
                        t, h = groups[g - 1]
                        wd, b = width[t], (g - 1) % 2
                        dve.wait_ge(S["att_exp"], w("att_exp"))
                        if sink is not None:
                            link(V_.tensor_tensor(rsum[:, 2 * b:2 * b + 2], rsum[:, 2 * b:2 * b + 2],
                                                  es[:, 2 * b:2 * b + 2], ALU.add))
                        link(V_.reciprocal(rr[:, 2 * b:2 * b + 2], rsum[:, 2 * b:2 * b + 2]))
                        for j in range(2):
                            p = pr[:, b, j * wd:(j + 1) * wd]
                            step(V_.tensor_scalar(p, p, rr[:, 2 * b + j:2 * b + j + 1], None, ALU.mult))
                        later()
                        dve.sem_inc(S["att_p"], 1)

            def glu(turns, tail, moe, gate):
                def ada_ops(k0, k1):
                    for k in range(k0, k1):
                        s, kc = k % 2, k // 2
                        if kc == 0:
                            dve.wait_ge(S[f"ada{s}_in"], w(f"ada{s}_in", 16))
                            V_.tensor_scalar(M["ada_acc"][:, s, :], M["ada_in"][:, s, 0, :], c_act[:, 0:1], None,
                                             ALU.mult).then_inc(S["ada_step"], 1)
                        else:
                            dve.wait_ge(S["ada_step"], w("ada_step"))
                            ins = V_.scalar_tensor_tensor(M["ada_acc"][:, s, :], M["ada_in"][:, s, kc, :],
                                                          c_act[:, kc:kc + 1], M["ada_acc"][:, s, :],
                                                          ALU.mult, ALU.add)
                            ins.then_inc(S["ada_step"], 1)
                    if k1 == 16:
                        dve.wait_ge(S["ada_step"], w("ada_step", 2))
                        dve.sem_inc(S["ada_done"], 1)

                if moe:
                    def make_sel(i, u):
                        e = i * 2 + u
                        ins = V_.tensor_scalar(sel[0:N_EXP, u, :], combT[0:N_EXP, :], eye_col(e), None, ALU.mult)
                        ins.then_inc(S["sel"], 1)
                at_eye = CW["eye"][0]

                def eye_col(e):
                    return const[0:N_EXP, bass.ds(at_eye + e, 1)]

                with dve.Fori(0, turns) as i:
                    w.enter(i, {"silu_ready": 4, "gut": 4, "comb_done": 2, "ada0_in": 16, "ada1_in": 16,
                                "ada_step": 16, "ada_sum": 1})
                    for u in range(2):
                        if moe:
                            make_sel(i, u)
                        for j in range(2):
                            dve.wait_ge(S["silu_ready"], w("silu_ready"))
                            if moe:
                                if j == 0:
                                    dve.wait_ge(S["comb_done"], w("comb_done"))
                                V_.tensor_tensor(silu[:, j, :], silu[:, j, :], bank[2][:, 0:T], ALU.mult)\
                                    .then_inc(S["gut"], 1)
                                dve.wait_ge(S["gut"], w("gut"))
                            V_.tensor_tensor(gu[:, j, :], silu[:, j, :], bank[j][:, T:2 * T], ALU.mult)\
                                .then_inc(S["gu_ready"], 1)
                            f = 2 * u + j
                            if moe and f < 3:
                                ada_ops((0, 6, 12)[f], (6, 12, 16)[f])
                    if moe:
                        dve.wait_ge(S["ada_sum"], w("ada_sum"))
                        V_.tensor_tensor(ada[:, bass.ds(i * 9, 9)], bank[3][:, 0:9], b_ada[:, bass.ds(i * 9, 9)],
                                         ALU.add).then_inc(S["ada_ready"], 1)
                    w.leave(turns)
                for u in range(tail):
                    for j in range(2):
                        dve.wait_ge(S["silu_ready"], w("silu_ready"))
                        V_.tensor_tensor(gu[:, j, :], silu[:, j, :], bank[j][:, T:2 * T], ALU.mult)\
                            .then_inc(S["gu_ready"], 1)
                dve.wait_ge(S["down_done"], w("down_done", 2 * turns + tail))
                if moe:
                    dve.wait_ge(S["ada_ready"], turns)
                for d in range(KD):
                    ps = bank[4 + d // 2][:, (d % 2) * T:(d % 2 + 1) * T]
                    if gate is None:
                        ins = V_.tensor_tensor(xT[:, d, :], xT[:, d, :], ps, ALU.add)
                    else:
                        ins = V_.scalar_tensor_tensor(xT[:, d, :], ps, gate(d), xT[:, d, :], ALU.mult, ALU.add)
                    ins.then_inc(S["x_ready"], 1)
                dve.wait_ge(S["x_ready"], w("x_ready", KD))

            def zero_operand():
                link(V_.memset(lnt[:, :], 0.0))
                dve.sem_inc(S["zero"], 1)

            dve.wait_ge(S["params"], w("params"))
            dve.wait_ge(S["const_in"], w("const_in", 16))
            link(V_.memset(B1["u"][:, :, 0:30], 0.0))
            norm(xT, lambda j: col("g_mix", j), hT)
            scale_rs(B1["ki"], col("g_idx_k"), 1)
            dve.sem_inc(S["ki_normed"], 1)
            for x in range(2):
                rope(B1["qi"][:, 2 * x:2 * x + 2, :], 2, B1["tmp"], B1["tmp2"])
            rope(B1["ki"], 1, B1["tmp"], B1["tmp2"])
            dve.sem_inc(S["idx_roped"], 1)
            for x in range(2):
                scale_rs(B1["qa"][:, 2 * x:2 * x + 2, :], col("g_qa"), 2)
            scale_rs(B1["ka"], col("g_ka"), 1)
            dve.sem_inc(S["qka_normed"], 1)
            for g, (t, h) in enumerate(GROUPS):
                wd = P * (t + 1)
                dve.wait_ge(S["rl_ready"], w("rl_ready"))
                for j in range(2):
                    wcol = B1["wi"][:, t, h + 2 * j:h + 2 * j + 1]
                    src, dst = B1["rl"][:, g % 2, j, 0:wd], B1["score"][:, t, 0:wd]
                    if h == 0 and j == 0:
                        link(V_.tensor_scalar(dst, src, wcol, None, ALU.mult))
                    else:
                        link(V_.scalar_tensor_tensor(dst, src, wcol, dst, ALU.mult, ALU.add))
                dve.sem_inc(S["rl_used"], 1)
            for x in range(2):
                rope(B1["qa"][:, 2 * x:2 * x + 2, :], 2, B1["tmp"], B1["tmp2"])
            dve.sem_inc(S["qa_roped"], 1)
            rope(B1["ka"], 1, B1["tmp"], B1["tmp2"])
            dve.sem_inc(S["ka_roped"], 1)
            for t in range(NT):
                wd = P * (t + 1)
                pick = B1["pick"][:, t, 0:wd]
                link(V_.tensor_tensor(pick, B1["score"][:, t, 0:wd], C(f"causal{t}"), ALU.add))
                for r in range(TOPK // 8):
                    link(V_.max(tiny[:, 16:24], pick))
                    link(V_.match_replace(pick, tiny[:, 16:24], pick, PAD))
                link(V_.tensor_scalar(pick, pick, PAD, 1.0, ALU.is_equal, ALU.subtract))
                link(V_.scalar_tensor_tensor(B1["amask"][:, t, 0:wd], pick, -NEG, C(f"causal{t}"),
                                             ALU.mult, ALU.add))
            dve.sem_inc(S["dsa_mask"], 1)
            dve.wait_ge(S["glu_in"], w("glu_in"))
            link(V_.tensor_tensor(B1["u"][:, :, 30:30 + T], B1["u"][:, :, 30:30 + T], B1["ug"], ALU.mult))
            norm(memT, lambda j: col("g_mem", j), B1["memh"], "memh")
            dve.sem_inc(S["memh_all"], 1)
            for x in range(4):
                nm = "qm" if x < 2 else "km"
                scale_rs(B1[nm][:, 2 * (x % 2):2 * (x % 2) + 2, :], col("g_qm" if x < 2 else "g_km"), 2)
            dve.sem_inc(S["qkm_normed"], 1)
            for k in range(TAPS):
                for c in range(4):
                    src, tap = B1["u"][:, c, k:k + T], taps[:, k * 4 + c:k * 4 + c + 1]
                    if k == 0:
                        step(V_.tensor_scalar(B1["y"][:, c, :], src, tap, col("conv_b", c), ALU.mult, ALU.add))
                    else:
                        later(3)
                        step(V_.scalar_tensor_tensor(B1["y"][:, c, :], src, tap, B1["y"][:, c, :],
                                                     ALU.mult, ALU.add))
            later()
            dve.sem_inc(S["conv_y"], 1)
            attend(GROUPS, B1["sc"], B1["pr"], 64 ** -0.5, lambda t: B1["amask"][:, t, 0:P * (t + 1)])
            attend(MEM_GROUPS, B1["sc"], B1["pr"], P ** -0.5, None, mem=True)
            ps = take()
            for c in range(4):
                ins = V_.scalar_tensor_tensor(B1["y"][:, c, :], ps[:, 0:T], -1.0 / 512, B1["y"][:, c, :],
                                              ALU.mult, ALU.add)
                if c < 3:
                    step(ins)
            later()
            read(ins)
            dve.sem_inc(S["yc_ready"], 1)
            dve.wait_ge(S["rs"], w("rs"))
            for c in range(4):
                step(V_.scalar_tensor_tensor(B1["y"][:, c, :], B1["y"][:, c, :], col("ln_g", c), rsB[:, 0:T],
                                             ALU.mult, ALU.mult))
            later()
            dve.sem_inc(S["rs_used"], 1)
            dve.sem_inc(S["yn_ready"], 1)
            for n, br in enumerate((0, 2, 1)):
                for d in range(KD):
                    ps = take()
                    g = B1["gate"][:, br * KD + d, :]
                    if n == 0:
                        read(V_.tensor_tensor(B1["merged"][:, d, :], g, ps[:, 0:T], ALU.mult))
                    else:
                        read(V_.tensor_tensor(B1["tmp"][:, 0:T], g, ps[:, 0:T], ALU.mult))
                        link(V_.tensor_tensor(B1["merged"][:, d, :], B1["merged"][:, d, :], B1["tmp"][:, 0:T],
                                              ALU.add))
            dve.sem_inc(S["merged"], 1)

            def residual(gate):
                for d in range(KD):
                    ps = take()
                    if gate is None:
                        read(V_.tensor_tensor(xT[:, d, :], xT[:, d, :], ps[:, 0:T], ALU.add))
                    else:
                        read(V_.scalar_tensor_tensor(xT[:, d, :], ps[:, 0:T], gate(d), xT[:, d, :],
                                                     ALU.mult, ALU.add))
                    dve.sem_inc(S["x_ready"], 1)
                w("x_ready", KD)
            residual(None)
            norm(xT, lambda j: col("g_ffn", j), hT)

            ps = take()
            for t in range(NT):
                link(V_.memset(route("gpad", t, 16), PAD))
                link(V_.memset(route("epad", t, 48), PAD))
                link(V_.memset(route("list1", t, 8), PAD))
                link(V_.memset(route("list2", t, 8), PAD))
                ins = V_.tensor_tensor(route("lg", t, 36), ps[:, t * 64:t * 64 + 36], bbc[:, 0:36], ALU.add)
                if t == 0:
                    link(ins)
            read(ins)
            for t in range(NT):
                r = lambda nm, n, t=t: route(nm, t, n)
                link(V_.tensor_copy(r("gpad", 4), r("lg", 4)))
                link(V_.max(r("g8", 8), r("gpad", 16)))
                link(V_.tensor_copy(r("list1", 1), r("g8", 1)))
                link(V_.tensor_scalar(r("ngmax", 1), r("g8", 1), -1.0, None, ALU.mult))
            dve.sem_inc(S["router_max"], 1)
            for t in range(NT):
                r = lambda nm, n, t=t: route(nm, t, n)
                link(V_.match_replace(r("gpad", 16), r("list1", 8), r("gpad", 16), TAKEN1))
                link(V_.tensor_scalar(r("goh", 4), r("gpad", 4), TAKEN1, None, ALU.is_equal))
                link(V_.tensor_scalar(r("gneg", 4), r("goh", 4), 1.0, -NEG, ALU.subtract, ALU.mult))
                e = r("epad", 32).rearrange("p (g e) -> p g e", g=N_GROUP)
                lg = route("lg", t, 36)[:, 4:36].rearrange("p (g e) -> p g e", g=N_GROUP)
                wide = lambda v: v.unsqueeze(2).to_broadcast([P, N_GROUP, PER_GROUP])
                link(V_.tensor_tensor(e, lg, wide(r("goh", 4)), ALU.mult))
                link(V_.tensor_tensor(e, e, wide(r("gneg", 4)), ALU.add))
                link(V_.max(r("e8", 8), r("epad", 48)))
                link(V_.tensor_scalar(r("nv1", 1), r("e8", 1), -1.0, None, ALU.mult))
            dve.sem_inc(S["router_top2"], 1)
            dve.wait_ge(S["router_exp"], w("router_exp", 2))
            for t in range(NT):
                r = lambda nm, n, t=t: route(nm, t, n)
                link(V_.tensor_copy(r("list1", 1), r("e8", 1)))
                link(V_.tensor_copy(r("list2", 1), route("e8", t, 8)[:, 1:2]))
                link(V_.match_replace(r("epad", 48), r("list1", 8), r("epad", 48), TAKEN1))
                link(V_.match_replace(r("epad", 48), r("list2", 8), r("epad", 48), TAKEN2))
                link(V_.tensor_scalar(r("d", 1), r("e21", 1), 1.0, r("gsum", 1), ALU.add, ALU.mult))
                link(V_.reciprocal(r("w1", 1), r("d", 1)))
                link(V_.tensor_tensor(r("w2", 1), r("w1", 1), r("e21", 1), ALU.mult))
                comb = tiny[:, 96 + t * N_EXP:96 + (t + 1) * N_EXP]
                link(V_.tensor_scalar(comb, r("epad", 32), TAKEN1, r("w1", 1), ALU.is_equal, ALU.mult))
                link(V_.tensor_scalar(r("epad", 32), r("epad", 32), TAKEN2, r("w2", 1), ALU.is_equal, ALU.mult))
                link(V_.tensor_tensor(comb, comb, r("epad", 32), ALU.add))
            dve.sem_inc(S["comb_ready"], 1)
            ps = take()
            read(V_.tensor_copy(combT[0:N_EXP, :], ps[0:N_EXP, 0:T]))
            dve.wait_ge(S["c_act"], w("c_act"))
            dve.sem_inc(S["b1_done"], 1)
            zero_operand()
            glu(N_EXP // 2, 0, True, None)

            _, _, n2 = par_at("g_ffn1_2", 0)
            for l in range(LAYERS):
                at = 72 * l
                for s, name in enumerate(("g_ffn1_2", "g_mix_2", "g_ffn2_2")):
                    tile, ga, _ = par_at(name, l)
                    link(V_.scalar_tensor_tensor(modg[:, l * 6 + s, :], ada[:, at + (3 * s + 1) * 8:at + (3 * s + 2) * 8],
                                                 1.0, tile[:, ga:ga + 8], ALU.add, ALU.mult))
                    f = 1.0 if s == 1 else 0.5
                    link(V_.tensor_scalar(modg[:, l * 6 + 3 + s, :], ada[:, at + (3 * s + 2) * 8:at + (3 * s + 3) * 8],
                                          1.0, f, ALU.add, ALU.mult))

            for l in range(LAYERS):
                V = B2
                gain = lambda s, l=l: (lambda j: modg[:, l * 6 + s, j:j + 1])
                shift = lambda s, l=l: (lambda j: ada[:, 72 * l + 3 * s * 8 + j:72 * l + 3 * s * 8 + j + 1])
                gate = lambda s, l=l: (lambda j: modg[:, l * 6 + 3 + s, j:j + 1])

                def flat(nm):
                    return V[nm].rearrange("p a b -> p (a b)")
                norm(xT, gain(0), hT, bias=shift(0))
                zero_operand()
                glu(5, 1, False, gate(0))
                norm(xT, gain(1), hT, bias=shift(1))
                link(V_.memset(V["praw"][:, :, 0:1], 0.0))
                link(V_.memset(V["cu"][:, :, 0:2], 0.0))
                link(V_.memset(flat("state"), 0.0))
                dve.sem_inc(S["state_ready"], 1)
                dve.wait_ge(S["praw_ready"], w("praw_ready"))
                link(V_.tensor_tensor(V["ysh"], V["praw"][:, :, 0:T], V["praw"][:, :, 1:1 + T], ALU.subtract))
                for b in (6, 7, 2, 3, 0, 1, 4, 5):
                    step(V_.scalar_tensor_tensor(V["pm"][:, b, :], V["ysh"][:, b, :], col("rwkv_mu_2", b, l),
                                                 V["praw"][:, b, 1:1 + T], ALU.mult, ALU.add))
                later()
                dve.sem_inc(S["pm_ready"], 1)
                r_, k_, v_ = V["pm"][:, 0:2, :], V["pm"][:, 2:4, :], V["pm"][:, 4:6, :]
                for c in range(2):
                    step(V_.tensor_scalar(V["kk"][:, c, :], k_[:, c, :], col("rwkv_k_k_2", c, l), None, ALU.mult))
                later()
                dve.sem_inc(S["kk_raw"], 1)
                dve.wait_ge(S["sw_ready"], w("sw_ready"))
                for c in range(2):
                    step(V_.tensor_tensor_scan(V["cs"][:, c, :], C("reset"), V["sw"][:, c, :], 0.0, ALU.mult, ALU.add))
                later()
                link(V_.tensor_tensor(flat("csp"), flat("cs"), flat("sw"), ALU.subtract))
                dve.sem_inc(S["cs_ready"], 1)
                ps = take()
                read(V_.tensor_scalar(rsB[:, :], ps[:, :], 1e-24, float(2 ** KK_SHIFT), ALU.max, ALU.mult))
                dve.sem_inc(S["kk_sum"], 1)
                for c in range(2):
                    step(V_.tensor_scalar(V["ysh"][:, 2 + c, :], V["aa"][:, c, :], 1.0, col("rwkv_k_a_2", c, l),
                                          ALU.subtract, ALU.mult))
                later()
                link(V_.scalar_tensor_tensor(k_, V["ysh"][:, 2:4, :], 1.0, k_, ALU.add, ALU.mult))
                for c in range(2):
                    step(V_.scalar_tensor_tensor(V["ysh"][:, c, :], r_[:, c, :], col("rwkv_r_k_2", c, l),
                                                 k_[:, c, :], ALU.mult, ALU.mult))
                later()
                dve.sem_inc(S["bonus_in"], 1)
                dve.wait_ge(S["rs"], w("rs"))
                link(V_.tensor_tensor(flat("kk"), flat("kk"), rsB[:, :], ALU.mult))
                dve.sem_inc(S["rs_used"], 1)
                dve.wait_ge(S["w_ready"], w("w_ready"))
                step(V_.tensor_tensor(flat("al"), flat("kk"), flat("Wprev"), ALU.mult))
                step(V_.tensor_tensor(flat("csp"), flat("kk"), flat("aa"), ALU.mult))
                step(V_.tensor_tensor(V["kap"], k_, V["Winv"], ALU.mult))
                step(V_.tensor_tensor(V["rho"], r_, V["W"], ALU.mult))
                later(2)
                step(V_.tensor_tensor(flat("be"), flat("csp"), flat("Winv"), ALU.mult))
                for c in range(2):
                    for c4 in range(4):
                        step(V_.tensor_copy(tiny[:, 24 + c * 4 + c4:25 + c * 4 + c4],
                                            V["W"][:, c, (c4 + 1) * CHUNK - 1:(c4 + 1) * CHUNK]))
                later()
                dve.sem_inc(S["rwkv_in"], 1)
                for x in range(3):
                    dst = V["q"][:, 2 * x:2 * x + 2, :] if x < 2 else V["k"]
                    scale_rs(dst, col("att_q_gain_2" if x < 2 else "att_k_gain_2", 0, l), 2 if x < 2 else 1)
                dve.sem_inc(S["att_normed"], 1)
                ps = take()
                read(V_.tensor_tensor(flat("bon"), ps[:, :], v_.rearrange("p a b -> p (a b)"), ALU.mult))
                for dst, mask in (("AT", "strict"), ("BT", "strict"), ("C1T", "incl"), ("C2T", "incl")):
                    for g in range(2):
                        ps = take()
                        read(V_.tensor_tensor(V[dst][:, g, :].rearrange("p (a b) -> p a b", a=4),
                                              ps[:, :].rearrange("p (a b) -> p a b", a=4), b3(C(mask), 4), ALU.mult))
                        if dst == "AT":
                            for o in ("Tm", "TT"):
                                step(V_.tensor_copy(V[o][:, g, :].rearrange("p (a b) -> p a b", a=4), b3(C("eye"), 4)))
                            link(V_.tensor_tensor(V["off"][:, g, :].rearrange("p (a b) -> p a b", a=4),
                                                  V["AT"][:, g, :].rearrange("p (a b) -> p a b", a=4),
                                                  b3(C("level0"), 4), ALU.mult))
                            dve.sem_inc(S["off_ready"], 1)
                for lev in range(6):
                    for g in range(2):
                        if lev < 5:
                            ps = take()
                            read(V_.tensor_tensor(V["Tm"][:, g, :], V["Tm"][:, g, :], ps[:, :], ALU.subtract))
                        ps = take()
                        read(V_.tensor_tensor(V["TT"][:, g, :], V["TT"][:, g, :], ps[:, :], ALU.subtract))
                        if lev < 5:
                            link(V_.tensor_tensor(V["off"][:, g, :].rearrange("p (a b) -> p a b", a=4),
                                                  V["AT"][:, g, :].rearrange("p (a b) -> p a b", a=4),
                                                  b3(C(f"level{lev + 1}"), 4), ALU.mult))
                            dve.sem_inc(S["off_ready"], 1)
                dve.sem_inc(S["solve_ready"], 1)
                for c4 in range(4):
                    t, r0 = c4 // 2, (c4 % 2) * CHUNK
                    ps = take()
                    read(V_.tensor_scalar(V["negU"][r0:r0 + CHUNK, t, :], ps[r0:r0 + CHUNK, 0:T], -1.0, None, ALU.mult))
                    dve.sem_inc(S["u_ready"], 1)
                    if c4 < 3:
                        ps = take()
                        read(V_.tensor_tensor(flat("state"), ps[:, 0:T], flat("state"), ALU.add))
                        for c in range(2):
                            step(V_.scalar_tensor_tensor(V["state"][:, c, :], V["state"][:, c, :],
                                                         tiny[:, 24 + c * 4 + c4:25 + c * 4 + c4], C("half"),
                                                         ALU.mult, ALU.mult))
                        later()
                        dve.sem_inc(S["state_ready"], 1)
                dve.wait_ge(S["sconv_in"], w("sconv_in"))
                link(V_.tensor_tensor(V["cu"][:, :, 2:2 + T], V["cc"], V["ch"], ALU.mult))
                for k in range(3):
                    for c in range(2):
                        src, tap = V["cu"][:, c, k:k + T], col("conv_w_2", 2 * k + c, l)
                        if k == 0:
                            step(V_.tensor_scalar(V["cy"][:, c, :], src, tap, None, ALU.mult))
                        else:
                            later(1)
                            step(V_.scalar_tensor_tensor(V["cy"][:, c, :], src, tap, V["cy"][:, c, :],
                                                         ALU.mult, ALU.add))
                later()
                link(V_.tensor_tensor(flat("cy"), flat("cy"), flat("cb"), ALU.mult))
                dve.wait_ge(S["y_done"], w("y_done"))
                link(V_.tensor_copy(flat("W"), bank[7][:, :]))
                dve.sem_inc(S["y_ready"], 1)
                ps = take()
                read(V_.scalar_tensor_tensor(flat("W"), ps[:, :], -1.0 / 64, flat("W"), ALU.mult, ALU.add))
                dve.sem_inc(S["yc_ready"], 1)
                dve.wait_ge(S["rs"], w("rs"))
                for c in range(2):
                    step(V_.scalar_tensor_tensor(V["W"][:, c, :], V["W"][:, c, :], col("rwkv_gn_w_2", c, l),
                                                 rsB[:, c * T:(c + 1) * T], ALU.mult, ALU.mult))
                later()
                dve.sem_inc(S["rs_used"], 1)
                for c in range(2):
                    step(V_.scalar_tensor_tensor(V["W"][:, c, :], V["W"][:, c, :], col("rwkv_gn_b_2", c, l),
                                                 V["bon"][:, c, :], ALU.add, ALU.add))
                later()
                link(V_.tensor_tensor(flat("yr"), flat("W"), flat("gB"), ALU.mult))
                dve.sem_inc(S["mix_ready"], 1)
                attend(GROUPS, V["sc"], V["pr"], 64 ** -0.5,
                       lambda t: C("causal0") if t == 0 else C("window1"), sink=l)
                residual(gate(1))
                norm(xT, gain(2), hT, bias=shift(2))
                zero_operand()
                glu(5, 1, False, gate(2))
            for i in range(KD):
                dve.sem_inc(S["x_ready_pe"], 1)

        @block.sync
        def _(sp):
            w = Seen()
            n_slab = [0]

            def before(n):
                if n >= SLOTS:
                    name, k = slab_end[n - SLOTS]
                    sp.wait_ge(S[name], k)

            def load(src, view=None, first=True):
                n = n_slab[0]
                if first:
                    before(n)
                dst = slab[n % SLOTS]
                sp.dma_start(view(dst) if view else dst[:, :], src).then_inc(S[f"slab{n % SLOTS}_in"], 16)

            def done():
                n_slab[0] += 1

            def matrix(src, c0, cols, kc=KD, width=None):
                width = SLAB // kc
                for c in range(0, cols, width):
                    load(src[:, c0 + c:c0 + c + width].rearrange("(k p) c -> p k c", p=P),
                         lambda d: d[:, :].rearrange("p (k c) -> p k c", k=kc))
                    done()

            def glu_loads(w_up, w_down, f0, half, slot, waits):
                for x in range(3):
                    s = (slot + x) % SLOTS
                    if waits:
                        sp.wait_ge(S[waits[x][0]], waits[x][1])
                    if x < 2:
                        for ab in range(2):
                            src = w_up(ab * half, f0 + x * P)
                            dst = slab[s][:, :].rearrange("p (k c) -> p k c", k=KD)[:, :, ab * P:(ab + 1) * P]
                            sp.dma_start(dst, src).then_inc(S[f"slab{s}_in"], 16)
                    else:
                        sp.dma_start(slab[s][:, :].rearrange("p (j d) -> p j d", j=2), w_down(f0))\
                            .then_inc(S[f"slab{s}_in"], 16)

            def glu(turns, tail, up, down, half):
                n0 = n_slab[0]
                for u in range(2):
                    n = n0 + 3 * u
                    glu_loads(lambda ab, f, u=u: up(0, u, ab, f), lambda f, u=u: down(0, u, f), 0, half, n,
                              [slab_end[n + x - SLOTS] for x in range(3)])
                with sp.Fori(1, turns) as i:
                    for u in range(2):
                        n = n0 + 3 * u
                        waits = [(slab_end[n + x][0], (i - 1) * (4 if x < 2 else 2) + slab_end[n + x][1])
                                 for x in range(3)]
                        glu_loads(lambda ab, f, u=u: up(i, u, ab, f), lambda f, u=u: down(i, u, f), 0, half, n, waits)
                n_slab[0] += 6 * turns
                for u in range(tail):
                    n = n_slab[0]
                    glu_loads(lambda ab, f, u=u: up(turns, u, ab, f), lambda f, u=u: down(turns, u, f), 0, half, n,
                              [slab_end[n + x - SLOTS] for x in range(3)])
                    n_slab[0] += 3

            sp.dma_start(const[:, :], a["const"]).then_inc(S["const_in"], 16)
            sp.dma_start(xin, a["x"][0].rearrange("(t p) d -> p t d", p=P)).then_inc(S["x_in"], 16)
            sp.dma_start(memin, a["mem"][0].rearrange("(t p) d -> p t d", p=P)).then_inc(S["mem_in"], 16)
            w_in = a["w_in"][0]
            matrix(w_in, 768, 512)
            for x, (c0, cn, d0) in enumerate(((1280, 64, 0), (1280, 64, 64), (1344, 8, 128))):
                load(w_in[:, c0:c0 + cn].rearrange("(k p) c -> p k c", p=P),
                     lambda d, d0=d0, cn=cn: d[:, :].rearrange("p (k c) -> p k c", k=KD)[:, :, d0:d0 + cn], x == 0)
            done()
            matrix(w_in, 512, 256)
            matrix(w_in, 0, 512)
            matrix(w_in, 1352, 1024)
            matrix(w_in, 2376, 512)
            matrix(a["w_mem_kv"][0], 0, 1024)
            matrix(w_in, 2888, 3072)
            for name in ("w_br_a", "w_br_m", "w_br_b"):
                matrix(a[name][0], 0, D, kc=4)
            matrix(a["w_o"][0], 0, D)

            def moe_up(i, u, ab, f):
                wv = a["w_up"][0].rearrange("e r c -> (e r) c")
                return wv[bass.ds(i * 2 * D + u * D, D), ab + f:ab + f + P].rearrange("(k p) c -> p k c", p=P)

            def moe_down(i, u, f):
                wv = a["w_down"][0].rearrange("e r c -> (e r) c")
                return wv[bass.ds(i * 512 + u * 256, 256), :].rearrange("(j p) d -> p j d", p=P)
            glu(N_EXP // 2, 0, moe_up, moe_down, 256)

            for l in range(LAYERS):
                def ffn(up_w, down_w):
                    def up(i, u, ab, f):
                        return up_w[:, bass.ds(i * 512 + (u * 256 + ab + f), P)].rearrange("(k p) c -> p k c", p=P)

                    def down(i, u, f):
                        rows_ = bass.ds(i * 512 + u * 256, 256)
                        return down_w[rows_, :].rearrange("(j p) d -> p j d", p=P)
                    glu(5, 1, up, down, D_FF)
                ffn(a["w_ffn1_in_2"][l], a["w_ffn1_out_2"][l])
                wm = a["w_mix_in_2"][l]
                matrix(wm, 768, 1024)
                matrix(wm, 0, 768)
                matrix(wm, 1792, 768)
                matrix(a["w_mix_out_2"][l], 0, D)
                ffn(a["w_ffn2_in_2"][l], a["w_ffn2_out_2"][l])

        @block.gpsimd
        def _(pool):
            w = Seen()
            pool.wait_ge(S["b1_done"], 1)
            def load(l, i, s):
                cols = bass.ds(i * (2 * ADA_COLS) + s * ADA_COLS, ADA_COLS)
                pool.dma_start(M["ada_in"][:, s, :, :], a["w_ada_2"][l][:, cols].rearrange("(k p) c -> p k c", p=P))\
                    .then_inc(S[f"ada{s}_in"], 16)
            for l in range(LAYERS):
                if l == 0:
                    for s in range(2):
                        load(0, 0, s)
                with pool.Fori(1 if l == 0 else 0, ADA_SLABS // 2) as i:
                    pool.wait_ge(S["ada_step"], i * 16 + (0 if l == 0 else 8 * 16))
                    for s in range(2):
                        load(l, i, s)


ROW_COUNTS = [sum(n for _, n in ROWS_1), LAYERS * sum(n for _, n in ROWS_2), TAPS * 4, 72, 72]

INPUTS = ["x", "mem", "g_mix", "w_in", "b_gate", "g_qa", "g_ka", "g_idx_k", "conv_w", "conv_b", "ln_g", "ln_b",
          "g_mem", "w_mem_kv", "g_qm", "g_km", "w_br_a", "w_br_b", "w_br_m", "w_o", "g_ffn", "w_rg", "b_rg",
          "w_re", "b_re", "w_up", "w_down", "c_2", "w_ada_2", "b_ada_2", "g_ffn1_2", "w_ffn1_in_2",
          "w_ffn1_out_2", "g_mix_2", "w_mix_in_2", "w_mix_out_2", "att_q_gain_2", "att_k_gain_2",
          "att_sinks_2", "rwkv_mu_2", "rwkv_w0_2", "rwkv_w_w2_2", "rwkv_a0_2", "rwkv_a_w2_2", "rwkv_g_w2_2",
          "rwkv_k_k_2", "rwkv_k_a_2", "rwkv_r_k_2", "rwkv_gn_w_2", "rwkv_gn_b_2", "conv_w_2", "g_ffn2_2",
          "w_ffn2_in_2", "w_ffn2_out_2"]


def kernel(**inputs):
    import concourse.bacc as bacc
    from concourse.bass_utils import run_bass_kernel_spmd

    nc = bacc.Bacc("TRN2", target_bir_lowering=False, num_devices=1)
    arrays, a = {}, {}
    for name in INPUTS:
        v = np.ascontiguousarray(inputs[name])
        arrays["in_" + name] = v
        a[name] = nc.dram_tensor("in_" + name, v.shape, mybir.dt.from_np(v.dtype), kind="ExternalInput").ap()
    v = _constants()[0]
    arrays["in_const"] = v
    a["const"] = nc.dram_tensor("in_const", v.shape, mybir.dt.float32, kind="ExternalInput").ap()
    out = nc.dram_tensor("out_x", (1, T, D), mybir.dt.float32, kind="ExternalOutput").ap()
    build(nc, a, out)
    r = run_bass_kernel_spmd(nc, [arrays], core_ids=[0])
    return r.results[0]["out_x"]
```

```python
import math
from contextlib import ExitStack

import numpy as np
import concourse.bass as bass
from concourse import mybir

P = 128
D = 1024
KD = D // P
T = 256
NT = T // P
EPS = 1e-6
NEG = -1e30
PAD = -3e38
TAKEN1 = 3e38
TAKEN2 = 2e38
TOPK = 64
HEADS = 8
N_EXP = 32
N_GROUP = 4
PER_GROUP = N_EXP // N_GROUP
TAPS = 31
LAYERS = 2
D_FF = 2816
CHUNK = 64
SLOTS = 6
SLAB = 2048
RING = 7
ADA_COLS = 576
ADA_SLABS = 9 * D // ADA_COLS
DECAY_C = math.exp(-0.5)
KK_SHIFT = 24

def _constants():
    eye = np.eye(P, dtype=np.float32)
    ones = np.ones((P, P), np.float32)
    p = np.arange(P)
    half = (p[:, None] // 64 == p[None, :] // 64).astype(np.float32)
    rot = np.zeros((P, P), np.float32)
    for m in range(P):
        if m % 64 < 32:
            rot[m + 32, m] = -1.0
        else:
            rot[m - 32, m] = 1.0
    dup0 = (p[:, None] == p[None, :] % 64).astype(np.float32)
    dup1 = (p[:, None] == 64 + p[None, :] % 64).astype(np.float32)
    inv = np.float32(10000.0) ** (-np.arange(32, dtype=np.float32) / np.float32(32))
    ang = np.arange(T, dtype=np.float32)[None, :] * inv[p % 32][:, None].astype(np.float32)
    cos, sin = np.cos(ang).astype(np.float32), np.sin(ang).astype(np.float32)
    key = np.arange(T)
    causal0 = np.where(key[None, :P] <= p[:, None], 0.0, NEG).astype(np.float32)
    causal1 = np.where(key[None, :] <= P + p[:, None], 0.0, NEG).astype(np.float32)
    gap = P + p[:, None] - key[None, :]
    window1 = np.where((gap >= 0) & (gap < 128), 0.0, NEG).astype(np.float32)
    same = p[:, None] // CHUNK == p[None, :] // CHUNK
    strict = (same & (p[:, None] < p[None, :])).astype(np.float32)
    incl = (same & (p[:, None] <= p[None, :])).astype(np.float32)
    levels = []
    for m in (1, 2, 4, 8, 16, 32):
        blk = p[:, None] // (2 * m) == p[None, :] // (2 * m)
        levels.append((blk & (p[:, None] % (2 * m) < m) & (p[None, :] % (2 * m) >= m)).astype(np.float32))
    reset = np.tile((np.arange(T) % CHUNK != 0).astype(np.float32), (P, 1))
    small = np.zeros((P, 8), np.float32)
    small[:, 0] = EPS
    small[:, 1] = 64e-5
    small[:, 2] = 0.5 * KK_SHIFT * math.log(2.0)
    parts = dict(eye=eye, ones=ones, small=small, half=half, rot=rot, dup0=dup0, dup1=dup1, cos=cos,
                 sin=sin, causal0=causal0, causal1=causal1, window1=window1, strict=strict, incl=incl,
                 reset=reset, **{f"level{n}": v for n, v in enumerate(levels)})
    at, where = 0, {}
    for name, v in parts.items():
        where[name] = (at, v.shape[1])
        at += v.shape[1]
    return np.ascontiguousarray(np.concatenate(list(parts.values()), axis=1)), where


ROWS_1 = [("g_mix", 8), ("g_mem", 8), ("g_ffn", 8), ("b_gate", 24), ("conv_b", 4), ("ln_g", 4),
          ("ln_b", 4), ("g_qa", 1), ("g_ka", 1), ("g_idx_k", 1), ("g_qm", 1), ("g_km", 1), ("c_2", 8)]
ROWS_2 = [("g_ffn1_2", 8), ("g_mix_2", 8), ("g_ffn2_2", 8), ("att_q_gain_2", 1), ("att_k_gain_2", 1),
          ("rwkv_mu_2", 8), ("rwkv_w0_2", 2), ("rwkv_a0_2", 2), ("rwkv_k_k_2", 2), ("rwkv_k_a_2", 2),
          ("rwkv_r_k_2", 2), ("rwkv_gn_w_2", 2), ("rwkv_gn_b_2", 2), ("conv_w_2", 6)]

SEMAPHORES = {
    "const_in": "constants", "x_in": "tokens", "mem_in": "memory tokens", "rows_in": "block 1's vectors",
    "others_in": "the other small inputs", "const_more": "the other constants",
    **{f"slab{s}_in": "a weight slab in this slot" for s in range(SLOTS)},
    "ada_in0": "an even slab of w_ada", "ada_in1": "an odd one", "out_written": "the result is in DRAM",
    "for_act": "a product for ScalarE", "for_dve": "a product for VectorE",
    "read_by_act": "ScalarE has read one and written what came of it",
    "read_by_dve": "VectorE has read one and written what came of it",
    "up_done": "gate|up of 128 hidden features", "down_done": "a unit's part of the output",
    "comb_done": "an expert's combine weights on every partition", "ada_sum": "adaLN sums over partitions",
    "y_done": "the recurrence's output is complete",
    "act_step": "a step of its own chain", "params_more": "parameter columns of block 2, taps and biases", "params": "parameter columns", "c_act": "silu(c)",
    "sq": "four chunks of squares", "rs": "reciprocal norms", "ki_sq": "squares of the index key",
    "qka_sq": "squares of attention queries and key", "qkm_sq": "squares of memory queries and keys",
    "rl_ready": "rectified index logits", "glu_in": "conv value and gate", "att_exp": "exponentials and sums",
    "att_pT": "transposed probabilities", "oa_ready": "sparse attention output", "om_ready": "memory attention output",
    "swa_ready": "window attention output", "ob_ready": "conv branch output", "router_exp": "the router's exponentials",
    "silu_ready": "silu of a gate block", "praw_ready": "RWKV projections", "lora_in": "low-rank inputs",
    "sw_ready": "decay and rate sigmoids", "kk_sq": "squares of the removal key", "att_sq": "squares of q and k",
    "w_ready": "decay products", "sconv_in": "short conv inputs", "m1_ready": "first half of a doubling",
    "r_ready": "a chunk's right-hand side", "yc_sq": "squares of the centred output",
    "kdup_ready": "keys on both partition halves",
    **{f"hi{x}_ready": "the high part of slab x of a unit" for x in range(3)},
    "h_high": "the high part of a chunk of the normalised residual",
    **{f"lo{x}_ready": "the low part of slab x of a unit, and so the slab is free" for x in range(3)},
    "h_split": "both parts of a chunk of the normalised residual",
    "dve_step": "a step of its own chains", "hn": "a chunk of the normalised residual",
    "memh": "a chunk of the normalised memory", "memh_all": "all of it, its source is free",
    "rs_used": "the reciprocal norms are used", "ki_normed": "index key, normed", "idx_roped": "index queries and key",
    "qka_normed": "queries and key, normed", "rl_used": "rectified logits are used", "qa_roped": "queries, rotated",
    "ka_roped": "key, rotated", "dsa_mask": "the mask of selected keys", "qkm_normed": "memory queries and keys, normed",
    "conv_y": "convolution output", "att_max": "scaled scores and their maxima", "att_p": "probabilities",
    "yc_ready": "centred output", "yn_ready": "scaled output", "merged": "gated sum of the branches",
    "x_ready": "a chunk of the residual", "x_ready_pe": "the last residual", "router_max": "the groups' maximum",
    "router_top2": "the two best experts' logits", "comb_ready": "combine weights",
    "zero": "a zero operand", "sel": "an expert's row of the combine weights", "gut": "silu times combine weight",
    "gu_ready": "a block of hidden activations", "ada_step": "one chunk of an adaLN slab added",
    "ada_done": "a pair of adaLN slabs added up", "ada_ready": "nine adaLN columns", "state_ready": "the recurrent state",
    "pm_ready": "token-shifted projections", "kk_raw": "removal key before its norm", "cs_ready": "summed log decays",
    "kk_sum": "its clamped squared norm", "bonus_in": "r k r_k", "rwkv_in": "the recurrence's operands",
    "att_normed": "q and k, normed", "off_ready": "off-diagonal blocks", "solve_ready": "the inverses",
    "u_ready": "a chunk's solution", "y_ready": "the output on chip", "mix_ready": "RWKV output",
    "conv_ready": "short convolution's output",
}


SHORT_FIRST, OUT_EARLY = 2, 4
GATES_LAST = 3
TAPS_FIRST = 22


class Seen:

    def __init__(self):
        self.n, self.i, self.per, self.at = {}, None, {}, {}

    def __call__(self, name, k=1):
        self.n[name] = self.n.get(name, 0) + k
        if self.i is not None:
            return self.i * self.per[name] + self.n[name]
        return self.n[name]

    def enter(self, i, per):
        self.i, self.per, self.at = i, per, dict(self.n)

    def leave(self, turns):
        for name, v in self.n.items():
            grew = v - self.at.get(name, 0)
            if grew:
                assert grew == self.per[name], (name, grew, self.per[name])
                self.n[name] = self.at.get(name, 0) + grew * turns
        self.i = None


def build(nc, a, out, dbg=None):
    F = mybir.dt.float32
    ALU = mybir.AluOpType
    ACT = mybir.ActivationFunctionType
    AX = mybir.AxisListType.X
    _, CW = _constants()
    n_const = sum(w for _, w in CW.values())

    ctx = ExitStack()
    with ctx:
        def sb(name, shape):
            return ctx.enter_context(nc.sbuf_tensor(name, shape, F))

        S = {name: ctx.enter_context(nc.semaphore(name)) for name in SEMAPHORES}

        const = sb("const", [P, n_const])
        slab = [sb(f"slab{i}", [P, SLAB]) for i in range(SLOTS)]
        par1 = sb("par1", [P, sum(n for _, n in ROWS_1)])
        par2 = sb("par2", [P, LAYERS * sum(n for _, n in ROWS_2)])
        taps = sb("taps", [P, TAPS * 4])
        b_ada = sb("b_ada", [P, LAYERS * 72])
        ada = sb("ada", [P, LAYERS * 72])
        brow = sb("brow", [1, 52])
        bbc = sb("bbc", [P, 52])
        router = sb("router", [P, KD, 36])
        lora_wa = sb("lora_wa", [P, LAYERS, T])
        lora_g = sb("lora_g", [P, LAYERS, T])
        c_act = sb("c_act", [P, KD])
        modg = sb("modg", [P, LAYERS * 6, KD])
        xT = sb("xT", [P, KD, T])
        hT_at = nc.sbuf_base
        hT = sb("hT", [P, KD, T])
        sq = sb("sq", [P, KD, T])
        lnt = sb("lnt", [P, 512])
        rsB = sb("rsB", [P, 512])
        silu = sb("silu", [P, 2, T])
        gu = sb("gu", [P, 2, T])
        rows = [silu[:, 0, 0:P]] + [gu[:, n // 2, (n % 2) * P:(n % 2 + 1) * P] for n in range(4)]
        sel = sb("sel", [P, 2, T])
        combT = sb("combT", [P, T])
        tiny = sb("tiny", [P, 160])
        region_n = 25700
        region_at = (nc.sbuf_base + 31) // 32 * 32
        region = sb("region", [P, region_n])
        bank = [ctx.enter_context(nc.psum_tensor(f"bank{i}", [P, 512], F)) for i in range(8)]

        def C(name, lo=0, hi=None):
            at, w = CW[name]
            return const[:, at + lo:at + (w if hi is None else hi)]

        def layout(start, **sizes):
            views, at = {}, start
            for name, shape in sizes.items():
                n = int(np.prod(shape))
                v = region[:, at:at + n]
                if len(shape) == 2:
                    v = v.rearrange("p (a b) -> p a b", a=shape[0])
                elif len(shape) == 3:
                    v = v.rearrange("p (a b c) -> p a b c", a=shape[0], b=shape[1])
                views[name] = v
                at += n
            assert at <= region_n, at
            return views

        B1 = layout(0, qi=(4, T), ki=(T,), wi=(NT, 8), ka=(T,), kdup=(2, T), va=(NT, P), qa=(4, T),
                    u=(4, 30 + T), ug=(4, T), y=(4, T), qm=(4, T), km=(4, T), vm=(NT, 512),
                    memh=(8, T), gate=(24, T), oa=(4, T), score=(NT, T), pick=(NT, T), amask=(NT, T),
                    sc=(2, 512), pr=(2, 512), pT=(2, 512), tmp=(512,), tmp2=(512,))
        B1["om"], B1["ob"], B1["merged"] = B1["qi"], B1["ug"], B1["memh"]
        B1["rl"] = B1["sc"].rearrange("p a (b c) -> p a b c", b=2)
        xin = B1["gate"][:, 0:8, :].rearrange("p a b -> p (a b)").rearrange("p (t d) -> p t d", t=NT)
        memin = B1["gate"][:, 8:16, :].rearrange("p a b -> p (a b)").rearrange("p (t d) -> p t d", t=NT)
        memT = B1["gate"][:, 16:24, :]
        M = layout(0, ada_in=(KD, ADA_COLS), ada_acc=(2, ADA_COLS))
        assert KD * ADA_COLS <= 2 * KD * T + 512
        ada_in = (M["ada_in"], nc.alloc_sbuf_tensor_at("ada_odd", [P, KD, ADA_COLS], F, offset=hT_at)[:, :, :])
        FR = mybir.dt.float32r
        split_at = [region_at + 4 * (KD + 2) * ADA_COLS]

        def split(name, shape):
            t = nc.alloc_sbuf_tensor_at(name, [P, *shape], FR, offset=split_at[0])
            split_at[0] += 4 * int(np.prod(shape))
            assert split_at[0] <= region_at + 4 * region_n
            return t
        w_hi = [split(f"w_hi{x}", [SLAB]) for x in range(3)]
        w_lo = [split(f"w_lo{x}", [SLAB]) for x in range(3)]
        h_hi, h_lo = split("h_hi", [KD, T]), split("h_lo", [KD, T])
        gu_hi, gu_lo = split("gu_hi", [2, T]), split("gu_lo", [2, T])
        B2 = layout(0, q=(4, T), k=(T,), kdup=(2, T), v=(NT, P), o=(4, T), praw=(8, 1 + T), pm=(8, T),
                    cs=(2, T), W=(2, T), gB=(2, T), sw=(2, T), csp=(2, T), Winv=(2, T), Wprev=(2, T), aa=(2, T),
                    kk=(2, T), al=(2, T), be=(2, T), kap=(2, T), rho=(2, T), bon=(2, T),
                    ysh=(8, T), AT=(2, 512), BT=(2, 512), Tm=(2, 512), TT=(2, 512), off=(2, 512),
                    M1=(2, 512), R=(T,), state=(2, P), cb=(2, T), cc=(2, T), ch=(2, T), cu=(2, 2 + T),
                    cy=(2, T))
        for n, name in enumerate(("vt", "bt", "kt", "negU")):
            B2[name] = B2["ysh"][:, 2 * n:2 * n + 2, :]
        flat_praw = B2["praw"].rearrange("p a b -> p (a b)")
        B2["C1T"] = flat_praw[:, 0:1024].rearrange("p (a b) -> p a b", a=2)
        B2["C2T"] = flat_praw[:, 1024:2048].rearrange("p (a b) -> p a b", a=2)
        decays = B2["sw"].offset - region[:, 0:1].offset
        for n, name in enumerate(("sc", "pr", "pT")):
            B2[name] = region[:, decays + n * 1024:decays + (n + 1) * 1024].rearrange("p (a b) -> p a b", a=2)
        B2["th"], B2["yr"] = B2["R"], B2["cs"]

        def par_at(name, layer=None):
            spec, tile = (ROWS_1, par1) if layer is None else (ROWS_2, par2)
            at = 0 if layer is None else layer * sum(n for _, n in ROWS_2)
            for nm, n in spec:
                if nm == name:
                    return tile, at, n
                at += n
            raise KeyError(name)

        def col(name, j=0, layer=None):
            tile, at, _ = par_at(name, layer)
            return tile[:, at + j:at + j + 1]

        ROUTE = {}
        for nm, n in (("gpad", 16), ("epad", 48), ("list1", 8), ("list2", 8), ("lg", 36), ("g8", 8), ("e8", 8),
                      ("ngmax", 1), ("nv1", 1), ("gsum", 1), ("e21", 1), ("d", 1), ("w1", 1), ("w2", 1),
                      ("goh", 4), ("gneg", 4), ("ge", 4)):
            ROUTE[nm] = sum(k for _, k in ROUTE.values()), n
        rscratch = sb("rscratch", [P, NT, sum(k for _, k in ROUTE.values())])

        def route(name, t, n):
            at = ROUTE[name][0]
            return rscratch[:, t, at:at + n]

        def first_rows():
            at = 0
            for name, n in ROWS_1:
                yield from one_row(0, at, n, a[name][0])
                at += n

        def other_rows():
            yield rows[2][0:TAPS * 4, :], a["conv_w"][0, :, 0, :].rearrange("k (c p) -> (k c) p", p=P)
            at = 0
            for l in range(LAYERS):
                for name, n in ROWS_2:
                    src = a[name][l]
                    if len(src.shape) == 2:
                        src = src.rearrange("a b -> (a b)")
                    yield from one_row(1, at, n, src)
                    at += n
            for l in range(LAYERS):
                yield rows[3 + l][0:72, :], a["b_ada_2"][l].rearrange("(c p) -> c p", p=P)
                yield lora_wa[0:64, l, :], a["rwkv_w_w2_2"][l]
                yield lora_wa[64:128, l, :], a["rwkv_a_w2_2"][l]
                yield lora_g[:, l, :], a["rwkv_g_w2_2"][l]
            yield brow[0:1, 0:4], a["b_rg"]
            yield brow[0:1, 4:36], a["b_re"]
            yield brow[0:1, 36:52], a["att_sinks_2"].rearrange("(o l) h -> o (l h)", o=1)
            yield router[:, :, 0:4], a["w_rg"][0].rearrange("(k p) c -> p k c", p=P)
            yield router[:, :, 4:36], a["w_re"][0].rearrange("(k p) c -> p k c", p=P)

        def one_row(tile, at, n, src):
            if src.shape[0] == 64:
                for half in range(2):
                    yield rows[tile][at:at + 1, half * 64:half * 64 + 64], src.rearrange("(o p) -> o p", o=1)
            else:
                yield rows[tile][at:at + n, :], src.rearrange("(c p) -> c p", p=P)

        def b3(ap, n):
            return ap.unsqueeze(1).to_broadcast([ap.shape[0], n, ap.shape[1]])

        slab_end = []
        ring = []
        for_act, for_dve = [], []
        glu_starts = []

        block = ctx.enter_context(nc.Block())

        GROUPS = [(t, h) for t in range(NT) for h in (0, 1, 4, 5)]
        MEM_GROUPS = [(t, h) for t in range(NT) for h in (0, 2)]

        def fillers(i):
            n = len(GROUPS)
            if i <= n:
                return [i - 1] if i else []
            return [2 * (i - n - 1), 2 * (i - n - 1) + 1]

        @block.tensor
        def _(pe):
            w = Seen()
            n_slab = [0]
            made = {"lo0_ready": 0, "lo1_ready": 0, "lo2_ready": 0}

            def mm(o, lhsT, rhs, start=False):
                return nc.tensor.matmul(o, lhsT, rhs, start=start, stop=True, skip_group_check=True)

            def product(consumer):
                n = len(ring)
                if n >= RING:
                    who, k = ring[n - RING]
                    pe.wait_ge(S["read_by_" + who], k)
                b = n % RING
                ring.append((consumer, sum(r == consumer for r, _ in ring) + 1))
                (for_act if consumer == "act" else for_dve).append(b)
                return bank[b]

            def quiet():
                for who in ("act", "dve"):
                    k = sum(r == who for r, _ in ring)
                    if k:
                        pe.wait_ge(S["read_by_" + who], k)

            def arrive(k=16):
                s = n_slab[0] % SLOTS
                n_slab[0] += 1
                pe.wait_ge(S[f"slab{s}_in"], w(f"slab{s}_in", k))
                return slab[s]

            def used(name):
                count = {"for_act": len(for_act), "for_dve": len(for_dve), **made}
                slab_end.append((name, count[name]))

            def transpose(o, in_, last=None):
                k = in_.shape[0]
                return nc.tensor.transpose(o, in_, C("eye")[0:k, 0:k])

            def project(rhs, nblocks, consumer, kc=KD, k=16, first=None, per_slab=None):
                block = projection(rhs, nblocks, consumer, kc, k, first, per_slab)
                for b in range(nblocks):
                    block(b)

            def projection(rhs, nblocks, consumer, kc=KD, k=16, first=None, per_slab=None):
                per = per_slab or SLAB // (kc * P)
                here = {}

                def block(b):
                    if b % per == 0:
                        here["s"] = arrive(k).rearrange("p (k c) -> p k c", k=kc)
                    s = here["s"]
                    ps = product(consumer)
                    for j in range(kc):
                        if first and b == 0:
                            pe.wait_ge(S[first], w(first))
                        m = mm(ps[:, 0:T], s[:, j, (b % per) * P:(b % per + 1) * P], rhs[:, j, :], j == 0)
                    m.then_inc(S["for_" + consumer], 1)
                    if b % per == per - 1 or b == nblocks - 1:
                        used("for_" + consumer)
                return block

            def norm_sum(kc=KD):
                ps = product("act")
                for j in range(kc):
                    if j % 4 == 0:
                        pe.wait_ge(S["sq"], w("sq"))
                    m = mm(ps[:, 0:T], C("ones"), sq[:, j, :], j == 0)
                m.then_inc(S["for_act"], 1)

            def pair_sum(src, mat="half", consumer="act"):
                ps = product(consumer)
                n = src.shape[-1] if len(src.shape) == 2 else 2 * T
                mm(ps[:, 0:n], C(mat), src, True).then_inc(S["for_" + consumer], 1)

            def attention(groups, q, kdup, v, pr, pT, mem=False):
                width = [P * (t + 1) for t in range(NT)] if not mem else [T, T]

                def scores(g):
                    t, h = groups[g]
                    ps = product("dve")
                    for j in range(2):
                        o = ps[:, j * width[t]:(j + 1) * width[t]]
                        if mem:
                            m = mm(o, q[:, h + j, t * P:(t + 1) * P], kdup[:, h + j, :], j == 0)
                        else:
                            r = (h % 2) * 64
                            m = mm(o, q[r:r + 64, h // 2 + j, t * P:(t + 1) * P],
                                   kdup[r:r + 64, h // 4, 0:width[t]], j == 0)
                    m.then_inc(S["for_dve"], 1)

                def turn(g):
                    t, h = groups[g]
                    nk = width[t] // P
                    pe.wait_ge(S["att_p"], w("att_p"))
                    ps = product("act")
                    for x in range(2 * nk):
                        m = transpose(ps[:, x * P:(x + 1) * P], pr[:, g % 2, x * P:(x + 1) * P])
                    m.then_inc(S["for_act"], 1)

                def output(g):
                    t, h = groups[g]
                    nk = width[t] // P
                    pe.wait_ge(S["att_pT"], w("att_pT"))
                    ps = product("act")
                    for j in range(2):
                        for kt in range(nk):
                            x = pT[:, g % 2, (j * nk + kt) * P:(j * nk + kt + 1) * P]
                            if mem:
                                m = mm(ps[:, j * P:(j + 1) * P], v[:, kt, (h + j) * P:(h + j + 1) * P], x,
                                       j == 0 and kt == 0)
                            else:
                                r = (h % 2) * 64
                                m = mm(ps[r:r + 64, j * P:(j + 1) * P],
                                       v[:, kt, (h // 4) * 64:(h // 4) * 64 + 64], x, j == 0 and kt == 0)
                    m.then_inc(S["for_act"], 1)
                return scores, turn, output

            def attend(groups, *args, **kw):
                scores, turn, output = attention(groups, *args, **kw)
                for g in range(len(groups) + 1):
                    if g < len(groups):
                        scores(g)
                    if g:
                        turn(g - 1)
                        output(g - 1)

            def mm3(o, hi, lo, x_hi, x_lo):
                mm(o, hi, x_hi)
                mm(o, hi, x_lo)
                return mm(o, lo, x_hi)

            def glu_unit(u, moe):
                if moe:
                    pe.wait_ge(S["sel"], w("sel"))
                    mm(bank[2][:, 0:T], C("ones")[0:N_EXP, :], sel[0:N_EXP, u, :], True).then_inc(S["comb_done"], 1)
                for j in range(2):
                    n_slab[0] += 1
                    pe.wait_ge(S[f"lo{j}_ready"], w(f"lo{j}_ready"))
                    hi, lo = (v[:, :].rearrange("p (k c) -> p k c", k=KD) for v in (w_hi[j], w_lo[j]))
                    for ab in range(2):
                        o, cols = bank[j][:, ab * T:(ab + 1) * T], slice(ab * P, (ab + 1) * P)
                        for kc in range(KD):
                            mm(o, hi[:, kc, cols], h_hi[:, kc, :], kc == 0)
                            mm(o, hi[:, kc, cols], h_lo[:, kc, :])
                            m = mm(o, lo[:, kc, cols], h_hi[:, kc, :])
                    m.then_inc(S["up_done"], 1)
                    made[f"lo{j}_ready"] += 1
                    used(f"lo{j}_ready")
                n_slab[0] += 1
                pe.wait_ge(S["lo2_ready"], w("lo2_ready"))
                hi, lo = (v[:, :].rearrange("p (j d) -> p j d", j=2) for v in (w_hi[2], w_lo[2]))
                for j in range(2):
                    pe.wait_ge(S["gu_ready"], w("gu_ready"))
                    for d in range(KD):
                        m = mm3(bank[4 + d // 2][:, (d % 2) * T:(d % 2 + 1) * T], hi[:, j, d * P:(d + 1) * P],
                                lo[:, j, d * P:(d + 1) * P], gu_hi[:, j, :], gu_lo[:, j, :])
                m.then_inc(S["down_done"], 1)
                made["lo2_ready"] += 1
                used("lo2_ready")

            def glu(turns, tail, moe):
                quiet()
                glu_starts.append((n_slab[0], {f"slab{s}_in": w.n.get(f"slab{s}_in", 0) for s in range(SLOTS)}))
                for b in range(4, 8):
                    mm(bank[b][:, :], zero[:, 0:P], zero[:, :], True)
                for i in range(KD):
                    pe.wait_ge(S["h_split"], w("h_split"))
                if not moe:
                    w("hn", KD)
                at = n_slab[0]
                with pe.Fori(0, turns) as i:
                    n0, made0 = len(slab_end), dict(made)
                    w.enter(i, {"gu_ready": 4, "sel": 2, "ada_done": 1, "lo0_ready": 2, "lo1_ready": 2, "lo2_ready": 2})
                    for u in range(2):
                        glu_unit(u, moe)
                    if moe:
                        pe.wait_ge(S["ada_done"], w("ada_done"))
                        for b in range(9):
                            m = mm(bank[3][:, b:b + 1], ada_acc[:, b * P:(b + 1) * P], C("ones")[:, 0:1], b == 0)
                        m.then_inc(S["ada_sum"], 1)
                    w.leave(turns)
                n_slab[0] += 6 * (turns - 1)
                body = slab_end[n0:]
                for r in range(1, turns):
                    slab_end.extend((name, k + 2 * r) for name, k in body)
                for name in made:
                    made[name] = made0[name] + 2 * turns
                for u in range(tail):
                    glu_unit(u, moe)
                for n in range(at, n_slab[0]):
                    w(f"slab{n % SLOTS}_in", 16 if (n - at) % 3 == 2 else 32)

            zero = lnt[:, :].bitcast(mybir.dt.bfloat16)[:, 0:512]
            ada_acc = M["ada_acc"].rearrange("p a c -> p (a c)")

            pe.wait_ge(S["const_in"], w("const_in", 16))

            def to_features(src, sem):
                pe.wait_ge(S[sem], w(sem, 16))
                for kc in range(0, KD, 2):
                    ps = product("act")
                    for x in range(4):
                        m = transpose(ps[:, x * P:(x + 1) * P],
                                      src[:, x % 2, (kc + x // 2) * P:(kc + x // 2 + 1) * P])
                    m.then_inc(S["for_act"], 1)

            def to_columns(n):
                ps = product("act")
                transpose(ps[:, 0:ROW_COUNTS[n]], rows[n][0:ROW_COUNTS[n], :]).then_inc(S["for_act"], 1)
            to_features(xin, "x_in")
            norm_sum()
            pe.wait_ge(S["rows_in"], 16 * sum(1 for _ in first_rows()))
            to_columns(0)
            project(hT, 4, "act", first="hn")
            to_features(memin, "mem_in")
            norm_sum()
            s = arrive(48).rearrange("p (k c) -> p k c", k=KD)
            ps = product("act")
            for kc in range(KD):
                m = mm(ps[:, 0:T], s[:, kc, 0:P], hT[:, kc, :], kc == 0)
            m.then_inc(S["for_act"], 1)
            ps = product("act")
            for t in range(NT):
                for kc in range(KD):
                    m = mm(ps[:, t * 8:(t + 1) * 8], hT[:, kc, t * P:(t + 1) * P], s[:, kc, P:P + 8],
                           t == 0 and kc == 0)
            m.then_inc(S["for_act"], 1)
            used("for_act")

            def key_value():
                s = arrive().rearrange("p (k c) -> p k c", k=KD)
                ps = product("act")
                for kc in range(KD):
                    m = mm(ps[:, 0:T], s[:, kc, 0:P], hT[:, kc, :], kc == 0)
                m.then_inc(S["for_act"], 1)
                ps = product("act")
                for t in range(NT):
                    for kc in range(KD):
                        m = mm(ps[:, t * P:(t + 1) * P], hT[:, kc, t * P:(t + 1) * P], s[:, kc, P:2 * P],
                               t == 0 and kc == 0)
                m.then_inc(S["for_act"], 1)
                used("for_act")
            key_value()
            project(hT, 4, "act")
            pe.wait_ge(S["others_in"], 16 * sum(1 for _ in other_rows()))
            for n in range(1, len(ROW_COUNTS)):
                to_columns(n)
            ps = product("act")
            mm(ps[:, 0:52], C("ones")[0:1, :], brow[0:1, :], True).then_inc(S["for_act"], 1)
            pe.wait_ge(S["const_more"], w("const_more", 16))
            pe.wait_ge(S["ki_sq"], w("ki_sq"))
            pair_sum(sq[:, 0, :])
            for x in range(2):
                pair_sum(B1["qi"][:, 2 * x:2 * x + 2, :], "rot", "dve")
            pe.wait_ge(S["ki_normed"], w("ki_normed"))
            pair_sum(B1["ki"], "rot", "dve")
            pe.wait_ge(S["qka_sq"], w("qka_sq"))
            pair_sum(sq[:, 1:3, :])
            pair_sum(sq[:, 3:5, :])
            pair_sum(sq[:, 5, :])
            pe.wait_ge(S["idx_roped"], w("idx_roped"))
            for t, h in GROUPS:
                r, wd = (h % 2) * 64, P * (t + 1)
                ps = product("act")
                for j in range(2):
                    m = mm(ps[:, j * wd:(j + 1) * wd], B1["qi"][r:r + 64, h // 2 + j, t * P:(t + 1) * P],
                           B1["ki"][r:r + 64, 0:wd], j == 0)
                m.then_inc(S["for_act"], 1)
            pe.wait_ge(S["qka_normed"], w("qka_normed"))
            for x in range(2):
                pair_sum(B1["qa"][:, 2 * x:2 * x + 2, :], "rot", "dve")
            pair_sum(B1["ka"], "rot", "dve")
            project(hT, 8, "act")
            pe.wait_ge(S["ka_roped"], w("ka_roped"))
            for x in range(2):
                pair_sum(B1["ka"], f"dup{x}")
            project(hT, 4, "act")
            for i in range(KD):
                pe.wait_ge(S["memh"], w("memh"))
            project(B1["memh"], 4, "act")
            vslab = [arrive().rearrange("p (k c) -> p k c", k=KD) for _ in range(2)]
            for t in range(NT):
                ps = product("act")
                for x in range(2):
                    for kc in range(KD):
                        m = mm(ps[:, x * T:(x + 1) * T], B1["memh"][:, kc, t * P:(t + 1) * P],
                               vslab[x][:, kc, :], x == 0 and kc == 0)
                m.then_inc(S["for_act"], 1)
            used("for_act")
            used("for_act")
            pe.wait_ge(S["qkm_sq"], w("qkm_sq"))
            for x in range(4):
                pair_sum(sq[:, 2 * x:2 * x + 2, :], "ones")
            gates = projection(hT, 24, "act")
            for b in range(24 - GATES_LAST):
                gates(b)
            pe.wait_ge(S["conv_y"], w("conv_y"))
            ps = product("dve")
            for j in range(4):
                m = mm(ps[:, 0:T], C("ones"), B1["y"][:, j, :], j == 0)
            m.then_inc(S["for_dve"], 1)
            for b in range(24 - GATES_LAST, 24):
                gates(b)
            norm_sum(4)
            pe.wait_ge(S["qa_roped"], w("qa_roped"))
            pe.wait_ge(S["dsa_mask"], w("dsa_mask"))
            pe.wait_ge(S["qkm_normed"], w("qkm_normed"))
            own = attention(GROUPS, B1["qa"], B1["kdup"], B1["va"], B1["pr"], B1["pT"])
            mem = attention(MEM_GROUPS, B1["qm"], B1["km"], B1["vm"], B1["pr"], B1["pT"], mem=True)
            both = [(own, g) for g in range(len(GROUPS))] + [(mem, g) for g in range(len(MEM_GROUPS))]
            for i in range(len(both) + 1):
                if i < len(both):
                    (scores, _, _), g = both[i]
                    scores(g)
                if i == 1:
                    pe.wait_ge(S["ob_ready"], w("ob_ready"))
                    branch = projection(B1["ob"], KD, "dve", kc=4)
                if i == len(GROUPS) + 1:
                    pe.wait_ge(S["oa_ready"], w("oa_ready"))
                    branch = projection(B1["oa"], KD, "dve", kc=4)
                for b in fillers(i):
                    branch(b)
                if i:
                    (_, turn, output), g = both[i - 1]
                    turn(g)
                    output(g)
            pe.wait_ge(S["om_ready"], w("om_ready"))
            project(B1["om"], KD, "dve", kc=4)
            pe.wait_ge(S["merged"], w("merged"))
            project(B1["merged"], 8, "dve")
            norm_sum()
            for i in range(KD):
                pe.wait_ge(S["hn"], w("hn"))
            ps = product("dve")
            for t in range(NT):
                for kc in range(KD):
                    m = mm(ps[:, t * 64:t * 64 + 36], hT[:, kc, t * P:(t + 1) * P], router[:, kc, :],
                           t == 0 and kc == 0)
            m.then_inc(S["for_dve"], 1)
            pe.wait_ge(S["comb_ready"], w("comb_ready"))
            ps = product("dve")
            for t in range(NT):
                m = transpose(ps[0:N_EXP, t * P:(t + 1) * P], tiny[:, 96 + t * N_EXP:96 + (t + 1) * N_EXP])
            m.then_inc(S["for_dve"], 1)
            pe.wait_ge(S["zero"], w("zero"))
            glu(N_EXP // 2, 0, True)

            for l in range(LAYERS):
                for part in range(2):
                    norm_sum()
                    if part == 0:
                        pe.wait_ge(S["zero"], w("zero"))
                        glu(5, 1, False)
                        continue
                    V = B2
                    project(hT, 8, "act", first="hn")
                    project(hT, 4, "act")
                    key_value()
                    pe.wait_ge(S["lora_in"], w("lora_in"))
                    ps = product("act")
                    for c in range(2):
                        m = mm(ps[:, c * T:(c + 1) * T], lora_wa[0:64, l, c * P:(c + 1) * P],
                               V["th"][0:64, :], c == 0)
                    m.then_inc(S["for_act"], 1)
                    ps = product("act")
                    for c in range(2):
                        m = mm(ps[:, c * T:(c + 1) * T], lora_wa[64:128, l, c * P:(c + 1) * P],
                               V["pm"][64:128, 6, :], c == 0)
                    m.then_inc(S["for_act"], 1)
                    ps = product("act")
                    for c in range(2):
                        m = mm(ps[:, c * T:(c + 1) * T], lora_g[:, l, c * P:(c + 1) * P],
                               V["pm"][:, 7, :], c == 0)
                    m.then_inc(S["for_act"], 1)
                    pe.wait_ge(S["kk_sq"], w("kk_sq"))
                    pair_sum(sq[:, 0:2, :], consumer="dve")
                    pe.wait_ge(S["att_sq"], w("att_sq"))
                    pair_sum(sq[:, 2:4, :])
                    pair_sum(sq[:, 4:6, :])
                    pair_sum(sq[:, 6, :])
                    short = projection(hT, 6, "act")
                    for b in range(SHORT_FIRST):
                        short(b)
                    pe.wait_ge(S["bonus_in"], w("bonus_in"))
                    pair_sum(V["ysh"][:, 0:2, :], consumer="dve")
                    pe.wait_ge(S["rwkv_in"], w("rwkv_in"))
                    for src in (V["pm"][:, 4:6, :], V["be"], V["kap"]):
                        ps = product("act")
                        for x in range(4):
                            t, c = x // 2, x % 2
                            m = transpose(ps[:, x * P:(x + 1) * P], src[:, c, t * P:(t + 1) * P])
                        m.then_inc(S["for_act"], 1)
                    for left, right in (("be", "al"), ("kap", "al"), ("be", "rho"), ("kap", "rho")):
                        for g in range(2):
                            r = g * 64
                            ps = product("dve")
                            for x in range(4):
                                t, c = x // 2, x % 2
                                m = mm(ps[:, x * P:(x + 1) * P], V[left][r:r + 64, c, t * P:(t + 1) * P],
                                       V[right][r:r + 64, c, t * P:(t + 1) * P], x == 0)
                            m.then_inc(S["for_dve"], 1)
                    pe.wait_ge(S["att_normed"], w("att_normed"))
                    for x in range(2):
                        pair_sum(V["k"], f"dup{x}")
                    scores, turn, output = attention(GROUPS, V["q"], V["kdup"], V["v"], V["pr"], V["pT"])
                    for lev in range(6):
                        for g in range(2):
                            pe.wait_ge(S["off_ready"], w("off_ready"))
                            ps = product("act")
                            for x in range(4):
                                X = slice(x * P, (x + 1) * P)
                                m = mm(ps[:, X], V["off"][:, g, X], V["Tm"][:, g, X], x == 0)
                            m.then_inc(S["for_act"], 1)
                        if lev == 0:
                            pe.wait_ge(S["kdup_ready"], w("kdup_ready"))
                        scores(lev)
                        if SHORT_FIRST + lev < 6:
                            short(SHORT_FIRST + lev)
                        if lev:
                            turn(lev - 1)
                        for g in range(2):
                            pe.wait_ge(S["m1_ready"], w("m1_ready"))
                            if lev < 5:
                                ps = product("dve")
                                for x in range(4):
                                    X = slice(x * P, (x + 1) * P)
                                    m = mm(ps[:, X], V["TT"][:, g, X], V["M1"][:, g, X], x == 0)
                                m.then_inc(S["for_dve"], 1)
                            ps = product("dve")
                            for x in range(4):
                                X = slice(x * P, (x + 1) * P)
                                m = mm(ps[:, X], V["M1"][:, g, X], V["TT"][:, g, X], x == 0)
                            m.then_inc(S["for_dve"], 1)
                        if lev:
                            output(lev - 1)
                    for c4 in range(T // CHUNK):
                        t, r0 = c4 // 2, (c4 % 2) * CHUNK
                        if c4 == 0:
                            pe.wait_ge(S["solve_ready"], w("solve_ready"))
                        pe.wait_ge(S["state_ready"], w("state_ready"))
                        ps = product("act")
                        for h in range(4):
                            X = slice((2 * t + h // 2) * P, (2 * t + h // 2 + 1) * P)
                            mm(ps[:, h * 64:(h + 1) * 64], V["BT"][:, h % 2, X],
                               V["vt"][:, t, h * 64:(h + 1) * 64], h == 0)
                        for c in range(2):
                            m = mm(ps[:, c * P:(c + 1) * P], V["al"][:, c, t * P:(t + 1) * P],
                                   V["state"][:, c, :])
                        m.then_inc(S["for_act"], 1)
                        if 6 + c4 < len(GROUPS):
                            scores(6 + c4)
                        if 5 + c4 < len(GROUPS):
                            turn(5 + c4)
                        for c in range(2):
                            tok = slice(c4 * CHUNK, (c4 + 1) * CHUNK)
                            mm(bank[7][:, c * T + c4 * CHUNK:c * T + (c4 + 1) * CHUNK], V["state"][:, c, :],
                               V["rho"][:, c, tok], c4 == 0 and c == 0)
                        pe.wait_ge(S["r_ready"], w("r_ready"))
                        ps = product("dve")
                        for h in range(4):
                            X = slice((2 * t + h // 2) * P, (2 * t + h // 2 + 1) * P)
                            m = mm(ps[:, h * 64:(h + 1) * 64], V["TT"][:, h % 2, X],
                                   V["R"][:, h * 64:(h + 1) * 64], h == 0)
                        m.then_inc(S["for_dve"], 1)
                        if 5 + c4 < len(GROUPS):
                            output(5 + c4)
                        pe.wait_ge(S["u_ready"], w("u_ready"))
                        if c4 < 3:
                            ps = product("dve")
                            for c in range(2):
                                mm(ps[:, c * P:(c + 1) * P], V["bt"][r0:r0 + CHUNK, t, c * P:(c + 1) * P],
                                   V["negU"][r0:r0 + CHUNK, t, c * P:(c + 1) * P], c == 0)
                                m = mm(ps[:, c * P:(c + 1) * P], V["kt"][r0:r0 + CHUNK, t, c * P:(c + 1) * P],
                                       V["vt"][r0:r0 + CHUNK, t, c * P:(c + 1) * P])
                            m.then_inc(S["for_dve"], 1)
                        if c4 % 2:
                            for h in range(4):
                                X = slice((2 * t + h // 2) * P, (2 * t + h // 2 + 1) * P)
                                o = bank[7][(h % 2) * 64:(h % 2) * 64 + 64,
                                            (h // 2) * T + t * P:(h // 2) * T + (t + 1) * P]
                                mm(o, V["vt"][:, t, h * 64:(h + 1) * 64], V["C2T"][:, h % 2, X])
                                m = mm(o, V["negU"][:, t, h * 64:(h + 1) * 64], V["C1T"][:, h % 2, X])
                            if c4 == 3:
                                m.then_inc(S["y_done"], 1)
                    pe.wait_ge(S["y_ready"], w("y_ready"))
                    pair_sum(V["W"], consumer="dve")
                    pe.wait_ge(S["yc_sq"], w("yc_sq"))
                    pair_sum(sq[:, 0:2, :])
                    pe.wait_ge(S["swa_ready"], w("swa_ready"))
                    pe.wait_ge(S["conv_ready"], w("conv_ready"))
                    parts = [V["o"][:, j, :] for j in range(4)] + [V["yr"][:, j, :] for j in range(2)] \
                        + [V["cy"][:, j, :] for j in range(2)]
                    early, slabs, places = (0, 1, 2, 3, 6, 7), [], []
                    for b in range(KD):
                        if b % 2 == 0 and b < OUT_EARLY:
                            slabs.append(arrive().rearrange("p (k c) -> p k c", k=KD))
                        if b < OUT_EARLY:
                            places.append(product("dve"))
                            for j in early:
                                mm(places[b][:, 0:T], slabs[b // 2][:, j, (b % 2) * P:(b % 2 + 1) * P], parts[j], j == 0)
                    pe.wait_ge(S["mix_ready"], w("mix_ready"))
                    for b in range(KD):
                        if b >= OUT_EARLY:
                            if b % 2 == 0:
                                slabs.append(arrive().rearrange("p (k c) -> p k c", k=KD))
                            places.append(product("dve"))
                        for j in (4, 5) if b < OUT_EARLY else range(KD):
                            m = mm(places[b][:, 0:T], slabs[b // 2][:, j, (b % 2) * P:(b % 2 + 1) * P], parts[j],
                                   j == 0)
                        m.then_inc(S["for_dve"], 1)
                        if b % 2:
                            used("for_dve")
                norm_sum()
                pe.wait_ge(S["zero"], w("zero"))
                glu(5, 1, False)
            for i in range(KD):
                pe.wait_ge(S["x_ready_pe"], w("x_ready_pe"))
            for t in range(NT):
                for x in range(2):
                    ps = product("act")
                    for j in range(4):
                        kc = 4 * x + j
                        m = transpose(ps[:, j * P:(j + 1) * P], xT[:, kc, t * P:(t + 1) * P])
                    m.then_inc(S["for_act"], 1)

        @block.scalar
        def _(act):
            w = Seen()
            banks = iter(for_act)
            table = [None]
            started = set()
            starts = list(glu_starts)

            def tables(name):
                if table[0] != name:
                    nc.scalar.preload_act_table_set(name)
                    table[0] = name
            LNEXP, SIG, SILU = "natural_log_exp_and_others", "sigmoid_and_others", "silu_and_others"

            def take():
                act.wait_ge(S["for_act"], w("for_act"))
                return bank[next(banks)]

            def read(ins):
                ins.then_inc(S["read_by_act"], 1)
                w("read_by_act")

            def link(ins):
                ins.then_inc(S["act_step"], 1)
                act.wait_ge(S["act_step"], w("act_step"))

            def evac(dst, src_cols=None, func=ACT.Copy, shape=None, **kw):
                ps = take()
                src = ps[:, 0:src_cols or T]
                if shape:
                    src = src.rearrange("p (a b) -> p a b", a=shape)
                read(nc.scalar.activation(dst, src, func, **kw))

            def rsqrt_of(ps_ap, dst, scale, bias, sem=None):
                n = ps_ap.shape[-1]
                if "rs" in w.n:
                    act.wait_ge(S["rs"], w.n["rs"])
                w("rs")
                ins = nc.scalar.activation(lnt[:, 0:n], ps_ap, ACT.Ln, scale=scale, bias=bias)
                read(ins)
                act.wait_ge(S["read_by_act"], w.n["read_by_act"])
                if "rs" in started:
                    act.wait_ge(S["rs_used"], w("rs_used"))
                started.add("rs")
                nc.scalar.activation(dst, lnt[:, 0:n], ACT.Exp, scale=-0.5).then_inc(S[sem], 1)

            def squares(src, dst=None):
                n = src.shape[1]
                for x in range(0, n, 4):
                    nc.scalar.activation(sq[:, x:x + 4, :], src[:, x:x + 4, :], ACT.Square)\
                        .then_inc(S["sq"], 1)

            def norm(src, own=False, scale=1.0 / D, glu_next=False):
                if not own:
                    for i in range(KD):
                        act.wait_ge(S["x_ready"], w("x_ready"))
                squares(src)
                at = split_first() if glu_next else None
                tables(LNEXP)
                rsqrt_of(take()[:, 0:T], rsB[:, 0:T], scale, C("small", 0, 1), "rs")
                if glu_next:
                    split_h()
                else:
                    w("hn", KD)
                return at

            def attention(groups, sc, pr, pT, o, mem=False, sink=None):
                width = [P * (t + 1) for t in range(NT)] if not mem else [T, T]
                nm, rsum, es = tiny[:, 0:4], tiny[:, 4:8], tiny[:, 8:12]

                def exps(g):
                    t, h = groups[g]
                    act.wait_ge(S["att_max"], w("att_max"))
                    for j in range(2):
                        k = (g % 2) * 2 + j
                        if sink is not None:
                            hh = h + 2 * j
                            nc.scalar.activation(es[:, k:k + 1], bbc[:, 36 + 8 * sink + hh:37 + 8 * sink + hh], ACT.Exp,
                                                 bias=nm[:, k:k + 1])
                        m = nc.scalar.activation(pr[:, g % 2, j * width[t]:(j + 1) * width[t]],
                                                 sc[:, g % 2, j * width[t]:(j + 1) * width[t]], ACT.Exp,
                                                 bias=nm[:, k:k + 1], accum_out=rsum[:, k:k + 1])
                    m.then_inc(S["att_exp"], 1)

                def turned(g):
                    n = 2 * width[groups[g][0]]
                    ps = take()
                    read(nc.scalar.activation(pT[:, g % 2, 0:n], ps[:, 0:n], ACT.Copy))
                    act.wait_ge(S["read_by_act"], w.n["read_by_act"])
                    act.sem_inc(S["att_pT"], 1)

                def output(g):
                    t, h = groups[g]
                    ps = take()
                    if mem:
                        dst = o[:, h:h + 2, t * P:(t + 1) * P]
                        src = ps[:, 0:2 * P]
                    else:
                        r = (h % 2) * 64
                        dst = o[r:r + 64, h // 2:h // 2 + 2, t * P:(t + 1) * P]
                        src = ps[r:r + 64, 0:2 * P]
                    read(nc.scalar.activation(dst, src.rearrange("p (a b) -> p a b", a=2), ACT.Copy))
                return exps, turned, output

            def attend(groups, sc, pr, pT, o, sem, **kw):
                exps, turned, output = attention(groups, sc, pr, pT, o, **kw)
                for g in range(len(groups) + 1):
                    if g < len(groups):
                        exps(g)
                    if g:
                        turned(g - 1)
                        output(g - 1)
                act.wait_ge(S["read_by_act"], w.n["read_by_act"])
                act.sem_inc(S[sem], 1)

            def split_high(x, slot, k):
                act.wait_ge(S[f"slab{slot}_in"], w(f"slab{slot}_in", k))
                nc.scalar.activation(w_hi[x][:, :], slab[slot][:, :], ACT.Copy).then_inc(S[f"hi{x}_ready"], 1)

            def split_first():
                at, seen = starts.pop(0)
                for name, v in seen.items():
                    w.n[name] = v
                split_high(0, at % SLOTS, 32)
                split_high(1, (at + 1) % SLOTS, 32)
                return at

            def split_h():
                for j in range(KD):
                    act.wait_ge(S["hn"], w("hn"))
                    nc.scalar.activation(h_hi[:, j, :], hT[:, j, :], ACT.Copy).then_inc(S["h_high"], 1)

            def glu(at, turns, tail, moe):
                tables(SILU)
                split_high(2, (at + 2) % SLOTS, 16)

                def load_ada(l, i, u, used=None):
                    if used is not None:
                        act.wait_ge(S["ada_step"], used)
                    cols = a["w_ada_2"][l][:, bass.ds(i * (2 * ADA_COLS) + u * ADA_COLS, ADA_COLS)]
                    act.dma_start(ada_in[u], cols.rearrange("(k p) c -> p k c", p=P)).then_inc(S[f"ada_in{u}"], 16)

                def unit(u, pos, more, ada=None):
                    for j in range(2):
                        act.wait_ge(S["up_done"], w("up_done"))
                        nc.scalar.activation(silu[:, j, :], bank[j][:, 0:T], ACT.Silu)\
                            .then_inc(S["silu_ready"], 1)
                        if more:
                            split_high(j, (pos + j) % SLOTS, 32)
                        if ada and j == 0:
                            load_ada(*ada)
                    act.wait_ge(S["down_done"], w("down_done"))
                    if more:
                        split_high(2, (pos + 2) % SLOTS, 16)
                per = {"up_done": 4, "down_done": 2}
                per |= {f"slab{(at + x) % SLOTS}_in": (32, 32, 16)[x % 3] for x in range(6)}
                if not moe:
                    with act.Fori(0, turns) as i:
                        w.enter(i, per)
                        for u in range(2):
                            unit(u, at + 3 * (u + 1), True)
                        w.leave(turns)
                    unit(0, 0, False)
                    return
                half = turns // LAYERS
                load_ada(0, 0, 0)
                unit(0, at + 3, True, (0, 0, 1))
                unit(1, at + 6, True, (0, 1, 0, 8))
                for l in range(LAYERS):
                    start = 1 if l == 0 else 0
                    k = half - 1 - start
                    with act.Fori(start, half - 1) as i:
                        w.enter(i - start if start else i, per)
                        unit(0, at + 3, True, (l, i, 1, i * 16 + 16 * half * l))
                        unit(1, at + 6, True, (l, i + 1, 0, i * 16 + 16 * half * l + 8))
                        w.leave(k)
                    n = 16 * (half * (l + 1) - 1)
                    unit(0, at + 3, True, (l, half - 1, 1, n))
                    unit(1, at + 6, l < LAYERS - 1, (l + 1, 0, 0, n + 8) if l < LAYERS - 1 else None)

            for dst, src in first_rows():
                act.dma_start(dst, src).then_inc(S["rows_in"], 16)
            act.wait_ge(S["const_in"], w("const_in", 16))

            def columns(dst, n):
                ps = take()
                read(nc.scalar.activation(dst[:, 0:n], ps[:, 0:n], ACT.Copy))
            for kc in range(0, KD, 2):
                evac(xT[:, kc:kc + 2, :].rearrange("p a b -> p (a b)"), 512)
            act.wait_ge(S["read_by_act"], w.n["read_by_act"])
            squares(xT)
            tables(LNEXP)
            rsqrt_of(take()[:, 0:T], rsB[:, 0:T], 1.0 / D, C("small", 0, 1), "rs")
            columns(par1, ROW_COUNTS[0])
            act.wait_ge(S["read_by_act"], w.n["read_by_act"])
            act.sem_inc(S["params"], 1)
            w("hn", KD)
            for c in range(4):
                evac(B1["qi"][:, c, :])
            for kc in range(0, KD, 2):
                evac(memT[:, kc:kc + 2, :].rearrange("p a b -> p (a b)"), 512)
            act.wait_ge(S["read_by_act"], w.n["read_by_act"])
            squares(memT)
            rsqrt_of(take()[:, 0:T], rsB[:, 0:T], 1.0 / D, C("small", 0, 1), "rs")
            evac(B1["ki"])
            ps = take()
            read(nc.scalar.activation(B1["wi"], ps[:, 0:16].rearrange("p (a b) -> p a b", a=2), ACT.Copy,
                                      scale=8 ** -0.5))
            act.wait_ge(S["read_by_act"], w.n["read_by_act"])
            nc.scalar.activation(sq[:, 0, :], B1["ki"], ACT.Square).then_inc(S["ki_sq"], 1)
            evac(B1["ka"])
            evac(B1["va"], shape=2)
            for c in range(4):
                evac(B1["qa"][:, c, :])
            for dst, n in ((par2, ROW_COUNTS[1]), (taps, ROW_COUNTS[2]),
                           (b_ada[:, 0:72], 72), (b_ada[:, 72:144], 72), (bbc, 52)):
                columns(dst, n)
            act.wait_ge(S["read_by_act"], w.n["read_by_act"])
            act.sem_inc(S["params_more"], 1)
            nc.scalar.activation(sq[:, 1:5, :], B1["qa"], ACT.Square)
            nc.scalar.activation(sq[:, 5, :], B1["ka"], ACT.Square).then_inc(S["qka_sq"], 1)
            rsqrt_of(take()[:, 0:T], rsB[:, 0:T], 1.0 / 64, C("small", 0, 1), "rs")
            for x in range(3):
                n = 512 if x < 2 else T
                rsqrt_of(take()[:, 0:n], rsB[:, 0:n], 1.0 / 64, C("small", 0, 1), "rs")
            for g, (t, h) in enumerate(GROUPS):
                wd = P * (t + 1)
                ps = take()
                if g >= 2:
                    act.wait_ge(S["rl_used"], w("rl_used"))
                read(nc.scalar.activation(B1["rl"][:, g % 2, :, 0:wd],
                                          ps[:, 0:2 * wd].rearrange("p (a b) -> p a b", a=2), ACT.Relu,
                                          scale=64 ** -0.5))
                act.wait_ge(S["read_by_act"], w.n["read_by_act"])
                act.sem_inc(S["rl_ready"], 1)
            for c in range(4):
                evac(B1["u"][:, c, 30:30 + T])
            tables(SIG)
            for c in range(4):
                evac(B1["ug"][:, c, :], func=ACT.Sigmoid)
            act.wait_ge(S["read_by_act"], w.n["read_by_act"])
            act.sem_inc(S["glu_in"], 1)
            for x in range(2):
                evac(B1["kdup"][:, x, :])
            for c in range(4):
                evac(B1["qm"][:, c, :])
            tables(LNEXP)
            for c in range(4):
                evac(B1["km"][:, c, :])
            act.wait_ge(S["read_by_act"], w.n["read_by_act"])
            nc.scalar.activation(sq[:, 0:4, :], B1["qm"], ACT.Square)
            nc.scalar.activation(sq[:, 4:8, :], B1["km"], ACT.Square).then_inc(S["qkm_sq"], 1)
            for t in range(NT):
                evac(B1["vm"][:, t, :], 512)
            for x in range(4):
                rsqrt_of(take()[:, 0:512], rsB[:, 0:512], 1.0 / P, C("small", 0, 1), "rs")
            tables(SIG)
            act.wait_ge(S["memh_all"], w("memh_all"))
            for c in range(24 - GATES_LAST):
                evac(B1["gate"][:, c, :], func=ACT.Sigmoid, bias=col("b_gate", c))
            act.wait_ge(S["yc_ready"], w("yc_ready"))
            squares(B1["y"])
            for c in range(24 - GATES_LAST, 24):
                evac(B1["gate"][:, c, :], func=ACT.Sigmoid, bias=col("b_gate", c))
            tables(LNEXP)
            rsqrt_of(take()[:, 0:T], rsB[:, 0:T], 1.0 / 512, C("small", 0, 1), "rs")
            tables(SILU)
            _, ca, _ = par_at("c_2")
            nc.scalar.activation(c_act[:, :], par1[:, ca:ca + KD], ACT.Silu).then_inc(S["c_act"], 1)
            act.wait_ge(S["yn_ready"], w("yn_ready"))
            for c in range(4):
                m = nc.scalar.activation(B1["ob"][:, c, :], B1["y"][:, c, :], ACT.Silu, bias=col("ln_b", c))
            m.then_inc(S["ob_ready"], 1)
            tables(LNEXP)
            own = attention(GROUPS, B1["sc"], B1["pr"], B1["pT"], B1["oa"])
            mem = attention(MEM_GROUPS, B1["sc"], B1["pr"], B1["pT"], B1["om"], mem=True)
            both = [(own, g) for g in range(len(GROUPS))] + [(mem, g) for g in range(len(MEM_GROUPS))]
            for i in range(len(both) + 1):
                if i < len(both):
                    (exps, _, _), g = both[i]
                    exps(g)
                if i:
                    (_, turned, output), g = both[i - 1]
                    turned(g)
                    output(g)
                if i == len(GROUPS) or i == len(both):
                    act.wait_ge(S["read_by_act"], w.n["read_by_act"])
                    act.sem_inc(S["oa_ready" if i == len(GROUPS) else "om_ready"], 1)
            at = norm(xT, glu_next=True)
            act.wait_ge(S["router_max"], w("router_max"))
            for t in range(NT):
                m = nc.scalar.activation(route("ge", t, 4), route("lg", t, 4), ACT.Exp, bias=route("ngmax", t, 1),
                                         accum_out=route("gsum", t, 1))
            m.then_inc(S["router_exp"], 1)
            act.wait_ge(S["router_top2"], w("router_top2"))
            for t in range(NT):
                m = nc.scalar.activation(route("e21", t, 1), route("e8", t, 8)[:, 1:2], ACT.Exp,
                                         bias=route("nv1", t, 1))
            m.then_inc(S["router_exp"], 1)
            glu(at, N_EXP // 2, 0, True)

            for l in range(LAYERS):
                V = B2
                at = norm(xT, glu_next=True)
                glu(at, 5, 1, False)
                norm(xT)
                for b in range(8):
                    evac(V["praw"][:, b, 1:1 + T])
                act.wait_ge(S["read_by_act"], w.n["read_by_act"])
                act.sem_inc(S["praw_ready"], 1)
                for c in range(4):
                    evac(V["q"][:, c, :])
                evac(V["k"])
                evac(V["v"], shape=2)
                tables(SIG)
                act.wait_ge(S["pm_ready"], w("pm_ready"))
                nc.scalar.activation(V["th"][0:64, :], V["pm"][0:64, 6, :], ACT.Tanh)
                nc.scalar.activation(V["pm"][:, 7, :], V["pm"][:, 7, :], ACT.Sigmoid).then_inc(S["lora_in"], 1)
                ps = take()
                nc.scalar.activation(V["sw"][:, 0, :], ps[:, 0:T], ACT.Sigmoid, bias=col("rwkv_w0_2", 0, l))
                read(nc.scalar.activation(V["sw"][:, 1, :], ps[:, T:2 * T], ACT.Sigmoid,
                                          bias=col("rwkv_w0_2", 1, l)))
                ps = take()
                nc.scalar.activation(V["aa"][:, 0, :], ps[:, 0:T], ACT.Sigmoid, bias=col("rwkv_a0_2", 0, l))
                read(nc.scalar.activation(V["aa"][:, 1, :], ps[:, T:2 * T], ACT.Sigmoid,
                                          bias=col("rwkv_a0_2", 1, l)))
                act.wait_ge(S["read_by_act"], w.n["read_by_act"])
                act.sem_inc(S["sw_ready"], 1)
                evac(V["gB"], 512, shape=2)
                act.wait_ge(S["kk_raw"], w("kk_raw"))
                nc.scalar.activation(sq[:, 0:2, :], V["kk"], ACT.Square).then_inc(S["kk_sq"], 1)
                nc.scalar.activation(sq[:, 2:6, :], V["q"], ACT.Square)
                nc.scalar.activation(sq[:, 6, :], V["k"], ACT.Square).then_inc(S["att_sq"], 1)
                tables(LNEXP)
                act.wait_ge(S["kk_sum"], w("kk_sum"))
                act.wait_ge(S["rs"], w.n["rs"])
                w("rs")
                link(nc.scalar.activation(lnt[:, :], rsB[:, :], ACT.Ln))
                act.wait_ge(S["rs_used"], w("rs_used"))
                nc.scalar.activation(rsB[:, :], lnt[:, :], ACT.Exp, scale=-0.5, bias=C("small", 2, 3))\
                    .then_inc(S["rs"], 1)
                act.wait_ge(S["cs_ready"], w("cs_ready"))
                nc.scalar.activation(V["W"], V["cs"], ACT.Exp, scale=-DECAY_C)
                nc.scalar.activation(V["Winv"], V["cs"], ACT.Exp, scale=DECAY_C)
                nc.scalar.activation(V["Wprev"], V["csp"], ACT.Exp, scale=-DECAY_C).then_inc(S["w_ready"], 1)
                for x in range(3):
                    n = 512 if x < 2 else T
                    rsqrt_of(take()[:, 0:n], rsB[:, 0:n], 1.0 / 64, C("small", 0, 1), "rs")
                short = [V[dst][:, c, :] for dst in ("cb", "cc", "ch") for c in range(2)]
                for b in range(SHORT_FIRST):
                    evac(short[b])
                for dst in ("vt", "bt", "kt"):
                    evac(V[dst], 512, shape=2)
                for x in range(2):
                    evac(V["kdup"][:, x, :])
                act.wait_ge(S["read_by_act"], w.n["read_by_act"])
                act.sem_inc(S["kdup_ready"], 1)
                exps, turned, output = attention(GROUPS, V["sc"], V["pr"], V["pT"], V["o"], sink=l)
                for lev in range(6):
                    for g in range(2):
                        evac(V["M1"][:, g, :], 512)
                        act.wait_ge(S["read_by_act"], w.n["read_by_act"])
                        act.sem_inc(S["m1_ready"], 1)
                    if SHORT_FIRST + lev < 6:
                        evac(short[SHORT_FIRST + lev])
                        if SHORT_FIRST + lev == 5:
                            act.wait_ge(S["read_by_act"], w.n["read_by_act"])
                            act.sem_inc(S["sconv_in"], 1)
                    if lev:
                        turned(lev - 1)
                    exps(lev)
                    if lev:
                        output(lev - 1)
                for c4 in range(4):
                    evac(V["R"], T)
                    act.wait_ge(S["read_by_act"], w.n["read_by_act"])
                    act.sem_inc(S["r_ready"], 1)
                    if 5 + c4 < len(GROUPS):
                        turned(5 + c4)
                    if 6 + c4 < len(GROUPS):
                        exps(6 + c4)
                    if 5 + c4 < len(GROUPS):
                        output(5 + c4)
                act.wait_ge(S["read_by_act"], w.n["read_by_act"])
                act.sem_inc(S["swa_ready"], 1)
                act.wait_ge(S["yc_ready"], w("yc_ready"))
                nc.scalar.activation(sq[:, 0:2, :], V["W"], ACT.Square).then_inc(S["yc_sq"], 1)
                rsqrt_of(take()[:, 0:512], rsB[:, 0:512], 1.0 / 64, C("small", 1, 2), "rs")
                at = norm(xT, glu_next=True)
                glu(at, 5, 1, False)
            for t in range(NT):
                for x in range(2):
                    evac(hT[:, 4 * t + 2 * x:4 * t + 2 * x + 2, :].rearrange("p a b -> p (a b)"), 512)
            act.wait_ge(S["read_by_act"], w.n["read_by_act"])
            act.dma_start(out[0].rearrange("(t p) d -> p t d", p=P),
                          hT[:, :, :].rearrange("p a b -> p (a b)").rearrange("p (t d) -> p t d", t=NT))\
                .then_inc(S["out_written"], 16)
            act.wait_ge(S["out_written"], 16)

        @block.vector
        def _(dve):
            w = Seen()
            banks = iter(for_dve)
            V_ = nc.vector
            starts = [n for n, _ in glu_starts]

            def take():
                dve.wait_ge(S["for_dve"], w("for_dve"))
                return bank[next(banks)]

            def read(ins):
                ins.then_inc(S["read_by_dve"], 1)
                dve.wait_ge(S["read_by_dve"], w("read_by_dve"))

            def step(ins):
                ins.then_inc(S["dve_step"], 1)
                w("dve_step")

            def later(k=0):
                dve.wait_ge(S["dve_step"], w.n["dve_step"] - k)

            def link(ins):
                step(ins)
                later()

            def norm(src, gain, dst, sem="hn", bias=None, last_free=None, n=KD, own=False):
                dve.wait_ge(S["rs"], w("rs"))
                for j in range(n):
                    ins = V_.scalar_tensor_tensor(dst[:, j, :], src[:, j, :], gain(j), rsB[:, 0:T],
                                                  ALU.mult, ALU.mult)
                    if bias is None:
                        ins.then_inc(S[sem], 1)
                    else:
                        step(ins)
                if bias is None:
                    dve.wait_ge(S[sem], w(sem, n))
                    dve.sem_inc(S["rs_used"], 1)
                else:
                    for j in range(n):
                        later(n - 1 - j)
                        V_.tensor_scalar(dst[:, j, :], dst[:, j, :], bias(j), None, ALU.add)\
                            .then_inc(S[sem], 1)
                    dve.wait_ge(S[sem], w(sem, n))
                    dve.sem_inc(S["rs_used"], 1)

            def split_low(x, n):
                dve.wait_ge(S[f"hi{x}_ready"], w(f"hi{x}_ready"))
                V_.tensor_tensor(w_lo[x][:, :], slab[n % SLOTS][:, :], w_hi[x][:, :].bitcast(F), ALU.subtract)\
                    .then_inc(S[f"lo{x}_ready"], 1)

            def split_h():
                for j in range(KD):
                    dve.wait_ge(S["h_high"], w("h_high"))
                    V_.tensor_tensor(h_lo[:, j, :], hT[:, j, :], h_hi[:, j, :].bitcast(F), ALU.subtract)\
                        .then_inc(S["h_split"], 1)

            def scale_rs(dst, gain_col, nb):
                dve.wait_ge(S["rs"], w("rs"))
                link(V_.scalar_tensor_tensor(dst, dst, gain_col, rsB[:, 0:nb * T].rearrange("p (a b) -> p a b", a=nb)
                                             if nb > 1 else rsB[:, 0:T], ALU.mult, ALU.mult))
                dve.sem_inc(S["rs_used"], 1)

            def rope(x, nb, tmp, tmp2):
                ps = take()
                cos, sin = C("cos"), C("sin")
                tv, t2 = tmp[:, 0:nb * T], tmp2[:, 0:nb * T]
                src = ps[:, 0:nb * T]
                if nb > 1:
                    cos, sin = b3(cos, nb), b3(sin, nb)
                    tv, t2, src = (v.rearrange("p (a b) -> p a b", a=nb) for v in (tv, t2, src))
                read(V_.tensor_tensor(tv, src, sin, ALU.mult))
                link(V_.tensor_tensor(t2, x, cos, ALU.mult))
                link(V_.tensor_tensor(x, tv, t2, ALU.add))

            def attention(groups, sc, pr, scale, mask, mem=False, sink=None):
                width = [P * (t + 1) for t in range(NT)] if not mem else [T, T]
                nm, rsum, es, rr = tiny[:, 0:4], tiny[:, 4:8], tiny[:, 8:12], tiny[:, 12:16]

                def scaled(g):
                    t, h = groups[g]
                    wd, b = width[t], g % 2
                    ps = take()
                    src = ps[:, 0:2 * wd].rearrange("p (a b) -> p a b", a=2)
                    dst = sc[:, b, 0:2 * wd].rearrange("p (a b) -> p a b", a=2)
                    if mask is None:
                        read(V_.tensor_scalar(dst, src, scale, None, ALU.mult))
                    else:
                        read(V_.scalar_tensor_tensor(dst, src, scale, b3(mask(t), 2), ALU.mult, ALU.add))
                    link(V_.tensor_reduce(nm[:, 2 * b:2 * b + 2], dst, AX, ALU.max, negate=True))
                    if sink is not None:
                        for j in range(2):
                            sk = bbc[:, 36 + 8 * sink + h + 2 * j:37 + 8 * sink + h + 2 * j]
                            link(V_.tensor_scalar(rr[:, 2 * b + j:2 * b + j + 1], sk, -1.0, None, ALU.mult))
                            link(V_.tensor_tensor(nm[:, 2 * b + j:2 * b + j + 1], nm[:, 2 * b + j:2 * b + j + 1],
                                                  rr[:, 2 * b + j:2 * b + j + 1], ALU.min))
                    dve.sem_inc(S["att_max"], 1)

                def probabilities(g):
                    wd, b = width[groups[g][0]], g % 2
                    dve.wait_ge(S["att_exp"], w("att_exp"))
                    if sink is not None:
                        link(V_.tensor_tensor(rsum[:, 2 * b:2 * b + 2], rsum[:, 2 * b:2 * b + 2],
                                              es[:, 2 * b:2 * b + 2], ALU.add))
                    link(V_.reciprocal(rr[:, 2 * b:2 * b + 2], rsum[:, 2 * b:2 * b + 2]))
                    for j in range(2):
                        p = pr[:, b, j * wd:(j + 1) * wd]
                        step(V_.tensor_scalar(p, p, rr[:, 2 * b + j:2 * b + j + 1], None, ALU.mult))
                    later()
                    dve.sem_inc(S["att_p"], 1)
                return scaled, probabilities

            def attend(groups, *args, **kw):
                scaled, probabilities = attention(groups, *args, **kw)
                for g in range(len(groups) + 1):
                    if g < len(groups):
                        scaled(g)
                    if g:
                        probabilities(g - 1)

            def glu(at, turns, tail, moe, gate):
                mine = (0,) if moe else (0, 1)

                A1, A2 = 4, 5

                def ada_ops(k0, k1, u):
                    for kc in range(k0, k1):
                        acc = M["ada_acc"][:, u, :]
                        if kc == 0:
                            dve.wait_ge(S[f"ada_in{u}"], w(f"ada_in{u}", 16))
                            ins = V_.tensor_scalar(acc, ada_in[u][:, 0, :], c_act[:, 0:1], None, ALU.mult)
                        else:
                            ins = V_.scalar_tensor_tensor(acc, ada_in[u][:, kc, :], c_act[:, kc:kc + 1], acc,
                                                          ALU.mult, ALU.add)
                        ins.then_inc(S["ada_step"], 1)
                        dve.wait_ge(S["ada_step"], w("ada_step"))

                def eye_col(e):
                    return const[0:N_EXP, bass.ds(CW["eye"][0] + e, 1)]

                def select(e, u):
                    V_.tensor_scalar(sel[0:N_EXP, u, :], combT[0:N_EXP, :], eye_col(e), None, ALU.mult)\
                        .then_inc(S["sel"], 1)

                def unit(i, u, pos, more):
                    for j in range(2):
                        dve.wait_ge(S["silu_ready"], w("silu_ready"))
                        if moe:
                            if j == 0:
                                dve.wait_ge(S["comb_done"], w("comb_done"))
                            V_.tensor_tensor(silu[:, j, :], silu[:, j, :], bank[2][:, 0:T], ALU.mult)\
                                .then_inc(S["gut"], 1)
                            dve.wait_ge(S["gut"], w("gut"))
                        V_.tensor_tensor(gu[:, j, :], silu[:, j, :], bank[j][:, T:2 * T], ALU.mult)\
                            .then_inc(S["gut"], 1)
                        dve.wait_ge(S["gut"], w("gut"))
                        V_.tensor_copy(gu_hi[:, j, :], gu[:, j, :]).then_inc(S["gut"], 1)
                        dve.wait_ge(S["gut"], w("gut"))
                        V_.tensor_tensor(gu_lo[:, j, :], gu[:, j, :], gu_hi[:, j, :].bitcast(F), ALU.subtract)\
                            .then_inc(S["gu_ready"], 1)
                        if more and j in mine:
                            split_low(j, pos + j)
                        if moe and more and j == 0:
                            select(i * 2 + u + 1, 1 - u)
                        if moe and u == 1 and j == 0:
                            ada_ops(A1, A2, 1)
                    if moe:
                        if u == 0:
                            ada_ops(0, KD, 0)
                            ada_ops(0, A1, 1)
                        else:
                            ada_ops(A2, KD, 1)
                            dve.sem_inc(S["ada_done"], 1)
                            dve.wait_ge(S["ada_sum"], w("ada_sum"))
                            V_.tensor_tensor(ada[:, bass.ds(i * 9, 9)], bank[3][:, 0:9], b_ada[:, bass.ds(i * 9, 9)],
                                             ALU.add).then_inc(S["ada_ready"], 1)

                loop = turns if tail else turns - 1
                if moe:
                    select(0, 0)
                with dve.Fori(0, loop) as i:
                    w.enter(i, {"silu_ready": 4, "gut": 12 if moe else 8, "comb_done": 2, "ada_in0": 16, "ada_in1": 16, "ada_step": 16,
                                "ada_sum": 1, "hi0_ready": 2, "hi1_ready": 2})
                    for u in range(2):
                        unit(i, u, at + 3 * (u + 1), True)
                    w.leave(loop)
                if tail:
                    unit(turns, 0, 0, False)
                else:
                    unit(turns - 1, 0, at + 3, True)
                    unit(turns - 1, 1, 0, False)
                dve.wait_ge(S["down_done"], w("down_done", 2 * turns + tail))
                if moe:
                    dve.wait_ge(S["ada_ready"], turns)
                for d in range(KD):
                    ps = bank[4 + d // 2][:, (d % 2) * T:(d % 2 + 1) * T]
                    if gate is None:
                        ins = V_.tensor_tensor(xT[:, d, :], xT[:, d, :], ps, ALU.add)
                    else:
                        ins = V_.scalar_tensor_tensor(xT[:, d, :], ps, gate(d), xT[:, d, :], ALU.mult, ALU.add)
                    ins.then_inc(S["x_ready"], 1)
                dve.wait_ge(S["x_ready"], w("x_ready", KD))

            def zero_operand():
                link(V_.memset(lnt[:, :], 0.0))
                dve.sem_inc(S["zero"], 1)

            dve.wait_ge(S["params"], w("params"))
            link(V_.memset(B1["u"][:, :, 0:30], 0.0))
            norm(xT, lambda j: col("g_mix", j), hT)
            norm(memT, lambda j: col("g_mem", j), B1["memh"], "memh")
            dve.sem_inc(S["memh_all"], 1)
            dve.wait_ge(S["const_more"], w("const_more", 16))
            scale_rs(B1["ki"], col("g_idx_k"), 1)
            dve.sem_inc(S["ki_normed"], 1)
            for x in range(2):
                rope(B1["qi"][:, 2 * x:2 * x + 2, :], 2, B1["tmp"], B1["tmp2"])
            rope(B1["ki"], 1, B1["tmp"], B1["tmp2"])
            dve.sem_inc(S["idx_roped"], 1)
            for x in range(2):
                scale_rs(B1["qa"][:, 2 * x:2 * x + 2, :], col("g_qa"), 2)
            scale_rs(B1["ka"], col("g_ka"), 1)
            dve.sem_inc(S["qka_normed"], 1)
            for g, (t, h) in enumerate(GROUPS):
                wd = P * (t + 1)
                dve.wait_ge(S["rl_ready"], w("rl_ready"))
                for j in range(2):
                    wcol = B1["wi"][:, t, h + 2 * j:h + 2 * j + 1]
                    src, dst = B1["rl"][:, g % 2, j, 0:wd], B1["score"][:, t, 0:wd]
                    if h == 0 and j == 0:
                        link(V_.tensor_scalar(dst, src, wcol, None, ALU.mult))
                    else:
                        link(V_.scalar_tensor_tensor(dst, src, wcol, dst, ALU.mult, ALU.add))
                dve.sem_inc(S["rl_used"], 1)
            for x in range(2):
                rope(B1["qa"][:, 2 * x:2 * x + 2, :], 2, B1["tmp"], B1["tmp2"])
            dve.sem_inc(S["qa_roped"], 1)
            rope(B1["ka"], 1, B1["tmp"], B1["tmp2"])
            dve.sem_inc(S["ka_roped"], 1)
            for t in range(NT):
                wd = P * (t + 1)
                pick = B1["pick"][:, t, 0:wd]
                link(V_.tensor_tensor(pick, B1["score"][:, t, 0:wd], C(f"causal{t}"), ALU.add))
                for r in range(TOPK // 8):
                    link(V_.max(tiny[:, 16:24], pick))
                    link(V_.match_replace(pick, tiny[:, 16:24], pick, PAD))
                link(V_.tensor_scalar(pick, pick, PAD, 1.0, ALU.is_equal, ALU.subtract))
                link(V_.scalar_tensor_tensor(B1["amask"][:, t, 0:wd], pick, -NEG, C(f"causal{t}"),
                                             ALU.mult, ALU.add))
            dve.sem_inc(S["dsa_mask"], 1)
            dve.wait_ge(S["params_more"], w("params_more"))
            dve.wait_ge(S["glu_in"], w("glu_in"))
            link(V_.tensor_tensor(B1["u"][:, :, 30:30 + T], B1["u"][:, :, 30:30 + T], B1["ug"], ALU.mult))
            for k in range(TAPS):
                if k == TAPS_FIRST:
                    later()
                    for x in range(4):
                        nm = "qm" if x < 2 else "km"
                        scale_rs(B1[nm][:, 2 * (x % 2):2 * (x % 2) + 2, :], col("g_qm" if x < 2 else "g_km"), 2)
                    dve.sem_inc(S["qkm_normed"], 1)
                for c in range(4):
                    src, tap = B1["u"][:, c, k:k + T], taps[:, k * 4 + c:k * 4 + c + 1]
                    if k == 0:
                        step(V_.tensor_scalar(B1["y"][:, c, :], src, tap, col("conv_b", c), ALU.mult, ALU.add))
                    else:
                        later(3)
                        step(V_.scalar_tensor_tensor(B1["y"][:, c, :], src, tap, B1["y"][:, c, :],
                                                     ALU.mult, ALU.add))
            later()
            dve.sem_inc(S["conv_y"], 1)
            ps = take()
            for c in range(4):
                ins = V_.scalar_tensor_tensor(B1["y"][:, c, :], ps[:, 0:T], -1.0 / 512, B1["y"][:, c, :],
                                              ALU.mult, ALU.add)
                if c < 3:
                    step(ins)
            later()
            read(ins)
            dve.sem_inc(S["yc_ready"], 1)
            dve.wait_ge(S["rs"], w("rs"))
            for c in range(4):
                step(V_.scalar_tensor_tensor(B1["y"][:, c, :], B1["y"][:, c, :], col("ln_g", c), rsB[:, 0:T],
                                             ALU.mult, ALU.mult))
            later()
            dve.sem_inc(S["rs_used"], 1)
            dve.sem_inc(S["yn_ready"], 1)
            def merge(br, d):
                ps = take()
                g = B1["gate"][:, br * KD + d, :]
                if br == 1:
                    read(V_.tensor_tensor(B1["merged"][:, d, :], g, ps[:, 0:T], ALU.mult))
                else:
                    read(V_.tensor_tensor(B1["tmp"][:, 0:T], g, ps[:, 0:T], ALU.mult))
                    link(V_.tensor_tensor(B1["merged"][:, d, :], B1["merged"][:, d, :], B1["tmp"][:, 0:T],
                                          ALU.add))
            own = attention(GROUPS, B1["sc"], B1["pr"], 64 ** -0.5, lambda t: B1["amask"][:, t, 0:P * (t + 1)])
            mem = attention(MEM_GROUPS, B1["sc"], B1["pr"], P ** -0.5, None, mem=True)
            both = [(own, g) for g in range(len(GROUPS))] + [(mem, g) for g in range(len(MEM_GROUPS))]
            for i in range(len(both) + 1):
                if i < len(both):
                    (scaled, _), g = both[i]
                    scaled(g)
                if i:
                    (_, probabilities), g = both[i - 1]
                    probabilities(g)
                for d in fillers(i):
                    merge(1 if i <= len(GROUPS) else 0, d)
            for d in range(KD):
                merge(2, d)
            dve.sem_inc(S["merged"], 1)

            def residual(gate):
                for d in range(KD):
                    ps = take()
                    if gate is None:
                        read(V_.tensor_tensor(xT[:, d, :], xT[:, d, :], ps[:, 0:T], ALU.add))
                    else:
                        read(V_.scalar_tensor_tensor(xT[:, d, :], ps[:, 0:T], gate(d), xT[:, d, :],
                                                     ALU.mult, ALU.add))
                    dve.sem_inc(S["x_ready"], 1)
                w("x_ready", KD)
            residual(None)
            at = starts.pop(0)
            split_low(0, at)
            norm(xT, lambda j: col("g_ffn", j), hT)
            split_h()

            ps = take()
            for t in range(NT):
                link(V_.memset(route("gpad", t, 16), PAD))
                link(V_.memset(route("epad", t, 48), PAD))
                link(V_.memset(route("list1", t, 8), PAD))
                link(V_.memset(route("list2", t, 8), PAD))
                ins = V_.tensor_tensor(route("lg", t, 36), ps[:, t * 64:t * 64 + 36], bbc[:, 0:36], ALU.add)
                if t == 0:
                    link(ins)
            read(ins)
            for t in range(NT):
                r = lambda nm, n, t=t: route(nm, t, n)
                link(V_.tensor_copy(r("gpad", 4), r("lg", 4)))
                link(V_.max(r("g8", 8), r("gpad", 16)))
                link(V_.tensor_copy(r("list1", 1), r("g8", 1)))
                link(V_.tensor_scalar(r("ngmax", 1), r("g8", 1), -1.0, None, ALU.mult))
            dve.sem_inc(S["router_max"], 1)
            for t in range(NT):
                r = lambda nm, n, t=t: route(nm, t, n)
                link(V_.match_replace(r("gpad", 16), r("list1", 8), r("gpad", 16), TAKEN1))
                link(V_.tensor_scalar(r("goh", 4), r("gpad", 4), TAKEN1, None, ALU.is_equal))
                link(V_.tensor_scalar(r("gneg", 4), r("goh", 4), 1.0, -NEG, ALU.subtract, ALU.mult))
                e = r("epad", 32).rearrange("p (g e) -> p g e", g=N_GROUP)
                lg = route("lg", t, 36)[:, 4:36].rearrange("p (g e) -> p g e", g=N_GROUP)
                wide = lambda v: v.unsqueeze(2).to_broadcast([P, N_GROUP, PER_GROUP])
                link(V_.tensor_tensor(e, lg, wide(r("goh", 4)), ALU.mult))
                link(V_.tensor_tensor(e, e, wide(r("gneg", 4)), ALU.add))
                link(V_.max(r("e8", 8), r("epad", 48)))
                link(V_.tensor_scalar(r("nv1", 1), r("e8", 1), -1.0, None, ALU.mult))
            dve.sem_inc(S["router_top2"], 1)
            dve.wait_ge(S["router_exp"], w("router_exp", 2))
            for t in range(NT):
                r = lambda nm, n, t=t: route(nm, t, n)
                link(V_.tensor_copy(r("list1", 1), r("e8", 1)))
                link(V_.tensor_copy(r("list2", 1), route("e8", t, 8)[:, 1:2]))
                link(V_.match_replace(r("epad", 48), r("list1", 8), r("epad", 48), TAKEN1))
                link(V_.match_replace(r("epad", 48), r("list2", 8), r("epad", 48), TAKEN2))
                link(V_.tensor_scalar(r("d", 1), r("e21", 1), 1.0, r("gsum", 1), ALU.add, ALU.mult))
                link(V_.reciprocal(r("w1", 1), r("d", 1)))
                link(V_.tensor_tensor(r("w2", 1), r("w1", 1), r("e21", 1), ALU.mult))
                comb = tiny[:, 96 + t * N_EXP:96 + (t + 1) * N_EXP]
                link(V_.tensor_scalar(comb, r("epad", 32), TAKEN1, r("w1", 1), ALU.is_equal, ALU.mult))
                link(V_.tensor_scalar(r("epad", 32), r("epad", 32), TAKEN2, r("w2", 1), ALU.is_equal, ALU.mult))
                link(V_.tensor_tensor(comb, comb, r("epad", 32), ALU.add))
            dve.sem_inc(S["comb_ready"], 1)
            ps = take()
            read(V_.tensor_copy(combT[0:N_EXP, :], ps[0:N_EXP, 0:T]))
            dve.wait_ge(S["c_act"], w("c_act"))
            zero_operand()
            glu(at, N_EXP // 2, 0, True, None)
            w("hi1_ready", N_EXP)

            _, _, n2 = par_at("g_ffn1_2", 0)
            for l in range(LAYERS):
                at = 72 * l
                for s, name in enumerate(("g_ffn1_2", "g_mix_2", "g_ffn2_2")):
                    tile, ga, _ = par_at(name, l)
                    link(V_.scalar_tensor_tensor(modg[:, l * 6 + s, :], ada[:, at + (3 * s + 1) * 8:at + (3 * s + 2) * 8],
                                                 1.0, tile[:, ga:ga + 8], ALU.add, ALU.mult))
                    f = 1.0 if s == 1 else 0.5
                    link(V_.tensor_scalar(modg[:, l * 6 + 3 + s, :], ada[:, at + (3 * s + 2) * 8:at + (3 * s + 3) * 8],
                                          1.0, f, ALU.add, ALU.mult))

            for l in range(LAYERS):
                V = B2
                gain = lambda s, l=l: (lambda j: modg[:, l * 6 + s, j:j + 1])
                shift = lambda s, l=l: (lambda j: ada[:, 72 * l + 3 * s * 8 + j:72 * l + 3 * s * 8 + j + 1])
                gate = lambda s, l=l: (lambda j: modg[:, l * 6 + 3 + s, j:j + 1])

                def flat(nm):
                    return V[nm].rearrange("p a b -> p (a b)")
                at = starts.pop(0)
                split_low(0, at)
                split_low(1, at + 1)
                norm(xT, gain(0), hT, bias=shift(0))
                zero_operand()
                split_h()
                glu(at, 5, 1, False, gate(0))
                norm(xT, gain(1), hT, bias=shift(1))
                link(V_.memset(V["praw"][:, :, 0:1], 0.0))
                link(V_.memset(V["cu"][:, :, 0:2], 0.0))
                link(V_.memset(flat("state"), 0.0))
                dve.sem_inc(S["state_ready"], 1)
                dve.wait_ge(S["praw_ready"], w("praw_ready"))
                link(V_.tensor_tensor(V["ysh"], V["praw"][:, :, 0:T], V["praw"][:, :, 1:1 + T], ALU.subtract))
                for b in (6, 7, 2, 3, 0, 1, 4, 5):
                    step(V_.scalar_tensor_tensor(V["pm"][:, b, :], V["ysh"][:, b, :], col("rwkv_mu_2", b, l),
                                                 V["praw"][:, b, 1:1 + T], ALU.mult, ALU.add))
                later()
                dve.sem_inc(S["pm_ready"], 1)
                r_, k_, v_ = V["pm"][:, 0:2, :], V["pm"][:, 2:4, :], V["pm"][:, 4:6, :]
                for c in range(2):
                    step(V_.tensor_scalar(V["kk"][:, c, :], k_[:, c, :], col("rwkv_k_k_2", c, l), None, ALU.mult))
                later()
                dve.sem_inc(S["kk_raw"], 1)
                dve.wait_ge(S["sw_ready"], w("sw_ready"))
                for c in range(2):
                    step(V_.tensor_tensor_scan(V["cs"][:, c, :], C("reset"), V["sw"][:, c, :], 0.0, ALU.mult, ALU.add))
                later()
                link(V_.tensor_tensor(flat("csp"), flat("cs"), flat("sw"), ALU.subtract))
                dve.sem_inc(S["cs_ready"], 1)
                ps = take()
                read(V_.tensor_scalar(rsB[:, :], ps[:, :], 1e-24, float(2 ** KK_SHIFT), ALU.max, ALU.mult))
                dve.sem_inc(S["kk_sum"], 1)
                for c in range(2):
                    step(V_.tensor_scalar(V["ysh"][:, 2 + c, :], V["aa"][:, c, :], 1.0, col("rwkv_k_a_2", c, l),
                                          ALU.subtract, ALU.mult))
                later()
                link(V_.scalar_tensor_tensor(k_, V["ysh"][:, 2:4, :], 1.0, k_, ALU.add, ALU.mult))
                for c in range(2):
                    step(V_.scalar_tensor_tensor(V["ysh"][:, c, :], r_[:, c, :], col("rwkv_r_k_2", c, l),
                                                 k_[:, c, :], ALU.mult, ALU.mult))
                later()
                dve.sem_inc(S["bonus_in"], 1)
                dve.wait_ge(S["rs"], w("rs"))
                link(V_.tensor_tensor(flat("kk"), flat("kk"), rsB[:, :], ALU.mult))
                dve.sem_inc(S["rs_used"], 1)
                dve.wait_ge(S["w_ready"], w("w_ready"))
                step(V_.tensor_tensor(flat("al"), flat("kk"), flat("Wprev"), ALU.mult))
                step(V_.tensor_tensor(flat("csp"), flat("kk"), flat("aa"), ALU.mult))
                step(V_.tensor_tensor(V["kap"], k_, V["Winv"], ALU.mult))
                step(V_.tensor_tensor(V["rho"], r_, V["W"], ALU.mult))
                later(2)
                step(V_.tensor_tensor(flat("be"), flat("csp"), flat("Winv"), ALU.mult))
                for c in range(2):
                    for c4 in range(4):
                        step(V_.tensor_copy(tiny[:, 24 + c * 4 + c4:25 + c * 4 + c4],
                                            V["W"][:, c, (c4 + 1) * CHUNK - 1:(c4 + 1) * CHUNK]))
                later()
                dve.sem_inc(S["rwkv_in"], 1)
                for x in range(3):
                    dst = V["q"][:, 2 * x:2 * x + 2, :] if x < 2 else V["k"]
                    scale_rs(dst, col("att_q_gain_2" if x < 2 else "att_k_gain_2", 0, l), 2 if x < 2 else 1)
                dve.sem_inc(S["att_normed"], 1)
                ps = take()
                read(V_.tensor_tensor(flat("bon"), ps[:, :], v_.rearrange("p a b -> p (a b)"), ALU.mult))
                for dst, mask in (("AT", "strict"), ("BT", "strict"), ("C1T", "incl"), ("C2T", "incl")):
                    for g in range(2):
                        ps = take()
                        read(V_.tensor_tensor(V[dst][:, g, :].rearrange("p (a b) -> p a b", a=4),
                                              ps[:, :].rearrange("p (a b) -> p a b", a=4), b3(C(mask), 4), ALU.mult))
                        if dst == "AT":
                            for o in ("Tm", "TT"):
                                step(V_.tensor_copy(V[o][:, g, :].rearrange("p (a b) -> p a b", a=4), b3(C("eye"), 4)))
                            link(V_.tensor_tensor(V["off"][:, g, :].rearrange("p (a b) -> p a b", a=4),
                                                  V["AT"][:, g, :].rearrange("p (a b) -> p a b", a=4),
                                                  b3(C("level0"), 4), ALU.mult))
                            dve.sem_inc(S["off_ready"], 1)
                scaled, probabilities = attention(GROUPS, V["sc"], V["pr"], 64 ** -0.5,
                                                  lambda t: C("causal0") if t == 0 else C("window1"), sink=l)
                for lev in range(6):
                    scaled(lev)
                    for g in range(2):
                        if lev < 5:
                            ps = take()
                            read(V_.tensor_tensor(V["Tm"][:, g, :], V["Tm"][:, g, :], ps[:, :], ALU.subtract))
                        ps = take()
                        read(V_.tensor_tensor(V["TT"][:, g, :], V["TT"][:, g, :], ps[:, :], ALU.subtract))
                        if lev < 5:
                            link(V_.tensor_tensor(V["off"][:, g, :].rearrange("p (a b) -> p a b", a=4),
                                                  V["AT"][:, g, :].rearrange("p (a b) -> p a b", a=4),
                                                  b3(C(f"level{lev + 1}"), 4), ALU.mult))
                            dve.sem_inc(S["off_ready"], 1)
                    if lev == 5:
                        dve.sem_inc(S["solve_ready"], 1)
                    probabilities(lev)
                for c4 in range(4):
                    t, r0 = c4 // 2, (c4 % 2) * CHUNK
                    if 6 + c4 < len(GROUPS):
                        scaled(6 + c4)
                    ps = take()
                    read(V_.tensor_scalar(V["negU"][r0:r0 + CHUNK, t, :], ps[r0:r0 + CHUNK, 0:T], -1.0, None, ALU.mult))
                    dve.sem_inc(S["u_ready"], 1)
                    if c4 < 3:
                        ps = take()
                        read(V_.tensor_tensor(flat("state"), ps[:, 0:T], flat("state"), ALU.add))
                        for c in range(2):
                            step(V_.scalar_tensor_tensor(V["state"][:, c, :], V["state"][:, c, :],
                                                         tiny[:, 24 + c * 4 + c4:25 + c * 4 + c4], C("half"),
                                                         ALU.mult, ALU.mult))
                        later()
                        dve.sem_inc(S["state_ready"], 1)
                    if 6 + c4 < len(GROUPS):
                        probabilities(6 + c4)
                dve.wait_ge(S["sconv_in"], w("sconv_in"))
                link(V_.tensor_tensor(V["cu"][:, :, 2:2 + T], V["cc"], V["ch"], ALU.mult))
                for k in range(3):
                    for c in range(2):
                        src, tap = V["cu"][:, c, k:k + T], col("conv_w_2", 2 * k + c, l)
                        if k == 0:
                            step(V_.tensor_scalar(V["cy"][:, c, :], src, tap, None, ALU.mult))
                        else:
                            later(1)
                            step(V_.scalar_tensor_tensor(V["cy"][:, c, :], src, tap, V["cy"][:, c, :],
                                                         ALU.mult, ALU.add))
                later()
                link(V_.tensor_tensor(flat("cy"), flat("cy"), flat("cb"), ALU.mult))
                dve.sem_inc(S["conv_ready"], 1)
                dve.wait_ge(S["y_done"], w("y_done"))
                link(V_.tensor_copy(flat("W"), bank[7][:, :]))
                dve.sem_inc(S["y_ready"], 1)
                ps = take()
                read(V_.scalar_tensor_tensor(flat("W"), ps[:, :], -1.0 / 64, flat("W"), ALU.mult, ALU.add))
                dve.sem_inc(S["yc_ready"], 1)
                dve.wait_ge(S["rs"], w("rs"))
                for c in range(2):
                    step(V_.scalar_tensor_tensor(V["W"][:, c, :], V["W"][:, c, :], col("rwkv_gn_w_2", c, l),
                                                 rsB[:, c * T:(c + 1) * T], ALU.mult, ALU.mult))
                later()
                dve.sem_inc(S["rs_used"], 1)
                for c in range(2):
                    step(V_.scalar_tensor_tensor(V["W"][:, c, :], V["W"][:, c, :], col("rwkv_gn_b_2", c, l),
                                                 V["bon"][:, c, :], ALU.add, ALU.add))
                later()
                link(V_.tensor_tensor(flat("yr"), flat("W"), flat("gB"), ALU.mult))
                dve.sem_inc(S["mix_ready"], 1)
                residual(gate(1))
                at = starts.pop(0)
                split_low(0, at)
                split_low(1, at + 1)
                norm(xT, gain(2), hT, bias=shift(2))
                zero_operand()
                split_h()
                glu(at, 5, 1, False, gate(2))
            for i in range(KD):
                dve.sem_inc(S["x_ready_pe"], 1)

        @block.sync
        def _(sp):
            w = Seen()
            n_slab = [0]

            def before(n):
                if n >= SLOTS:
                    name, k = slab_end[n - SLOTS]
                    sp.wait_ge(S[name], k)

            def load(src, view=None, first=True):
                n = n_slab[0]
                if first:
                    before(n)
                dst = slab[n % SLOTS]
                sp.dma_start(view(dst) if view else dst[:, :], src).then_inc(S[f"slab{n % SLOTS}_in"], 16)

            def done():
                n_slab[0] += 1

            def matrix(src, c0, cols, kc=KD, width=None):
                width = SLAB // kc
                for c in range(0, cols, width):
                    load(src[:, c0 + c:c0 + c + width].rearrange("(k p) c -> p k c", p=P),
                         lambda d: d[:, :].rearrange("p (k c) -> p k c", k=kc))
                    done()

            def glu_loads(w_up, w_down, f0, half, slot, waits):
                for x in range(3):
                    s = (slot + x) % SLOTS
                    if waits:
                        sp.wait_ge(S[waits[x][0]], waits[x][1])
                    if x < 2:
                        for ab in range(2):
                            src = w_up(ab * half, f0 + x * P)
                            dst = slab[s][:, :].rearrange("p (k c) -> p k c", k=KD)[:, :, ab * P:(ab + 1) * P]
                            sp.dma_start(dst, src).then_inc(S[f"slab{s}_in"], 16)
                    else:
                        sp.dma_start(slab[s][:, :].rearrange("p (j d) -> p j d", j=2), w_down(f0))\
                            .then_inc(S[f"slab{s}_in"], 16)

            def glu(turns, tail, up, down, half):
                n0 = n_slab[0]
                for u in range(2):
                    n = n0 + 3 * u
                    glu_loads(lambda ab, f, u=u: up(0, u, ab, f), lambda f, u=u: down(0, u, f), 0, half, n,
                              [slab_end[n + x - SLOTS] for x in range(3)])
                with sp.Fori(1, turns) as i:
                    for u in range(2):
                        n = n0 + 3 * u
                        waits = [(slab_end[n + x][0], (i - 1) * 2 + slab_end[n + x][1])
                                 for x in range(3)]
                        glu_loads(lambda ab, f, u=u: up(i, u, ab, f), lambda f, u=u: down(i, u, f), 0, half, n, waits)
                n_slab[0] += 6 * turns
                for u in range(tail):
                    n = n_slab[0]
                    glu_loads(lambda ab, f, u=u: up(turns, u, ab, f), lambda f, u=u: down(turns, u, f), 0, half, n,
                              [slab_end[n + x - SLOTS] for x in range(3)])
                    n_slab[0] += 3

            first_c = CW["half"][0]
            sp.dma_start(const[:, 0:first_c], a["const"][:, 0:first_c]).then_inc(S["const_in"], 16)
            sp.dma_start(xin, a["x"][0].rearrange("(t p) d -> p t d", p=P)).then_inc(S["x_in"], 16)
            w_in = a["w_in"][0]
            matrix(w_in, 768, 512)
            sp.dma_start(memin, a["mem"][0].rearrange("(t p) d -> p t d", p=P)).then_inc(S["mem_in"], 16)
            for x, (c0, cn, d0) in enumerate(((1280, 64, 0), (1280, 64, 64), (1344, 8, 128))):
                load(w_in[:, c0:c0 + cn].rearrange("(k p) c -> p k c", p=P),
                     lambda d, d0=d0, cn=cn: d[:, :].rearrange("p (k c) -> p k c", k=KD)[:, :, d0:d0 + cn], x == 0)
            done()
            matrix(w_in, 512, 256)
            sp.dma_start(const[:, first_c:], a["const"][:, first_c:]).then_inc(S["const_more"], 16)
            matrix(w_in, 0, 512)
            matrix(w_in, 1352, 1024)
            matrix(w_in, 2376, 512)
            matrix(a["w_mem_kv"][0], 0, 1024)
            matrix(w_in, 2888, 3072)
            for name in ("w_br_b", "w_br_a", "w_br_m"):
                matrix(a[name][0], 0, D, kc=4)
            matrix(a["w_o"][0], 0, D)

            def moe_up(i, u, ab, f):
                wv = a["w_up"][0].rearrange("e r c -> (e r) c")
                return wv[bass.ds(i * 2 * D + u * D, D), ab + f:ab + f + P].rearrange("(k p) c -> p k c", p=P)

            def moe_down(i, u, f):
                wv = a["w_down"][0].rearrange("e r c -> (e r) c")
                return wv[bass.ds(i * 512 + u * 256, 256), :].rearrange("(j p) d -> p j d", p=P)
            glu(N_EXP // 2, 0, moe_up, moe_down, 256)

            for l in range(LAYERS):
                def ffn(up_w, down_w):
                    def up(i, u, ab, f):
                        return up_w[:, bass.ds(i * 512 + (u * 256 + ab + f), P)].rearrange("(k p) c -> p k c", p=P)

                    def down(i, u, f):
                        rows_ = bass.ds(i * 512 + u * 256, 256)
                        return down_w[rows_, :].rearrange("(j p) d -> p j d", p=P)
                    glu(5, 1, up, down, D_FF)
                ffn(a["w_ffn1_in_2"][l], a["w_ffn1_out_2"][l])
                wm = a["w_mix_in_2"][l]
                matrix(wm, 768, 1024)
                matrix(wm, 0, 768)
                matrix(wm, 1792, 768)
                matrix(a["w_mix_out_2"][l], 0, D)
                ffn(a["w_ffn2_in_2"][l], a["w_ffn2_out_2"][l])

        @block.gpsimd
        def _(pool):
            w = Seen()
            for dst, src in other_rows():
                pool.dma_start(dst, src).then_inc(S["others_in"], 16)

            def split_low(x, n):
                pool.wait_ge(S[f"hi{x}_ready"], w(f"hi{x}_ready"))
                nc.gpsimd.tensor_tensor(w_lo[x][:, :], slab[n % SLOTS][:, :], w_hi[x][:, :].bitcast(F), ALU.subtract)\
                    .then_inc(S[f"lo{x}_ready"], 1)

            def glu(at, turns, moe):
                mine = (1, 2) if moe else (2,)
                for x in mine:
                    split_low(x, at + x)
                if not moe:
                    w("hi1_ready", 2 * turns + 1)
                loop = turns - 1 if moe else turns
                with pool.Fori(0, loop) as i:
                    w.enter(i, {f"hi{x}_ready": 2 for x in mine})
                    for u in range(2):
                        for x in mine:
                            split_low(x, at + 3 * (u + 1) + x)
                    w.leave(loop)
                if moe:
                    for x in mine:
                        split_low(x, at + 3 + x)

            for n, (at, _) in enumerate(glu_starts):
                glu(at, N_EXP // 2 if n == 0 else 5, n == 0)


ROW_COUNTS = [sum(n for _, n in ROWS_1), LAYERS * sum(n for _, n in ROWS_2), TAPS * 4, 72, 72]

INPUTS = ["x", "mem", "g_mix", "w_in", "b_gate", "g_qa", "g_ka", "g_idx_k", "conv_w", "conv_b", "ln_g", "ln_b",
          "g_mem", "w_mem_kv", "g_qm", "g_km", "w_br_a", "w_br_b", "w_br_m", "w_o", "g_ffn", "w_rg", "b_rg",
          "w_re", "b_re", "w_up", "w_down", "c_2", "w_ada_2", "b_ada_2", "g_ffn1_2", "w_ffn1_in_2",
          "w_ffn1_out_2", "g_mix_2", "w_mix_in_2", "w_mix_out_2", "att_q_gain_2", "att_k_gain_2",
          "att_sinks_2", "rwkv_mu_2", "rwkv_w0_2", "rwkv_w_w2_2", "rwkv_a0_2", "rwkv_a_w2_2", "rwkv_g_w2_2",
          "rwkv_k_k_2", "rwkv_k_a_2", "rwkv_r_k_2", "rwkv_gn_w_2", "rwkv_gn_b_2", "conv_w_2", "g_ffn2_2",
          "w_ffn2_in_2", "w_ffn2_out_2"]


def kernel(**inputs):
    import concourse.bacc as bacc
    from concourse.bass_utils import run_bass_kernel_spmd

    nc = bacc.Bacc("TRN2", target_bir_lowering=False, num_devices=1)
    arrays, a = {}, {}
    for name in INPUTS:
        v = np.ascontiguousarray(inputs[name])
        arrays["in_" + name] = v
        a[name] = nc.dram_tensor("in_" + name, v.shape, mybir.dt.from_np(v.dtype), kind="ExternalInput").ap()
    v = _constants()[0]
    arrays["in_const"] = v
    a["const"] = nc.dram_tensor("in_const", v.shape, mybir.dt.float32, kind="ExternalInput").ap()
    out = nc.dram_tensor("out_x", (1, T, D), mybir.dt.float32, kind="ExternalOutput").ap()
    build(nc, a, out)
    r = run_bass_kernel_spmd(nc, [arrays], core_ids=[0])
    return r.results[0]["out_x"]
```

```python
import math
from contextlib import ExitStack

import numpy as np
import concourse.bass as bass
from concourse import mybir

P = 128
D = 1024
KD = D // P
T = 256
NT = T // P
EPS = 1e-6
NEG = -1e30
PAD = -3e38
TAKEN1 = 3e38
TAKEN2 = 2e38
TOPK = 64
HEADS = 8
N_EXP = 32
N_GROUP = 4
PER_GROUP = N_EXP // N_GROUP
TAPS = 31
LAYERS = 2
D_FF = 2816
CHUNK = 64
SLOTS = 6
SLAB = 2048
RING = 7
ADA_COLS = 576
ADA_SLABS = 9 * D // ADA_COLS
DECAY_C = math.exp(-0.5)
KK_SHIFT = 24

def _constants():
    eye = np.eye(P, dtype=np.float32)
    ones = np.ones((P, P), np.float32)
    p = np.arange(P)
    half = (p[:, None] // 64 == p[None, :] // 64).astype(np.float32)
    rot = np.zeros((P, P), np.float32)
    for m in range(P):
        if m % 64 < 32:
            rot[m + 32, m] = -1.0
        else:
            rot[m - 32, m] = 1.0
    dup0 = (p[:, None] == p[None, :] % 64).astype(np.float32)
    dup1 = (p[:, None] == 64 + p[None, :] % 64).astype(np.float32)
    inv = np.float32(10000.0) ** (-np.arange(32, dtype=np.float32) / np.float32(32))
    ang = np.arange(T, dtype=np.float32)[None, :] * inv[p % 32][:, None].astype(np.float32)
    cos, sin = np.cos(ang).astype(np.float32), np.sin(ang).astype(np.float32)
    key = np.arange(T)
    causal0 = np.where(key[None, :P] <= p[:, None], 0.0, NEG).astype(np.float32)
    causal1 = np.where(key[None, :] <= P + p[:, None], 0.0, NEG).astype(np.float32)
    gap = P + p[:, None] - key[None, :]
    window1 = np.where((gap >= 0) & (gap < 128), 0.0, NEG).astype(np.float32)
    same = p[:, None] // CHUNK == p[None, :] // CHUNK
    strict = (same & (p[:, None] < p[None, :])).astype(np.float32)
    incl = (same & (p[:, None] <= p[None, :])).astype(np.float32)
    levels = []
    for m in (1, 2, 4, 8, 16, 32):
        blk = p[:, None] // (2 * m) == p[None, :] // (2 * m)
        levels.append((blk & (p[:, None] % (2 * m) < m) & (p[None, :] % (2 * m) >= m)).astype(np.float32))
    reset = np.tile((np.arange(T) % CHUNK != 0).astype(np.float32), (P, 1))
    small = np.zeros((P, 8), np.float32)
    small[:, 0] = EPS
    small[:, 1] = 64e-5
    small[:, 2] = 0.5 * KK_SHIFT * math.log(2.0)
    parts = dict(eye=eye, ones=ones, small=small, half=half, rot=rot, dup0=dup0, dup1=dup1, cos=cos,
                 sin=sin, causal0=causal0, causal1=causal1, window1=window1, strict=strict, incl=incl,
                 reset=reset, **{f"level{n}": v for n, v in enumerate(levels)})
    at, where = 0, {}
    for name, v in parts.items():
        where[name] = (at, v.shape[1])
        at += v.shape[1]
    return np.ascontiguousarray(np.concatenate(list(parts.values()), axis=1)), where


ROWS_0 = [("g_mix", 8), ("g_mem", 8)]
ROWS_1 = [("g_ffn", 8), ("b_gate", 24), ("conv_b", 4), ("ln_g", 4),
          ("ln_b", 4), ("g_qa", 1), ("g_ka", 1), ("g_idx_k", 1), ("g_qm", 1), ("g_km", 1), ("c_2", 8)]
ROWS_2 = [("g_ffn1_2", 8), ("g_mix_2", 8), ("g_ffn2_2", 8), ("att_q_gain_2", 1), ("att_k_gain_2", 1),
          ("rwkv_mu_2", 8), ("rwkv_w0_2", 2), ("rwkv_a0_2", 2), ("rwkv_k_k_2", 2), ("rwkv_k_a_2", 2),
          ("rwkv_r_k_2", 2), ("rwkv_gn_w_2", 2), ("rwkv_gn_b_2", 2), ("conv_w_2", 6)]

SEMAPHORES = {
    "const_in": "constants", "x_in": "tokens", "mem_in": "memory tokens", "rows_in": "block 1's vectors",
    "others_in": "the other small inputs", "const_more": "the other constants",
    **{f"slab{s}_in": "a weight slab in this slot" for s in range(SLOTS)},
    "ada_in0": "an even slab of w_ada", "ada_in1": "an odd one", "out_written": "the result is in DRAM",
    "for_act": "a product for ScalarE", "for_dve": "a product for VectorE",
    "read_by_act": "ScalarE has read one and written what came of it",
    "read_by_dve": "VectorE has read one and written what came of it",
    "up_done": "gate|up of 128 hidden features", "down_done": "a unit's part of the output",
    "comb_done": "an expert's combine weights on every partition", "ada_sum": "adaLN sums over partitions",
    "y_done": "the recurrence's output is complete",
    "act_step": "a step of its own chain", "params_more": "parameter columns of block 2, taps and biases", "params": "parameter columns", "c_act": "silu(c)",
    "sq": "four chunks of squares", "rs": "reciprocal norms", "ki_sq": "squares of the index key",
    "qka_sq": "squares of attention queries and key", "qkm_sq": "squares of memory queries and keys",
    "rl_ready": "rectified index logits", "glu_in": "conv value and gate", "att_exp": "exponentials and sums",
    "att_pT": "transposed probabilities", "oa_ready": "sparse attention output", "om_ready": "memory attention output",
    "swa_ready": "window attention output", "ob_ready": "conv branch output", "router_exp": "the router's exponentials",
    "silu_ready": "silu of a gate block", "praw_ready": "RWKV projections", "lora_in": "low-rank inputs",
    "sw_ready": "decay and rate sigmoids", "kk_sq": "squares of the removal key", "att_sq": "squares of q and k",
    "w_ready": "decay products", "sconv_in": "short conv inputs", "m1_ready": "first half of a doubling",
    "r_ready": "a chunk's right-hand side", "yc_sq": "squares of the centred output",
    "kdup_ready": "keys on both partition halves",
    **{f"hi{x}_ready": "the high part of slab x of a unit" for x in range(3)},
    "h_high": "the high part of a chunk of the normalised residual",
    **{f"lo{x}_ready": "the low part of slab x of a unit, and so the slab is free" for x in range(3)},
    "h_split": "both parts of a chunk of the normalised residual",
    "dve_step": "a step of its own chains", "hn": "a chunk of the normalised residual",
    "memh": "a chunk of the normalised memory", "memh_all": "all of it, its source is free",
    "rs_used": "the reciprocal norms are used", "ki_normed": "index key, normed", "idx_roped": "index queries and key",
    "qka_normed": "queries and key, normed", "rl_used": "rectified logits are used", "qa_roped": "queries, rotated",
    "ka_roped": "key, rotated", "dsa_mask": "the mask of selected keys", "qkm_normed": "memory queries and keys, normed",
    "conv_y": "convolution output", "att_max": "scaled scores and their maxima", "att_p": "probabilities",
    "yc_ready": "centred output", "yn_ready": "scaled output", "merged": "gated sum of the branches",
    "x_ready": "a chunk of the residual", "x_ready_pe": "the last residual", "router_max": "the groups' maximum",
    "router_top2": "the two best experts' logits", "comb_ready": "combine weights",
    "phi_ready": "the high part of a slab of a split projection", "plo_ready": "and its low part",
    "p_high": "the high part of block 1's h", "p_split": "and its low part",
    "comb_turned": "combine weights, an expert a row", "sel": "an expert's row of the combine weights", "gut": "silu times combine weight",
    "gu_ready": "a block of hidden activations", "ada_step": "one chunk of an adaLN slab added",
    "ada_done": "a pair of adaLN slabs added up", "ada_ready": "nine adaLN columns", "state_ready": "the recurrent state",
    "pm_ready": "token-shifted projections", "kk_raw": "removal key before its norm", "cs_ready": "summed log decays",
    "kk_sum": "its clamped squared norm", "bonus_in": "r k r_k", "rwkv_in": "the recurrence's operands",
    "att_normed": "q and k, normed", "off_ready": "off-diagonal blocks", "solve_ready": "the inverses",
    "u_ready": "a chunk's solution", "y_ready": "the output on chip", "mix_ready": "RWKV output",
    "conv_ready": "short convolution's output",
}


SHORT_FIRST, OUT_EARLY = 2, 4
FFN_UNITS = 11
CONV_SUM, CONV_VAR = 12, 16
TAPS_FIRST = 22


class Seen:

    def __init__(self):
        self.n, self.i, self.per, self.at = {}, None, {}, {}

    def __call__(self, name, k=1):
        self.n[name] = self.n.get(name, 0) + k
        if self.i is not None:
            return self.i * self.per[name] + self.n[name]
        return self.n[name]

    def enter(self, i, per):
        self.i, self.per, self.at = i, per, dict(self.n)

    def leave(self, turns):
        for name, v in self.n.items():
            grew = v - self.at.get(name, 0)
            if grew:
                assert grew == self.per[name], (name, grew, self.per[name])
                self.n[name] = self.at.get(name, 0) + grew * turns
        self.i = None


def build(nc, a, out, dbg=None):
    F = mybir.dt.float32
    ALU = mybir.AluOpType
    ACT = mybir.ActivationFunctionType
    AX = mybir.AxisListType.X
    _, CW = _constants()
    n_const = sum(w for _, w in CW.values())

    ctx = ExitStack()
    with ctx:
        def sb(name, shape):
            return ctx.enter_context(nc.sbuf_tensor(name, shape, F))

        S = {name: ctx.enter_context(nc.semaphore(name)) for name in SEMAPHORES}

        const = sb("const", [P, n_const])
        slab_at = nc.sbuf_base
        slab = [sb(f"slab{i}", [P, SLAB]) for i in range(SLOTS)]
        par0 = sb("par0", [P, sum(n for _, n in ROWS_0)])
        par1 = sb("par1", [P, sum(n for _, n in ROWS_1)])
        par2 = sb("par2", [P, LAYERS * sum(n for _, n in ROWS_2)])
        taps = sb("taps", [P, TAPS * 4])
        b_ada = sb("b_ada", [P, LAYERS * 72])
        ada = sb("ada", [P, LAYERS * 72])
        brow = sb("brow", [1, 52])
        bbc = sb("bbc", [P, 52])
        router = sb("router", [P, KD, 36])
        lora_wa = sb("lora_wa", [P, LAYERS, T])
        lora_g = sb("lora_g", [P, LAYERS, T])
        c_act = sb("c_act", [P, KD])
        modg = sb("modg", [P, LAYERS * 6, KD])
        xT = sb("xT", [P, KD, T])
        hT_at = nc.sbuf_base
        hT = sb("hT", [P, KD, T])
        sq = sb("sq", [P, KD, T])
        lnt = sb("lnt", [P, 512])
        rsB = sb("rsB", [P, 512])
        silu_at = nc.sbuf_base
        silu = sb("silu", [P, 2, T])
        gu = sb("gu", [P, 2, T])
        rows = [silu[:, 0, 0:P]] + [gu[:, n // 2, (n % 2) * P:(n % 2 + 1) * P] for n in range(4)] \
            + [silu[:, 1, 0:P]]
        sel = sb("sel", [P, 2, T])
        combT = sb("combT", [P, 2 * T])
        tiny = sb("tiny", [P, 160])
        region_n = 25700
        region_at = (nc.sbuf_base + 31) // 32 * 32
        region = sb("region", [P, region_n])
        bank = [ctx.enter_context(nc.psum_tensor(f"bank{i}", [P, 512], F)) for i in range(8)]

        def C(name, lo=0, hi=None):
            at, w = CW[name]
            return const[:, at + lo:at + (w if hi is None else hi)]

        def layout(start, **sizes):
            views, at = {}, start
            for name, shape in sizes.items():
                n = int(np.prod(shape))
                v = region[:, at:at + n]
                if len(shape) == 2:
                    v = v.rearrange("p (a b) -> p a b", a=shape[0])
                elif len(shape) == 3:
                    v = v.rearrange("p (a b c) -> p a b c", a=shape[0], b=shape[1])
                views[name] = v
                at += n
            assert at <= region_n, at
            return views

        B1 = layout(0, memh=(8, T), qi=(4, T), ki=(T,), wi=(NT, 8), ka=(T,), kdup=(2, T), va=(NT, P), qa=(4, T),
                    u=(4, 30 + T), ug=(4, T), y=(4, T), qm=(4, T), km=(4, T), vm=(NT, 512),
                    gate=(24, T), oa=(4, T), amask=(NT, T), score=(NT, T), pick=(NT, T),
                    pT=(2, 512), sc=(2, 512), pr=(2, 512), tmp=(512,), tmp2=(512,))
        B1["om"], B1["ob"], B1["merged"] = B1["qi"], B1["ug"], B1["memh"]
        B1["rl"] = B1["sc"].rearrange("p a (b c) -> p a b c", b=2)
        xin = B1["gate"][:, 0:8, :].rearrange("p a b -> p (a b)").rearrange("p (t d) -> p t d", t=NT)
        memin = B1["gate"][:, 8:16, :].rearrange("p a b -> p (a b)").rearrange("p (t d) -> p t d", t=NT)
        memT = B1["gate"][:, 16:24, :]
        M = layout(0, ada_in=(KD, ADA_COLS), ada_acc=(2, ADA_COLS))
        assert KD * ADA_COLS <= 2 * KD * T + 512
        ada_in = (M["ada_in"], nc.alloc_sbuf_tensor_at("ada_odd", [P, KD, ADA_COLS], F, offset=hT_at)[:, :, :])
        FR = mybir.dt.float32r
        split_at = [region_at + 4 * (KD + 2) * ADA_COLS]

        def split(name, shape):
            t = nc.alloc_sbuf_tensor_at(name, [P, *shape], FR, offset=split_at[0])
            split_at[0] += 4 * int(np.prod(shape))
            assert split_at[0] <= region_at + 4 * region_n
            return t
        w_hi = [split(f"w_hi{x}", [SLAB]) for x in range(3)]
        w_lo = [split(f"w_lo{x}", [SLAB]) for x in range(3)]
        h_hi, h_lo = split("h_hi", [KD, T]), split("h_lo", [KD, T])
        gu_hi, gu_lo = split("gu_hi", [2, T]), split("gu_lo", [2, T])

        def parts_at(name, shape, offset):
            return nc.alloc_sbuf_tensor_at(name, [P, *shape], FR, offset=offset)

        def over(name, view, shape=(SLAB,)):
            return parts_at(name, shape, region_at + 4 * (view.offset - region[:, 0:1].offset))
        slab_low = [parts_at(f"slab_low{n}", [SLAB], slab_at + 4 * SLAB * n) for n in range(SLOTS)]
        early_hi = [over("early_hi0", B1["gate"][:, 0:8, :]), over("early_hi1", B1["gate"][:, 8:16, :]),
                    over("early_hi2", B1["gate"][:, 16:24, :])]
        gates_hi = [over("gates_hi0", B1["sc"]), over("gates_hi1", B1["score"]),
                    over("gates_hi2", B1["memh"])]
        p_hi = parts_at("p_hi", [KD, T], silu_at)
        p_lo = parts_at("p_lo", [KD, T], hT_at)
        B2 = layout(0, q=(4, T), k=(T,), kdup=(2, T), v=(NT, P), o=(4, T), praw=(8, 1 + T), cs=(2, T),
                    pm=(8, T), W=(2, T), gB=(2, T), sw=(2, T), csp=(2, T), Winv=(2, T), Wprev=(2, T), aa=(2, T),
                    kk=(2, T), al=(2, T), be=(2, T), kap=(2, T), rho=(2, T), bon=(2, T),
                    ysh=(8, T), AT=(2, 512), BT=(2, 512), Tm=(2, 512), TT=(2, 512), off=(2, 512),
                    M1=(2, 512), R=(T,), state=(2, P), cb=(2, T), cc=(2, T), ch=(2, T), cu=(2, 2 + T),
                    cy=(2, T))
        for n, name in enumerate(("vt", "bt", "kt", "negU")):
            B2[name] = B2["ysh"][:, 2 * n:2 * n + 2, :]
        flat_praw = B2["praw"].rearrange("p a b -> p (a b)")
        B2["C1T"] = flat_praw[:, 0:1024].rearrange("p (a b) -> p a b", a=2)
        B2["C2T"] = flat_praw[:, 1024:2048].rearrange("p (a b) -> p a b", a=2)
        decays = B2["sw"].offset - region[:, 0:1].offset
        for n, name in enumerate(("sc", "pr", "pT")):
            B2[name] = region[:, decays + n * 1024:decays + (n + 1) * 1024].rearrange("p (a b) -> p a b", a=2)
        B2["th"], B2["yr"] = B2["R"], B2["cs"]
        mix_hi = [over("mix_hi0", B2["AT"]), over("mix_hi1", B2["Tm"]), over("mix_hi2", B2["csp"])]
        m_hi = over("m_hi", B2["off"], (KD, T))
        m_lo = over("m_lo", B2["al"], (KD, T))

        def par_at(name, layer=None):
            spec, tile = (ROWS_1, par1) if layer is None else (ROWS_2, par2)
            if layer is None and name in dict(ROWS_0):
                spec, tile = ROWS_0, par0
            at = 0 if layer is None else layer * sum(n for _, n in ROWS_2)
            for nm, n in spec:
                if nm == name:
                    return tile, at, n
                at += n
            raise KeyError(name)

        def col(name, j=0, layer=None):
            tile, at, _ = par_at(name, layer)
            return tile[:, at + j:at + j + 1]

        ROUTE = {}
        for nm, n in (("gpad", 16), ("epad", 48), ("list1", 8), ("list2", 8), ("lg", 36), ("g8", 8), ("e8", 8),
                      ("ngmax", 1), ("nv1", 1), ("gsum", 1), ("e21", 1), ("d", 1), ("w1", 1), ("w2", 1),
                      ("goh", 4), ("gneg", 4), ("ge", 4)):
            ROUTE[nm] = sum(k for _, k in ROUTE.values()), n
        rscratch = sb("rscratch", [P, NT, sum(k for _, k in ROUTE.values())])

        def route(name, t, n):
            at = ROUTE[name][0]
            return rscratch[:, t, at:at + n]

        def first_rows():
            at = 0
            for name, n in ROWS_0:
                yield from one_row(5, at, n, a[name][0])
                at += n

        def other_rows():
            at = 0
            for name, n in ROWS_1:
                yield from one_row(0, at, n, a[name][0])
                at += n
            yield rows[2][0:TAPS * 4, :], a["conv_w"][0, :, 0, :].rearrange("k (c p) -> (k c) p", p=P)
            at = 0
            for l in range(LAYERS):
                for name, n in ROWS_2:
                    src = a[name][l]
                    if len(src.shape) == 2:
                        src = src.rearrange("a b -> (a b)")
                    yield from one_row(1, at, n, src)
                    at += n
            for l in range(LAYERS):
                yield rows[3 + l][0:72, :], a["b_ada_2"][l].rearrange("(c p) -> c p", p=P)
                yield lora_wa[0:64, l, :], a["rwkv_w_w2_2"][l]
                yield lora_wa[64:128, l, :], a["rwkv_a_w2_2"][l]
                yield lora_g[:, l, :], a["rwkv_g_w2_2"][l]
            yield brow[0:1, 0:4], a["b_rg"]
            yield brow[0:1, 4:36], a["b_re"]
            yield brow[0:1, 36:52], a["att_sinks_2"].rearrange("(o l) h -> o (l h)", o=1)
            yield router[:, :, 0:4], a["w_rg"][0].rearrange("(k p) c -> p k c", p=P)
            yield router[:, :, 4:36], a["w_re"][0].rearrange("(k p) c -> p k c", p=P)

        def one_row(tile, at, n, src):
            if src.shape[0] == 64:
                for half in range(2):
                    yield rows[tile][at:at + 1, half * 64:half * 64 + 64], src.rearrange("(o p) -> o p", o=1)
            else:
                yield rows[tile][at:at + n, :], src.rearrange("(c p) -> c p", p=P)

        def b3(ap, n):
            return ap.unsqueeze(1).to_broadcast([ap.shape[0], n, ap.shape[1]])

        slab_end = []
        ring = []
        for_act, for_dve = [], []
        low_used = []
        glu_starts = []

        block = ctx.enter_context(nc.Block())

        GROUPS = [(t, h) for t in range(NT) for h in (0, 1, 4, 5)]
        MEM_GROUPS = [(t, h) for t in range(NT) for h in (0, 2)]

        def fillers(i):
            n = len(GROUPS)
            if i <= n + 1:
                return [i - 1] if 0 < i <= n else []
            return [2 * (i - n - 2), 2 * (i - n - 2) + 1]

        @block.tensor
        def _(pe):
            w = Seen()
            n_slab = [0]
            made = {"lo0_ready": 0, "lo1_ready": 0, "lo2_ready": 0}

            def mm(o, lhsT, rhs, start=False):
                return nc.tensor.matmul(o, lhsT, rhs, start=start, stop=True, skip_group_check=True)

            def product(consumer):
                n = len(ring)
                if n >= RING:
                    who, k = ring[n - RING]
                    if who:
                        pe.wait_ge(S["read_by_" + who], k)
                b = n % RING
                ring.append((consumer, sum(r == consumer for r, _ in ring) + 1))
                (for_act if consumer == "act" else for_dve).append(b)
                return bank[b]

            def quiet():
                for who in ("act", "dve"):
                    k = sum(r == who for r, _ in ring)
                    if k:
                        pe.wait_ge(S["read_by_" + who], k)

            def arrive(k=16):
                s = n_slab[0] % SLOTS
                n_slab[0] += 1
                pe.wait_ge(S[f"slab{s}_in"], w(f"slab{s}_in", k))
                return slab[s]

            def used(name):
                count = {"for_act": len(for_act), "for_dve": len(for_dve), **made}
                slab_end.append((name, count[name]))

            def transpose(o, in_, last=None):
                k = in_.shape[0]
                return nc.tensor.transpose(o, in_, C("eye")[0:k, 0:k])

            def project(rhs, nblocks, consumer, kc=KD, k=16, first=None, per_slab=None):
                block = projection(rhs, nblocks, consumer, kc, k, first, per_slab)
                for b in range(nblocks):
                    block(b)

            def projection(rhs, nblocks, consumer, kc=KD, k=16, first=None, per_slab=None):
                per = per_slab or SLAB // (kc * P)
                here = {}

                def block(b):
                    if b % per == 0:
                        here["s"] = arrive(k).rearrange("p (k c) -> p k c", k=kc)
                    s = here["s"]
                    ps = product(consumer)
                    for j in range(kc):
                        if first and b == 0:
                            pe.wait_ge(S[first], w(first))
                        m = mm(ps[:, 0:T], s[:, j, (b % per) * P:(b % per + 1) * P], rhs[:, j, :], j == 0)
                    m.then_inc(S["for_" + consumer], 1)
                    if b % per == per - 1 or b == nblocks - 1:
                        used("for_" + consumer)
                return block

            def split_slab(k, w_hi):
                slot = n_slab[0] % SLOTS
                n_slab[0] += 1
                low_used.append((slot, w(f"slab{slot}_in", 16)))
                pe.wait_ge(S["plo_ready"], w("plo_ready"))
                return [v[:, :].rearrange("p (k c) -> p k c", k=KD) for v in (w_hi[k % 3], slab_low[slot])]

            def project_split(blocks, w_hi, x_hi, x_lo, paced=False):
                for b in blocks:
                    if b % 2 == 0:
                        hi, lo = split_slab(b // 2, w_hi)
                    if paced and b == 0:
                        places = [product("act")[:, 0:T] for _ in range(2)]
                        for kc in range(KD):
                            pe.wait_ge(S["h_split"], w("h_split"))
                            for x, ps in enumerate(places):
                                cols = slice(x * P, (x + 1) * P)
                                mm(ps, hi[:, kc, cols], x_hi[:, kc, :], kc == 0)
                                mm(ps, hi[:, kc, cols], x_lo[:, kc, :])
                                m = mm(ps, lo[:, kc, cols], x_hi[:, kc, :])
                                if kc == KD - 1:
                                    m.then_inc(S["for_act"], 1)
                        used("for_act")
                    if paced and b < 2:
                        continue
                    cols = slice((b % 2) * P, (b % 2 + 1) * P)
                    ps = product("act")[:, 0:T]
                    for kc in range(KD):
                        mm(ps, hi[:, kc, cols], x_hi[:, kc, :], kc == 0)
                        mm(ps, hi[:, kc, cols], x_lo[:, kc, :])
                        m = mm(ps, lo[:, kc, cols], x_hi[:, kc, :])
                    m.then_inc(S["for_act"], 1)
                    if b % 2:
                        used("for_act")

            def norm_sum(kc=KD):
                ps = product("act")
                for j in range(kc):
                    if j % 2 == 0:
                        pe.wait_ge(S["sq"], w("sq"))
                    m = mm(ps[:, 0:T], C("ones"), sq[:, j, :], j == 0)
                m.then_inc(S["for_act"], 1)

            def pair_sum(src, mat="half", consumer="act"):
                ps = product(consumer)
                n = src.shape[-1] if len(src.shape) == 2 else 2 * T
                mm(ps[:, 0:n], C(mat), src, True).then_inc(S["for_" + consumer], 1)

            def attention(groups, q, kdup, v, pr, pT, mem=False):
                width = [P * (t + 1) for t in range(NT)] if not mem else [T, T]

                def scores(g):
                    t, h = groups[g]
                    ps = product("dve")
                    for j in range(2):
                        o = ps[:, j * width[t]:(j + 1) * width[t]]
                        if mem:
                            m = mm(o, q[:, h + j, t * P:(t + 1) * P], kdup[:, h + j, :], j == 0)
                        else:
                            r = (h % 2) * 64
                            m = mm(o, q[r:r + 64, h // 2 + j, t * P:(t + 1) * P],
                                   kdup[r:r + 64, h // 4, 0:width[t]], j == 0)
                    m.then_inc(S["for_dve"], 1)

                def turn(g):
                    t, h = groups[g]
                    nk = width[t] // P
                    pe.wait_ge(S["att_p"], w("att_p"))
                    ps = product("act")
                    for x in range(2 * nk):
                        m = transpose(ps[:, x * P:(x + 1) * P], pr[:, g % 2, x * P:(x + 1) * P])
                    m.then_inc(S["for_act"], 1)

                def output(g):
                    t, h = groups[g]
                    nk = width[t] // P
                    pe.wait_ge(S["att_pT"], w("att_pT"))
                    ps = product("act")
                    for j in range(2):
                        for kt in range(nk):
                            x = pT[:, g % 2, (j * nk + kt) * P:(j * nk + kt + 1) * P]
                            if mem:
                                m = mm(ps[:, j * P:(j + 1) * P], v[:, kt, (h + j) * P:(h + j + 1) * P], x,
                                       j == 0 and kt == 0)
                            else:
                                r = (h % 2) * 64
                                m = mm(ps[r:r + 64, j * P:(j + 1) * P],
                                       v[:, kt, (h // 4) * 64:(h // 4) * 64 + 64], x, j == 0 and kt == 0)
                    m.then_inc(S["for_act"], 1)
                return scores, turn, output

            def attend(groups, *args, **kw):
                scores, turn, output = attention(groups, *args, **kw)
                for g in range(len(groups) + 1):
                    if g < len(groups):
                        scores(g)
                    if g:
                        turn(g - 1)
                        output(g - 1)

            def spread(u):
                pe.wait_ge(S["sel"], w("sel"))
                mm(bank[2][:, 0:T], C("ones")[0:N_EXP, :], sel[0:N_EXP, u, :], True).then_inc(S["comb_done"], 1)

            def up_parts(j):
                return (v[:, :].rearrange("p (k c) -> p k c", k=KD) for v in (w_hi[j], w_lo[j]))

            def up_used(j):
                n_slab[0] += 1
                made[f"lo{j}_ready"] += 1
                used(f"lo{j}_ready")

            def down(first=False):
                n_slab[0] += 1
                pe.wait_ge(S["lo2_ready"], w("lo2_ready"))
                hi, lo = (v[:, :].rearrange("p (j d) -> p j d", j=2) for v in (w_hi[2], w_lo[2]))
                for j in range(2):
                    pe.wait_ge(S["gu_ready"], w("gu_ready"))
                    for d in range(KD):
                        o, c = bank[4 + d // 2][:, (d % 2) * T:(d % 2 + 1) * T], slice(d * P, (d + 1) * P)
                        mm(o, hi[:, j, c], gu_hi[:, j, :], first and j == 0 and d % 2 == 0)
                        mm(o, hi[:, j, c], gu_lo[:, j, :])
                        m = mm(o, lo[:, j, c], gu_hi[:, j, :])
                m.then_inc(S["down_done"], 1)
                made["lo2_ready"] += 1
                used("lo2_ready")

            def glu_unit(u, moe):
                if moe:
                    spread(u)
                for j in range(2):
                    pe.wait_ge(S[f"lo{j}_ready"], w(f"lo{j}_ready"))
                    hi, lo = up_parts(j)
                    for ab in range(2):
                        o, cols = bank[j][:, ab * T:(ab + 1) * T], slice(ab * P, (ab + 1) * P)
                        for kc in range(KD):
                            mm(o, hi[:, kc, cols], h_hi[:, kc, :], kc == 0)
                            mm(o, hi[:, kc, cols], h_lo[:, kc, :])
                            m = mm(o, lo[:, kc, cols], h_hi[:, kc, :])
                    m.then_inc(S["up_done"], 1)
                    up_used(j)
                down()

            def first_unit(moe):
                for j in range(2):
                    pe.wait_ge(S[f"lo{j}_ready"], w(f"lo{j}_ready"))
                for kc in range(KD):
                    pe.wait_ge(S["h_split"], w("h_split"))
                    for j in range(2):
                        hi, lo = up_parts(j)
                        for ab in range(2):
                            o, cols = bank[j][:, ab * T:(ab + 1) * T], slice(ab * P, (ab + 1) * P)
                            mm(o, hi[:, kc, cols], h_hi[:, kc, :], kc == 0 and ab == 0)
                            mm(o, hi[:, kc, cols], h_lo[:, kc, :])
                            m = mm(o, lo[:, kc, cols], h_hi[:, kc, :])
                        if kc == KD - 1:
                            m.then_inc(S["up_done"], 1)
                for j in range(2):
                    up_used(j)
                if moe:
                    pe.wait_ge(S["comb_ready"], w("comb_ready"))
                    for t in range(NT):
                        m = transpose(bank[3][0:N_EXP, t * P:(t + 1) * P],
                                      tiny[:, 96 + t * N_EXP:96 + (t + 1) * N_EXP])
                    m.then_inc(S["comb_turned"], 1)
                    spread(0)
                down(True)

            def ada_sum():
                pe.wait_ge(S["ada_done"], w("ada_done"))
                for b in range(9):
                    m = mm(bank[3][:, b:b + 1], ada_acc[:, b * P:(b + 1) * P], C("ones")[:, 0:1], b == 0)
                m.then_inc(S["ada_sum"], 1)

            def glu(units, moe):
                quiet()
                glu_starts.append((n_slab[0], {f"slab{s}_in": w.n.get(f"slab{s}_in", 0) for s in range(SLOTS)}))
                if not moe:
                    w("hn", KD)
                at = n_slab[0]
                first_unit(moe)
                if moe:
                    glu_unit(1, moe)
                    ada_sum()
                turns = (units - 1) // 2
                with pe.Fori(0, turns) as i:
                    n0, made0 = len(slab_end), dict(made)
                    w.enter(i, {"gu_ready": 4, "sel": 2, "ada_done": 1, "lo0_ready": 2, "lo1_ready": 2, "lo2_ready": 2})
                    for u in range(2):
                        glu_unit(u, moe)
                    if moe:
                        ada_sum()
                    w.leave(turns)
                n_slab[0] += 6 * (turns - 1)
                body = slab_end[n0:]
                for r in range(1, turns):
                    slab_end.extend((name, k + 2 * r) for name, k in body)
                for name in made:
                    made[name] = made0[name] + 2 * turns
                while len(ring) % RING:
                    ring.append((None, 0))
                for n in range(at, n_slab[0]):
                    w(f"slab{n % SLOTS}_in", 16 if (n - at) % 3 == 2 else 32)

            ada_acc = M["ada_acc"].rearrange("p a c -> p (a c)")

            pe.wait_ge(S["const_in"], w("const_in", 16))

            def to_features(src, sem):
                pe.wait_ge(S[sem], w(sem, 16))
                for kc in range(0, KD, 2):
                    ps = product("act")
                    for x in range(4):
                        m = transpose(ps[:, x * P:(x + 1) * P],
                                      src[:, x % 2, (kc + x // 2) * P:(kc + x // 2 + 1) * P])
                    m.then_inc(S["for_act"], 1)

            def to_columns(n):
                ps = product("act")
                transpose(ps[:, 0:ROW_COUNTS[n]], rows[n][0:ROW_COUNTS[n], :]).then_inc(S["for_act"], 1)
            to_features(xin, "x_in")
            norm_sum()
            pe.wait_ge(S["rows_in"], 16 * sum(1 for _ in first_rows()))
            to_columns(5)
            project(hT, 4, "act", first="hn")
            to_features(memin, "mem_in")
            norm_sum()
            s = arrive(48).rearrange("p (k c) -> p k c", k=KD)
            ps = product("act")
            for kc in range(KD):
                m = mm(ps[:, 0:T], s[:, kc, 0:P], hT[:, kc, :], kc == 0)
            m.then_inc(S["for_act"], 1)
            ps = product("act")
            for t in range(NT):
                for kc in range(KD):
                    m = mm(ps[:, t * 8:(t + 1) * 8], hT[:, kc, t * P:(t + 1) * P], s[:, kc, P:P + 8],
                           t == 0 and kc == 0)
            m.then_inc(S["for_act"], 1)
            used("for_act")

            def key_value():
                s = arrive().rearrange("p (k c) -> p k c", k=KD)
                ps = product("act")
                for kc in range(KD):
                    m = mm(ps[:, 0:T], s[:, kc, 0:P], hT[:, kc, :], kc == 0)
                m.then_inc(S["for_act"], 1)
                ps = product("act")
                for t in range(NT):
                    for kc in range(KD):
                        m = mm(ps[:, t * P:(t + 1) * P], hT[:, kc, t * P:(t + 1) * P], s[:, kc, P:2 * P],
                               t == 0 and kc == 0)
                m.then_inc(S["for_act"], 1)
                used("for_act")
            key_value()
            project(hT, 4, "act")
            pe.wait_ge(S["others_in"], 16 * sum(1 for _ in other_rows()))
            for n in range(5):
                to_columns(n)
            ps = product("act")
            mm(ps[:, 0:52], C("ones")[0:1, :], brow[0:1, :], True).then_inc(S["for_act"], 1)
            pe.wait_ge(S["const_more"], w("const_more", 16))
            pe.wait_ge(S["ki_sq"], w("ki_sq"))
            pair_sum(sq[:, 0, :])
            for x in range(2):
                pair_sum(B1["qi"][:, 2 * x:2 * x + 2, :], "rot", "dve")
            pe.wait_ge(S["ki_normed"], w("ki_normed"))
            pair_sum(B1["ki"], "rot", "dve")
            pe.wait_ge(S["qka_sq"], w("qka_sq"))
            pair_sum(sq[:, 1:3, :])
            pair_sum(sq[:, 3:5, :])
            pair_sum(sq[:, 5, :])
            pe.wait_ge(S["idx_roped"], w("idx_roped"))
            for t, h in GROUPS:
                r, wd = (h % 2) * 64, P * (t + 1)
                ps = product("act")
                for j in range(2):
                    m = mm(ps[:, j * wd:(j + 1) * wd], B1["qi"][r:r + 64, h // 2 + j, t * P:(t + 1) * P],
                           B1["ki"][r:r + 64, 0:wd], j == 0)
                m.then_inc(S["for_act"], 1)
            pe.wait_ge(S["qka_normed"], w("qka_normed"))
            for x in range(2):
                pair_sum(B1["qa"][:, 2 * x:2 * x + 2, :], "rot", "dve")
            pair_sum(B1["ka"], "rot", "dve")
            pe.wait_ge(S["p_split"], w("p_split"))
            project_split(range(8), early_hi, p_hi, p_lo)
            pe.wait_ge(S["ka_roped"], w("ka_roped"))
            for x in range(2):
                pair_sum(B1["ka"], f"dup{x}")
            project_split(range(8, 12), early_hi, p_hi, p_lo)
            for i in range(KD):
                pe.wait_ge(S["memh"], w("memh"))
            project(B1["memh"], 4, "act")
            vslab = [arrive().rearrange("p (k c) -> p k c", k=KD) for _ in range(2)]
            for t in range(NT):
                ps = product("act")
                for x in range(2):
                    for kc in range(KD):
                        m = mm(ps[:, x * T:(x + 1) * T], B1["memh"][:, kc, t * P:(t + 1) * P],
                               vslab[x][:, kc, :], x == 0 and kc == 0)
                m.then_inc(S["for_act"], 1)
            used("for_act")
            used("for_act")
            pe.wait_ge(S["qkm_sq"], w("qkm_sq"))
            for x in range(4):
                pair_sum(sq[:, 2 * x:2 * x + 2, :], "ones")
            project_split(range(CONV_SUM), gates_hi, p_hi, p_lo)
            pe.wait_ge(S["conv_y"], w("conv_y"))
            ps = product("dve")
            for j in range(4):
                m = mm(ps[:, 0:T], C("ones"), B1["y"][:, j, :], j == 0)
            m.then_inc(S["for_dve"], 1)
            project_split(range(CONV_SUM, CONV_VAR), gates_hi, p_hi, p_lo)
            norm_sum(4)
            project_split(range(CONV_VAR, 24), gates_hi, p_hi, p_lo)
            pe.wait_ge(S["qa_roped"], w("qa_roped"))
            pe.wait_ge(S["dsa_mask"], w("dsa_mask"))
            pe.wait_ge(S["qkm_normed"], w("qkm_normed"))
            own = attention(GROUPS, B1["qa"], B1["kdup"], B1["va"], B1["pr"], B1["pT"])
            mem = attention(MEM_GROUPS, B1["qm"], B1["km"], B1["vm"], B1["pr"], B1["pT"], mem=True)
            both = [(own, g) for g in range(len(GROUPS))] + [(mem, g) for g in range(len(MEM_GROUPS))]
            for i in range(len(both) + 2):
                if i < len(both):
                    (scores, _, _), g = both[i]
                    scores(g)
                if i == 1:
                    pe.wait_ge(S["ob_ready"], w("ob_ready"))
                    branch = projection(B1["ob"], KD, "dve", kc=4)
                if i == len(GROUPS) + 2:
                    pe.wait_ge(S["oa_ready"], w("oa_ready"))
                    branch = projection(B1["oa"], KD, "dve", kc=4)
                for b in fillers(i):
                    branch(b)
                if 1 <= i <= len(both):
                    (_, turn, _), g = both[i - 1]
                    turn(g)
                if i >= 2:
                    (_, _, output), g = both[i - 2]
                    output(g)
            pe.wait_ge(S["om_ready"], w("om_ready"))
            project(B1["om"], KD, "dve", kc=4)
            pe.wait_ge(S["merged"], w("merged"))
            project(B1["merged"], 8, "dve")
            norm_sum()
            for i in range(KD):
                pe.wait_ge(S["hn"], w("hn"))
            ps = product("dve")
            for t in range(NT):
                for kc in range(KD):
                    m = mm(ps[:, t * 64:t * 64 + 36], hT[:, kc, t * P:(t + 1) * P], router[:, kc, :],
                           t == 0 and kc == 0)
            m.then_inc(S["for_dve"], 1)
            glu(N_EXP, True)

            for l in range(LAYERS):
                for part in range(2):
                    norm_sum()
                    if part == 0:
                        glu(FFN_UNITS, False)
                        continue
                    V = B2
                    w("hn", KD)
                    project_split(range(12), mix_hi, m_hi, m_lo, paced=True)
                    key_value()
                    pe.wait_ge(S["lora_in"], w("lora_in"))
                    ps = product("act")
                    for c in range(2):
                        m = mm(ps[:, c * T:(c + 1) * T], lora_wa[0:64, l, c * P:(c + 1) * P],
                               V["th"][0:64, :], c == 0)
                    m.then_inc(S["for_act"], 1)
                    ps = product("act")
                    for c in range(2):
                        m = mm(ps[:, c * T:(c + 1) * T], lora_wa[64:128, l, c * P:(c + 1) * P],
                               V["pm"][64:128, 6, :], c == 0)
                    m.then_inc(S["for_act"], 1)
                    ps = product("act")
                    for c in range(2):
                        m = mm(ps[:, c * T:(c + 1) * T], lora_g[:, l, c * P:(c + 1) * P],
                               V["pm"][:, 7, :], c == 0)
                    m.then_inc(S["for_act"], 1)
                    pe.wait_ge(S["kk_sq"], w("kk_sq"))
                    pair_sum(sq[:, 0:2, :], consumer="dve")
                    pe.wait_ge(S["att_sq"], w("att_sq"))
                    pair_sum(sq[:, 2:4, :])
                    pair_sum(sq[:, 4:6, :])
                    pair_sum(sq[:, 6, :])
                    short = projection(hT, 6, "act")
                    for b in range(SHORT_FIRST):
                        short(b)
                    pe.wait_ge(S["bonus_in"], w("bonus_in"))
                    pair_sum(V["ysh"][:, 0:2, :], consumer="dve")
                    pe.wait_ge(S["rwkv_in"], w("rwkv_in"))
                    for src in (V["pm"][:, 4:6, :], V["be"], V["kap"]):
                        ps = product("act")
                        for x in range(4):
                            t, c = x // 2, x % 2
                            m = transpose(ps[:, x * P:(x + 1) * P], src[:, c, t * P:(t + 1) * P])
                        m.then_inc(S["for_act"], 1)
                    for left, right in (("be", "al"), ("kap", "al"), ("be", "rho"), ("kap", "rho")):
                        for g in range(2):
                            r = g * 64
                            ps = product("dve")
                            for x in range(4):
                                t, c = x // 2, x % 2
                                m = mm(ps[:, x * P:(x + 1) * P], V[left][r:r + 64, c, t * P:(t + 1) * P],
                                       V[right][r:r + 64, c, t * P:(t + 1) * P], x == 0)
                            m.then_inc(S["for_dve"], 1)
                    pe.wait_ge(S["att_normed"], w("att_normed"))
                    for x in range(2):
                        pair_sum(V["k"], f"dup{x}")
                    scores, turn, output = attention(GROUPS, V["q"], V["kdup"], V["v"], V["pr"], V["pT"])
                    for lev in range(6):
                        for g in range(2):
                            pe.wait_ge(S["off_ready"], w("off_ready"))
                            ps = product("act")
                            for x in range(4):
                                X = slice(x * P, (x + 1) * P)
                                m = mm(ps[:, X], V["off"][:, g, X], V["Tm"][:, g, X], x == 0)
                            m.then_inc(S["for_act"], 1)
                        if lev == 0:
                            pe.wait_ge(S["kdup_ready"], w("kdup_ready"))
                        scores(lev)
                        if lev:
                            turn(lev - 1)
                        for g in range(2):
                            pe.wait_ge(S["m1_ready"], w("m1_ready"))
                            if lev < 5:
                                ps = product("dve")
                                for x in range(4):
                                    X = slice(x * P, (x + 1) * P)
                                    m = mm(ps[:, X], V["TT"][:, g, X], V["M1"][:, g, X], x == 0)
                                m.then_inc(S["for_dve"], 1)
                            ps = product("dve")
                            for x in range(4):
                                X = slice(x * P, (x + 1) * P)
                                m = mm(ps[:, X], V["M1"][:, g, X], V["TT"][:, g, X], x == 0)
                            m.then_inc(S["for_dve"], 1)
                        if lev:
                            output(lev - 1)
                        if SHORT_FIRST + lev < 6:
                            short(SHORT_FIRST + lev)
                    for c4 in range(T // CHUNK):
                        t, r0 = c4 // 2, (c4 % 2) * CHUNK
                        if c4 == 0:
                            pe.wait_ge(S["solve_ready"], w("solve_ready"))
                        pe.wait_ge(S["state_ready"], w("state_ready"))
                        ps = product("act")
                        for h in range(4):
                            X = slice((2 * t + h // 2) * P, (2 * t + h // 2 + 1) * P)
                            mm(ps[:, h * 64:(h + 1) * 64], V["BT"][:, h % 2, X],
                               V["vt"][:, t, h * 64:(h + 1) * 64], h == 0)
                        for c in range(2):
                            m = mm(ps[:, c * P:(c + 1) * P], V["al"][:, c, t * P:(t + 1) * P],
                                   V["state"][:, c, :])
                        m.then_inc(S["for_act"], 1)
                        if 6 + c4 < len(GROUPS):
                            scores(6 + c4)
                        if 5 + c4 < len(GROUPS):
                            turn(5 + c4)
                        for c in range(2):
                            tok = slice(c4 * CHUNK, (c4 + 1) * CHUNK)
                            mm(bank[7][:, c * T + c4 * CHUNK:c * T + (c4 + 1) * CHUNK], V["state"][:, c, :],
                               V["rho"][:, c, tok], c4 == 0 and c == 0)
                        pe.wait_ge(S["r_ready"], w("r_ready"))
                        ps = product("dve")
                        for h in range(4):
                            X = slice((2 * t + h // 2) * P, (2 * t + h // 2 + 1) * P)
                            m = mm(ps[:, h * 64:(h + 1) * 64], V["TT"][:, h % 2, X],
                                   V["R"][:, h * 64:(h + 1) * 64], h == 0)
                        m.then_inc(S["for_dve"], 1)
                        if 5 + c4 < len(GROUPS):
                            output(5 + c4)
                        pe.wait_ge(S["u_ready"], w("u_ready"))
                        if c4 < 3:
                            ps = product("dve")
                            for c in range(2):
                                mm(ps[:, c * P:(c + 1) * P], V["bt"][r0:r0 + CHUNK, t, c * P:(c + 1) * P],
                                   V["negU"][r0:r0 + CHUNK, t, c * P:(c + 1) * P], c == 0)
                                m = mm(ps[:, c * P:(c + 1) * P], V["kt"][r0:r0 + CHUNK, t, c * P:(c + 1) * P],
                                       V["vt"][r0:r0 + CHUNK, t, c * P:(c + 1) * P])
                            m.then_inc(S["for_dve"], 1)
                        if c4 % 2:
                            for h in range(4):
                                X = slice((2 * t + h // 2) * P, (2 * t + h // 2 + 1) * P)
                                o = bank[7][(h % 2) * 64:(h % 2) * 64 + 64,
                                            (h // 2) * T + t * P:(h // 2) * T + (t + 1) * P]
                                mm(o, V["vt"][:, t, h * 64:(h + 1) * 64], V["C2T"][:, h % 2, X])
                                m = mm(o, V["negU"][:, t, h * 64:(h + 1) * 64], V["C1T"][:, h % 2, X])
                            if c4 == 3:
                                m.then_inc(S["y_done"], 1)
                    pe.wait_ge(S["y_ready"], w("y_ready"))
                    pair_sum(V["W"], consumer="dve")
                    pe.wait_ge(S["yc_sq"], w("yc_sq"))
                    pair_sum(sq[:, 0:2, :])
                    pe.wait_ge(S["swa_ready"], w("swa_ready"))
                    pe.wait_ge(S["conv_ready"], w("conv_ready"))
                    parts = [V["o"][:, j, :] for j in range(4)] + [V["yr"][:, j, :] for j in range(2)] \
                        + [V["cy"][:, j, :] for j in range(2)]
                    early, slabs, places = (0, 1, 2, 3, 6, 7), [], []
                    for b in range(KD):
                        if b % 2 == 0 and b < OUT_EARLY:
                            slabs.append(arrive().rearrange("p (k c) -> p k c", k=KD))
                        if b < OUT_EARLY:
                            places.append(product("dve"))
                            for j in early:
                                mm(places[b][:, 0:T], slabs[b // 2][:, j, (b % 2) * P:(b % 2 + 1) * P], parts[j], j == 0)
                    pe.wait_ge(S["mix_ready"], w("mix_ready"))
                    for b in range(KD):
                        if b >= OUT_EARLY:
                            if b % 2 == 0:
                                slabs.append(arrive().rearrange("p (k c) -> p k c", k=KD))
                            places.append(product("dve"))
                        for j in (4, 5) if b < OUT_EARLY else range(KD):
                            m = mm(places[b][:, 0:T], slabs[b // 2][:, j, (b % 2) * P:(b % 2 + 1) * P], parts[j],
                                   j == 0)
                        m.then_inc(S["for_dve"], 1)
                        if b % 2:
                            used("for_dve")
                norm_sum()
                glu(FFN_UNITS, False)
            for i in range(KD):
                pe.wait_ge(S["x_ready_pe"], w("x_ready_pe"))
            for t in range(NT):
                for x in range(2):
                    ps = product("act")
                    for j in range(4):
                        kc = 4 * x + j
                        m = transpose(ps[:, j * P:(j + 1) * P], xT[:, kc, t * P:(t + 1) * P])
                    m.then_inc(S["for_act"], 1)

        @block.scalar
        def _(act):
            w = Seen()
            banks = iter(for_act)
            table = [None]
            started = set()
            starts = list(glu_starts)

            def tables(name):
                if table[0] != name:
                    nc.scalar.preload_act_table_set(name)
                    table[0] = name
            LNEXP, SIG, SILU = "natural_log_exp_and_others", "sigmoid_and_others", "silu_and_others"

            def take():
                act.wait_ge(S["for_act"], w("for_act"))
                return bank[next(banks)]

            def read(ins):
                ins.then_inc(S["read_by_act"], 1)
                w("read_by_act")

            def link(ins):
                ins.then_inc(S["act_step"], 1)
                act.wait_ge(S["act_step"], w("act_step"))

            def evac(dst, src_cols=None, func=ACT.Copy, shape=None, **kw):
                ps = take()
                src = ps[:, 0:src_cols or T]
                if shape:
                    src = src.rearrange("p (a b) -> p a b", a=shape)
                read(nc.scalar.activation(dst, src, func, **kw))

            def rsqrt_of(ps_ap, dst, scale, bias, sem=None):
                n = ps_ap.shape[-1]
                if "rs" in w.n:
                    act.wait_ge(S["rs"], w.n["rs"])
                w("rs")
                ins = nc.scalar.activation(lnt[:, 0:n], ps_ap, ACT.Ln, scale=scale, bias=bias)
                read(ins)
                act.wait_ge(S["read_by_act"], w.n["read_by_act"])
                if "rs" in started:
                    act.wait_ge(S["rs_used"], w("rs_used"))
                started.add("rs")
                nc.scalar.activation(dst, lnt[:, 0:n], ACT.Exp, scale=-0.5).then_inc(S[sem], 1)

            def squares(src, dst=None):
                for x in range(0, src.shape[1], 2):
                    nc.scalar.activation(sq[:, x:x + 2, :], src[:, x:x + 2, :], ACT.Square)\
                        .then_inc(S["sq"], 1)

            def norm(glu_next=False, parts=None, chained=None):
                tables(LNEXP)
                if not glu_next:
                    split_slab(mix_hi, 0)
                for x in range(0, KD, 2):
                    act.wait_ge(S["x_ready"], w("x_ready", 2))
                    nc.scalar.activation(sq[:, x:x + 2, :], xT[:, x:x + 2, :], ACT.Square).then_inc(S["sq"], 1)
                if not glu_next:
                    split_slab(mix_hi, 1)
                if chained is not None:
                    split_high(2, (chained + 2) % SLOTS, 16)
                rsqrt_of(take()[:, 0:T], rsB[:, 0:T], 1.0 / D, C("small", 0, 1), "rs")
                if glu_next:
                    split_h()
                else:
                    split_h(parts)
                    split_slab(mix_hi, 2)

            def attention(groups, sc, pr, pT, o, mem=False, sink=None):
                width = [P * (t + 1) for t in range(NT)] if not mem else [T, T]
                nm, rsum, es = tiny[:, 0:4], tiny[:, 4:8], tiny[:, 8:12]

                def exps(g):
                    t, h = groups[g]
                    act.wait_ge(S["att_max"], w("att_max"))
                    for j in range(2):
                        k = (g % 2) * 2 + j
                        if sink is not None:
                            hh = h + 2 * j
                            nc.scalar.activation(es[:, k:k + 1], bbc[:, 36 + 8 * sink + hh:37 + 8 * sink + hh], ACT.Exp,
                                                 bias=nm[:, k:k + 1])
                        m = nc.scalar.activation(pr[:, g % 2, j * width[t]:(j + 1) * width[t]],
                                                 sc[:, g % 2, j * width[t]:(j + 1) * width[t]], ACT.Exp,
                                                 bias=nm[:, k:k + 1], accum_out=rsum[:, k:k + 1])
                    m.then_inc(S["att_exp"], 1)

                def turned(g):
                    n = 2 * width[groups[g][0]]
                    ps = take()
                    read(nc.scalar.activation(pT[:, g % 2, 0:n], ps[:, 0:n], ACT.Copy))
                    act.wait_ge(S["read_by_act"], w.n["read_by_act"])
                    act.sem_inc(S["att_pT"], 1)

                def output(g):
                    t, h = groups[g]
                    ps = take()
                    if mem:
                        dst = o[:, h:h + 2, t * P:(t + 1) * P]
                        src = ps[:, 0:2 * P]
                    else:
                        r = (h % 2) * 64
                        dst = o[r:r + 64, h // 2:h // 2 + 2, t * P:(t + 1) * P]
                        src = ps[r:r + 64, 0:2 * P]
                    read(nc.scalar.activation(dst, src.rearrange("p (a b) -> p a b", a=2), ACT.Copy))
                return exps, turned, output

            def attend(groups, sc, pr, pT, o, sem, **kw):
                exps, turned, output = attention(groups, sc, pr, pT, o, **kw)
                for g in range(len(groups) + 1):
                    if g < len(groups):
                        exps(g)
                    if g:
                        turned(g - 1)
                        output(g - 1)
                act.wait_ge(S["read_by_act"], w.n["read_by_act"])
                act.sem_inc(S[sem], 1)

            def split_high(x, slot, k):
                act.wait_ge(S[f"slab{slot}_in"], w(f"slab{slot}_in", k))
                nc.scalar.activation(w_hi[x][:, :], slab[slot][:, :], ACT.Copy).then_inc(S[f"hi{x}_ready"], 1)

            def split_first():
                at, seen = starts.pop(0)
                for name, v in seen.items():
                    w.n[name] = v
                for x in range(3):
                    split_high(x, (at + x) % SLOTS, (32, 32, 16)[x])
                return at

            low_slabs = iter(low_used)

            def split_slab(w_hi, k):
                slot, there = next(low_slabs)
                act.wait_ge(S[f"slab{slot}_in"], there)
                nc.scalar.activation(w_hi[k % 3][:, :], slab[slot][:, :], ACT.Copy).then_inc(S["phi_ready"], 1)

            def split_h(h_hi=h_hi):
                for j in range(KD):
                    act.wait_ge(S["hn"], w("hn"))
                    nc.scalar.activation(h_hi[:, j, :], hT[:, j, :], ACT.Copy).then_inc(S["h_high"], 1)

            def glu(at, turns, tail, moe, more):
                tables(SILU)

                def load_ada(l, i, u, used=None):
                    if used is not None:
                        act.wait_ge(S["ada_step"], used)
                    cols = a["w_ada_2"][l][:, bass.ds(i * (2 * ADA_COLS) + u * ADA_COLS, ADA_COLS)]
                    act.dma_start(ada_in[u], cols.rearrange("(k p) c -> p k c", p=P)).then_inc(S[f"ada_in{u}"], 16)

                def unit(u, pos, more, ada=None, last=False):
                    for j in range(2):
                        act.wait_ge(S["up_done"], w("up_done"))
                        nc.scalar.activation(silu[:, j, :], bank[j][:, 0:T], ACT.Silu)\
                            .then_inc(S["silu_ready"], 1)
                        if more:
                            split_high(j, (pos + j) % SLOTS, 32)
                        if ada and j == 0:
                            load_ada(*ada)
                    if last:
                        tables(LNEXP)
                    act.wait_ge(S["down_done"], w("down_done"))
                    if more and not last:
                        split_high(2, (pos + 2) % SLOTS, 16)
                per = {"up_done": 4, "down_done": 2}
                per |= {f"slab{(at + x) % SLOTS}_in": (32, 32, 16)[x % 3] for x in range(6)}
                if not moe:
                    with act.Fori(0, turns) as i:
                        w.enter(i, per)
                        for u in range(2):
                            unit(u, at + 3 * (u + 1), True)
                        w.leave(turns)
                    unit(0, at + 3, more, None, True)
                    return starts.pop(0)[0] if more else None
                half = turns // LAYERS
                load_ada(0, 0, 0)
                unit(0, at + 3, True, (0, 0, 1))
                unit(1, at + 6, True, (0, 1, 0, 8))
                for l in range(LAYERS):
                    start = 1 if l == 0 else 0
                    k = half - 1 - start
                    with act.Fori(start, half - 1) as i:
                        w.enter(i - start if start else i, per)
                        unit(0, at + 3, True, (l, i, 1, i * 16 + 16 * half * l))
                        unit(1, at + 6, True, (l, i + 1, 0, i * 16 + 16 * half * l + 8))
                        w.leave(k)
                    n = 16 * (half * (l + 1) - 1)
                    unit(0, at + 3, True, (l, half - 1, 1, n))
                    unit(1, at + 6, more or l < LAYERS - 1, (l + 1, 0, 0, n + 8) if l < LAYERS - 1 else None,
                         l == LAYERS - 1)
                return starts.pop(0)[0] if more else None

            for dst, src in first_rows():
                act.dma_start(dst, src).then_inc(S["rows_in"], 16)
            act.wait_ge(S["const_in"], w("const_in", 16))

            def columns(dst, n):
                ps = take()
                read(nc.scalar.activation(dst[:, 0:n], ps[:, 0:n], ACT.Copy))
            for kc in range(0, KD, 2):
                evac(xT[:, kc:kc + 2, :].rearrange("p a b -> p (a b)"), 512)
            act.wait_ge(S["read_by_act"], w.n["read_by_act"])
            squares(xT)
            tables(LNEXP)
            rsqrt_of(take()[:, 0:T], rsB[:, 0:T], 1.0 / D, C("small", 0, 1), "rs")
            columns(par0, ROW_COUNTS[5])
            act.wait_ge(S["read_by_act"], w.n["read_by_act"])
            act.sem_inc(S["params"], 1)
            w("hn", KD)
            for c in range(4):
                evac(B1["qi"][:, c, :])
            for kc in range(0, KD, 2):
                evac(memT[:, kc:kc + 2, :].rearrange("p a b -> p (a b)"), 512)
            act.wait_ge(S["read_by_act"], w.n["read_by_act"])
            squares(memT)
            rsqrt_of(take()[:, 0:T], rsB[:, 0:T], 1.0 / D, C("small", 0, 1), "rs")
            evac(B1["ki"])
            ps = take()
            read(nc.scalar.activation(B1["wi"], ps[:, 0:16].rearrange("p (a b) -> p a b", a=2), ACT.Copy,
                                      scale=8 ** -0.5))
            act.wait_ge(S["read_by_act"], w.n["read_by_act"])
            nc.scalar.activation(sq[:, 0, :], B1["ki"], ACT.Square).then_inc(S["ki_sq"], 1)
            evac(B1["ka"])
            evac(B1["va"], shape=2)
            for c in range(4):
                evac(B1["qa"][:, c, :])
            for dst, n in ((par1, ROW_COUNTS[0]), (par2, ROW_COUNTS[1]), (taps, ROW_COUNTS[2]),
                           (b_ada[:, 0:72], 72), (b_ada[:, 72:144], 72), (bbc, 52)):
                columns(dst, n)
            act.wait_ge(S["read_by_act"], w.n["read_by_act"])
            act.sem_inc(S["params_more"], 1)
            nc.scalar.activation(sq[:, 1:5, :], B1["qa"], ACT.Square)
            nc.scalar.activation(sq[:, 5, :], B1["ka"], ACT.Square).then_inc(S["qka_sq"], 1)
            rsqrt_of(take()[:, 0:T], rsB[:, 0:T], 1.0 / 64, C("small", 0, 1), "rs")
            for x in range(3):
                n = 512 if x < 2 else T
                rsqrt_of(take()[:, 0:n], rsB[:, 0:n], 1.0 / 64, C("small", 0, 1), "rs")
            nc.scalar.activation(p_hi[:, :, :], hT[:, :, :], ACT.Copy).then_inc(S["p_high"], 1)
            for k in range(3):
                split_slab(early_hi, k)
            for g, (t, h) in enumerate(GROUPS):
                wd = P * (t + 1)
                ps = take()
                if g >= 2:
                    act.wait_ge(S["rl_used"], w("rl_used"))
                read(nc.scalar.activation(B1["rl"][:, g % 2, :, 0:wd],
                                          ps[:, 0:2 * wd].rearrange("p (a b) -> p a b", a=2), ACT.Relu,
                                          scale=64 ** -0.5))
                act.wait_ge(S["read_by_act"], w.n["read_by_act"])
                act.sem_inc(S["rl_ready"], 1)
            for c in range(4):
                evac(B1["u"][:, c, 30:30 + T])
                if c % 2:
                    split_slab(early_hi, 3 + c // 2)
            tables(SIG)
            for c in range(4):
                evac(B1["ug"][:, c, :], func=ACT.Sigmoid)
                if c == 1:
                    split_slab(early_hi, 5)
            act.wait_ge(S["read_by_act"], w.n["read_by_act"])
            act.sem_inc(S["glu_in"], 1)
            for x in range(2):
                evac(B1["kdup"][:, x, :])
            for c in range(4):
                evac(B1["qm"][:, c, :])
            tables(LNEXP)
            for c in range(4):
                evac(B1["km"][:, c, :])
            act.wait_ge(S["read_by_act"], w.n["read_by_act"])
            nc.scalar.activation(sq[:, 0:4, :], B1["qm"], ACT.Square)
            nc.scalar.activation(sq[:, 4:8, :], B1["km"], ACT.Square).then_inc(S["qkm_sq"], 1)
            act.wait_ge(S["dsa_mask"], 1)
            for k in range(2):
                split_slab(gates_hi, k)
            for t in range(NT):
                evac(B1["vm"][:, t, :], 512)
            split_slab(gates_hi, 2)
            for x in range(4):
                rsqrt_of(take()[:, 0:512], rsB[:, 0:512], 1.0 / P, C("small", 0, 1), "rs")
            tables(SIG)
            act.wait_ge(S["memh_all"], w("memh_all"))
            def gate(c):
                evac(B1["gate"][:, c, :], func=ACT.Sigmoid, bias=col("b_gate", c))
                if c % 2 and c // 2 + 3 < 12:
                    split_slab(gates_hi, c // 2 + 3)
            for c in range(CONV_SUM + 1):
                gate(c)
            act.wait_ge(S["yc_ready"], w("yc_ready"))
            squares(B1["y"])
            for c in range(CONV_SUM + 1, CONV_VAR):
                gate(c)
            tables(LNEXP)
            rsqrt_of(take()[:, 0:T], rsB[:, 0:T], 1.0 / 512, C("small", 0, 1), "rs")
            tables(SILU)
            _, ca, _ = par_at("c_2")
            nc.scalar.activation(c_act[:, :], par1[:, ca:ca + KD], ACT.Silu).then_inc(S["c_act"], 1)
            act.wait_ge(S["yn_ready"], w("yn_ready"))
            for c in range(4):
                m = nc.scalar.activation(B1["ob"][:, c, :], B1["y"][:, c, :], ACT.Silu, bias=col("ln_b", c))
            m.then_inc(S["ob_ready"], 1)
            tables(SIG)
            for c in range(CONV_VAR, 24):
                gate(c)
            tables(LNEXP)
            own = attention(GROUPS, B1["sc"], B1["pr"], B1["pT"], B1["oa"])
            mem = attention(MEM_GROUPS, B1["sc"], B1["pr"], B1["pT"], B1["om"], mem=True)
            both = [(own, g) for g in range(len(GROUPS))] + [(mem, g) for g in range(len(MEM_GROUPS))]
            for i in range(len(both) + 2):
                if i < len(both):
                    (exps, _, _), g = both[i]
                    exps(g)
                if 1 <= i <= len(both):
                    (_, turned, _), g = both[i - 1]
                    turned(g)
                if i >= 2:
                    (_, _, output), g = both[i - 2]
                    output(g)
                if i == len(GROUPS) + 1 or i == len(both) + 1:
                    act.wait_ge(S["read_by_act"], w.n["read_by_act"])
                    act.sem_inc(S["oa_ready" if i == len(GROUPS) + 1 else "om_ready"], 1)
            act.wait_ge(S["merged"], 1)
            at = split_first()
            norm(glu_next=True)
            act.wait_ge(S["router_max"], w("router_max"))
            for t in range(NT):
                m = nc.scalar.activation(route("ge", t, 4), route("lg", t, 4), ACT.Exp, bias=route("ngmax", t, 1),
                                         accum_out=route("gsum", t, 1))
            m.then_inc(S["router_exp"], 1)
            act.wait_ge(S["router_top2"], w("router_top2"))
            for t in range(NT):
                m = nc.scalar.activation(route("e21", t, 1), route("e8", t, 8)[:, 1:2], ACT.Exp,
                                         bias=route("nv1", t, 1))
            m.then_inc(S["router_exp"], 1)
            at = glu(at, N_EXP // 2, 0, True, True)

            for l in range(LAYERS):
                V = B2
                norm(glu_next=True, chained=at)
                glu(at, 5, 1, False, False)
                norm(parts=m_hi)
                for b in range(8):
                    evac(V["praw"][:, b, 1:1 + T])
                    if b % 2 and b < 6:
                        split_slab(mix_hi, b // 2 + 3)
                act.wait_ge(S["read_by_act"], w.n["read_by_act"])
                act.sem_inc(S["praw_ready"], 1)
                for c in range(4):
                    evac(V["q"][:, c, :])
                evac(V["k"])
                evac(V["v"], shape=2)
                tables(SIG)
                act.wait_ge(S["pm_ready"], w("pm_ready"))
                nc.scalar.activation(V["th"][0:64, :], V["pm"][0:64, 6, :], ACT.Tanh)
                nc.scalar.activation(V["pm"][:, 7, :], V["pm"][:, 7, :], ACT.Sigmoid).then_inc(S["lora_in"], 1)
                ps = take()
                nc.scalar.activation(V["sw"][:, 0, :], ps[:, 0:T], ACT.Sigmoid, bias=col("rwkv_w0_2", 0, l))
                read(nc.scalar.activation(V["sw"][:, 1, :], ps[:, T:2 * T], ACT.Sigmoid,
                                          bias=col("rwkv_w0_2", 1, l)))
                ps = take()
                nc.scalar.activation(V["aa"][:, 0, :], ps[:, 0:T], ACT.Sigmoid, bias=col("rwkv_a0_2", 0, l))
                read(nc.scalar.activation(V["aa"][:, 1, :], ps[:, T:2 * T], ACT.Sigmoid,
                                          bias=col("rwkv_a0_2", 1, l)))
                act.wait_ge(S["read_by_act"], w.n["read_by_act"])
                act.sem_inc(S["sw_ready"], 1)
                evac(V["gB"], 512, shape=2)
                act.wait_ge(S["kk_raw"], w("kk_raw"))
                nc.scalar.activation(sq[:, 0:2, :], V["kk"], ACT.Square).then_inc(S["kk_sq"], 1)
                nc.scalar.activation(sq[:, 2:6, :], V["q"], ACT.Square)
                nc.scalar.activation(sq[:, 6, :], V["k"], ACT.Square).then_inc(S["att_sq"], 1)
                tables(LNEXP)
                act.wait_ge(S["kk_sum"], w("kk_sum"))
                act.wait_ge(S["rs"], w.n["rs"])
                w("rs")
                link(nc.scalar.activation(lnt[:, :], rsB[:, :], ACT.Ln))
                act.wait_ge(S["rs_used"], w("rs_used"))
                nc.scalar.activation(rsB[:, :], lnt[:, :], ACT.Exp, scale=-0.5, bias=C("small", 2, 3))\
                    .then_inc(S["rs"], 1)
                act.wait_ge(S["cs_ready"], w("cs_ready"))
                nc.scalar.activation(V["W"], V["cs"], ACT.Exp, scale=-DECAY_C)
                nc.scalar.activation(V["Winv"], V["cs"], ACT.Exp, scale=DECAY_C)
                nc.scalar.activation(V["Wprev"], V["csp"], ACT.Exp, scale=-DECAY_C).then_inc(S["w_ready"], 1)
                for x in range(3):
                    n = 512 if x < 2 else T
                    rsqrt_of(take()[:, 0:n], rsB[:, 0:n], 1.0 / 64, C("small", 0, 1), "rs")
                short = [V[dst][:, c, :] for dst in ("cb", "cc", "ch") for c in range(2)]
                for b in range(SHORT_FIRST):
                    evac(short[b])
                for dst in ("vt", "bt", "kt"):
                    evac(V[dst], 512, shape=2)
                for x in range(2):
                    evac(V["kdup"][:, x, :])
                act.wait_ge(S["read_by_act"], w.n["read_by_act"])
                act.sem_inc(S["kdup_ready"], 1)
                exps, turned, output = attention(GROUPS, V["sc"], V["pr"], V["pT"], V["o"], sink=l)
                for lev in range(6):
                    for g in range(2):
                        evac(V["M1"][:, g, :], 512)
                        act.wait_ge(S["read_by_act"], w.n["read_by_act"])
                        act.sem_inc(S["m1_ready"], 1)
                    if lev:
                        turned(lev - 1)
                    exps(lev)
                    if lev:
                        output(lev - 1)
                    if SHORT_FIRST + lev < 6:
                        evac(short[SHORT_FIRST + lev])
                        if SHORT_FIRST + lev == 5:
                            act.wait_ge(S["read_by_act"], w.n["read_by_act"])
                            act.sem_inc(S["sconv_in"], 1)
                for c4 in range(4):
                    evac(V["R"], T)
                    act.wait_ge(S["read_by_act"], w.n["read_by_act"])
                    act.sem_inc(S["r_ready"], 1)
                    if 5 + c4 < len(GROUPS):
                        turned(5 + c4)
                    if 6 + c4 < len(GROUPS):
                        exps(6 + c4)
                    if 5 + c4 < len(GROUPS):
                        output(5 + c4)
                act.wait_ge(S["read_by_act"], w.n["read_by_act"])
                act.sem_inc(S["swa_ready"], 1)
                act.wait_ge(S["yc_ready"], w("yc_ready"))
                nc.scalar.activation(sq[:, 0:2, :], V["W"], ACT.Square).then_inc(S["yc_sq"], 1)
                rsqrt_of(take()[:, 0:512], rsB[:, 0:512], 1.0 / 64, C("small", 1, 2), "rs")
                act.wait_ge(S["mix_ready"], l + 1)
                at = split_first()
                norm(glu_next=True)
                at = glu(at, 5, 1, False, l < LAYERS - 1)
            for t in range(NT):
                for x in range(2):
                    evac(hT[:, 4 * t + 2 * x:4 * t + 2 * x + 2, :].rearrange("p a b -> p (a b)"), 512)
            act.wait_ge(S["read_by_act"], w.n["read_by_act"])
            act.dma_start(out[0].rearrange("(t p) d -> p t d", p=P),
                          hT[:, :, :].rearrange("p a b -> p (a b)").rearrange("p (t d) -> p t d", t=NT))\
                .then_inc(S["out_written"], 16)
            act.wait_ge(S["out_written"], 16)

        @block.vector
        def _(dve):
            w = Seen()
            banks = iter(for_dve)
            V_ = nc.vector
            starts = [n for n, _ in glu_starts]

            def take():
                dve.wait_ge(S["for_dve"], w("for_dve"))
                return bank[next(banks)]

            def read(ins):
                ins.then_inc(S["read_by_dve"], 1)
                dve.wait_ge(S["read_by_dve"], w("read_by_dve"))

            def step(ins):
                ins.then_inc(S["dve_step"], 1)
                w("dve_step")

            def later(k=0):
                dve.wait_ge(S["dve_step"], w.n["dve_step"] - k)

            def link(ins):
                step(ins)
                later()

            def norm(src, gain, dst, sem="hn", bias=None, split=False, hi=h_hi, lo=h_lo):
                dve.wait_ge(S["rs"], w("rs"))
                for j in range(KD + 3):
                    if j < KD:
                        ins = V_.scalar_tensor_tensor(dst[:, j, :], src[:, j, :], gain(j), rsB[:, 0:T],
                                                      ALU.mult, ALU.mult)
                        if bias is None:
                            ins.then_inc(S[sem], 1)
                        else:
                            step(ins)
                    if bias is not None and 1 <= j <= KD:
                        later(1 if j < KD else 0)
                        V_.tensor_scalar(dst[:, j - 1, :], dst[:, j - 1, :], bias(j - 1), None, ALU.add)\
                            .then_inc(S[sem], 1)
                    if j == KD:
                        dve.wait_ge(S[sem], w(sem, KD))
                        dve.sem_inc(S["rs_used"], 1)
                    if split and j >= 3:
                        dve.wait_ge(S["h_high"], w("h_high"))
                        V_.tensor_tensor(lo[:, j - 3, :], hT[:, j - 3, :], hi[:, j - 3, :].bitcast(F),
                                         ALU.subtract).then_inc(S["h_split"], 1)

            def split_low(x, n):
                dve.wait_ge(S[f"hi{x}_ready"], w(f"hi{x}_ready"))
                V_.tensor_tensor(w_lo[x][:, :], slab[n % SLOTS][:, :], w_hi[x][:, :].bitcast(F), ALU.subtract)\
                    .then_inc(S[f"lo{x}_ready"], 1)

            def scale_rs(dst, gain_col, nb):
                dve.wait_ge(S["rs"], w("rs"))
                link(V_.scalar_tensor_tensor(dst, dst, gain_col, rsB[:, 0:nb * T].rearrange("p (a b) -> p a b", a=nb)
                                             if nb > 1 else rsB[:, 0:T], ALU.mult, ALU.mult))
                dve.sem_inc(S["rs_used"], 1)

            def rope(x, nb, tmp, tmp2):
                ps = take()
                cos, sin = C("cos"), C("sin")
                tv, t2 = tmp[:, 0:nb * T], tmp2[:, 0:nb * T]
                src = ps[:, 0:nb * T]
                if nb > 1:
                    cos, sin = b3(cos, nb), b3(sin, nb)
                    tv, t2, src = (v.rearrange("p (a b) -> p a b", a=nb) for v in (tv, t2, src))
                read(V_.tensor_tensor(tv, src, sin, ALU.mult))
                link(V_.tensor_tensor(t2, x, cos, ALU.mult))
                link(V_.tensor_tensor(x, tv, t2, ALU.add))

            def attention(groups, sc, pr, scale, mask, mem=False, sink=None):
                width = [P * (t + 1) for t in range(NT)] if not mem else [T, T]
                nm, rsum, es, rr = tiny[:, 0:4], tiny[:, 4:8], tiny[:, 8:12], tiny[:, 12:16]

                def scaled(g):
                    t, h = groups[g]
                    wd, b = width[t], g % 2
                    ps = take()
                    src = ps[:, 0:2 * wd].rearrange("p (a b) -> p a b", a=2)
                    dst = sc[:, b, 0:2 * wd].rearrange("p (a b) -> p a b", a=2)
                    if mask is None:
                        read(V_.tensor_scalar(dst, src, scale, None, ALU.mult))
                    else:
                        read(V_.scalar_tensor_tensor(dst, src, scale, b3(mask(t), 2), ALU.mult, ALU.add))
                    link(V_.tensor_reduce(nm[:, 2 * b:2 * b + 2], dst, AX, ALU.max, negate=True))
                    if sink is not None:
                        for j in range(2):
                            sk = bbc[:, 36 + 8 * sink + h + 2 * j:37 + 8 * sink + h + 2 * j]
                            link(V_.tensor_scalar(rr[:, 2 * b + j:2 * b + j + 1], sk, -1.0, None, ALU.mult))
                            link(V_.tensor_tensor(nm[:, 2 * b + j:2 * b + j + 1], nm[:, 2 * b + j:2 * b + j + 1],
                                                  rr[:, 2 * b + j:2 * b + j + 1], ALU.min))
                    dve.sem_inc(S["att_max"], 1)

                def probabilities(g):
                    wd, b = width[groups[g][0]], g % 2
                    dve.wait_ge(S["att_exp"], w("att_exp"))
                    if sink is not None:
                        link(V_.tensor_tensor(rsum[:, 2 * b:2 * b + 2], rsum[:, 2 * b:2 * b + 2],
                                              es[:, 2 * b:2 * b + 2], ALU.add))
                    link(V_.reciprocal(rr[:, 2 * b:2 * b + 2], rsum[:, 2 * b:2 * b + 2]))
                    for j in range(2):
                        p = pr[:, b, j * wd:(j + 1) * wd]
                        step(V_.tensor_scalar(p, p, rr[:, 2 * b + j:2 * b + j + 1], None, ALU.mult))
                    later()
                    dve.sem_inc(S["att_p"], 1)
                return scaled, probabilities

            def attend(groups, *args, **kw):
                scaled, probabilities = attention(groups, *args, **kw)
                for g in range(len(groups) + 1):
                    if g < len(groups):
                        scaled(g)
                    if g:
                        probabilities(g - 1)

            def glu(at, turns, tail, moe, gate, more):
                mine = (0,) if moe else (0, 1)

                A1, A2 = 4, 5

                def ada_ops(k0, k1, u):
                    for kc in range(k0, k1):
                        acc = M["ada_acc"][:, u, :]
                        if kc == 0:
                            dve.wait_ge(S[f"ada_in{u}"], w(f"ada_in{u}", 16))
                            ins = V_.tensor_scalar(acc, ada_in[u][:, 0, :], c_act[:, 0:1], None, ALU.mult)
                        else:
                            ins = V_.scalar_tensor_tensor(acc, ada_in[u][:, kc, :], c_act[:, kc:kc + 1], acc,
                                                          ALU.mult, ALU.add)
                        ins.then_inc(S["ada_step"], 1)
                        dve.wait_ge(S["ada_step"], w("ada_step"))

                def unit(i, u, pos, more, mine=mine, last=False):
                    for j in range(2):
                        dve.wait_ge(S["silu_ready"], w("silu_ready"))
                        if moe:
                            if j == 0:
                                dve.wait_ge(S["comb_done"], w("comb_done"))
                            V_.tensor_tensor(silu[:, j, :], silu[:, j, :], bank[2][:, 0:T], ALU.mult)\
                                .then_inc(S["gut"], 1)
                            dve.wait_ge(S["gut"], w("gut"))
                        V_.tensor_tensor(gu[:, j, :], silu[:, j, :], bank[j][:, T:2 * T], ALU.mult)\
                            .then_inc(S["gut"], 1)
                        dve.wait_ge(S["gut"], w("gut"))
                        V_.tensor_copy(gu_hi[:, j, :], gu[:, j, :]).then_inc(S["gut"], 1)
                        dve.wait_ge(S["gut"], w("gut"))
                        V_.tensor_tensor(gu_lo[:, j, :], gu[:, j, :], gu_hi[:, j, :].bitcast(F), ALU.subtract)\
                            .then_inc(S["gu_ready"], 1)
                        if more and j in mine:
                            split_low(j, pos + j)
                        if moe and not last and j == 0:
                            select(i * 2 + u + 1, 1 - u)
                        if moe and u == 1 and j == 0:
                            ada_ops(A1, A2, 1)
                    if moe:
                        if u == 0:
                            ada_ops(0, KD, 0)
                            ada_ops(0, A1, 1)
                        else:
                            ada_ops(A2, KD, 1)
                            dve.sem_inc(S["ada_done"], 1)
                            dve.wait_ge(S["ada_sum"], w("ada_sum"))
                            V_.tensor_tensor(ada[:, bass.ds(i * 9, 9)], bank[3][:, 0:9], b_ada[:, bass.ds(i * 9, 9)],
                                             ALU.add).then_inc(S["ada_ready"], 1)

                loop = turns if tail else turns - 1
                with dve.Fori(0, loop) as i:
                    w.enter(i, {"silu_ready": 4, "gut": 12 if moe else 8, "comb_done": 2, "ada_in0": 16, "ada_in1": 16, "ada_step": 16,
                                "ada_sum": 1, "hi0_ready": 2, "hi1_ready": 2})
                    for u in range(2):
                        unit(i, u, at + 3 * (u + 1), True)
                    w.leave(loop)
                if tail:
                    unit(turns, 0, at + 3, more)
                else:
                    unit(turns - 1, 0, at + 3, True)
                    w("hi1_ready", N_EXP)
                    unit(turns - 1, 1, at + 6, more, (0, 1), True)
                dve.wait_ge(S["down_done"], w("down_done", 2 * turns + tail))
                if moe:
                    dve.wait_ge(S["ada_ready"], turns)
                for d in range(KD):
                    ps = bank[4 + d // 2][:, (d % 2) * T:(d % 2 + 1) * T]
                    if gate is None:
                        ins = V_.tensor_tensor(xT[:, d, :], xT[:, d, :], ps, ALU.add)
                    else:
                        ins = V_.scalar_tensor_tensor(xT[:, d, :], ps, gate(d), xT[:, d, :], ALU.mult, ALU.add)
                    ins.then_inc(S["x_ready"], 1)
                dve.wait_ge(S["x_ready"], w("x_ready", KD))

            def select(e, u):
                eye = const[0:N_EXP, bass.ds(CW["eye"][0] + e, 1)]
                V_.tensor_scalar(sel[0:N_EXP, u, :], combT[0:N_EXP, 0:T], eye, None, ALU.mult).then_inc(S["sel"], 1)

            dve.wait_ge(S["params"], w("params"))
            link(V_.memset(B1["u"][:, :, 0:30], 0.0))
            norm(xT, lambda j: col("g_mix", j), hT)
            norm(memT, lambda j: col("g_mem", j), B1["memh"], "memh")
            dve.sem_inc(S["memh_all"], 1)
            dve.wait_ge(S["const_more"], w("const_more", 16))
            dve.wait_ge(S["params_more"], w("params_more"))
            scale_rs(B1["ki"], col("g_idx_k"), 1)
            dve.sem_inc(S["ki_normed"], 1)
            for x in range(2):
                rope(B1["qi"][:, 2 * x:2 * x + 2, :], 2, B1["tmp"], B1["tmp2"])
            rope(B1["ki"], 1, B1["tmp"], B1["tmp2"])
            dve.sem_inc(S["idx_roped"], 1)
            for x in range(2):
                scale_rs(B1["qa"][:, 2 * x:2 * x + 2, :], col("g_qa"), 2)
            scale_rs(B1["ka"], col("g_ka"), 1)
            dve.sem_inc(S["qka_normed"], 1)
            for g, (t, h) in enumerate(GROUPS):
                wd = P * (t + 1)
                dve.wait_ge(S["rl_ready"], w("rl_ready"))
                for j in range(2):
                    wcol = B1["wi"][:, t, h + 2 * j:h + 2 * j + 1]
                    src, dst = B1["rl"][:, g % 2, j, 0:wd], B1["score"][:, t, 0:wd]
                    if h == 0 and j == 0:
                        link(V_.tensor_scalar(dst, src, wcol, None, ALU.mult))
                    else:
                        link(V_.scalar_tensor_tensor(dst, src, wcol, dst, ALU.mult, ALU.add))
                dve.sem_inc(S["rl_used"], 1)
            for x in range(2):
                rope(B1["qa"][:, 2 * x:2 * x + 2, :], 2, B1["tmp"], B1["tmp2"])
            dve.sem_inc(S["qa_roped"], 1)
            rope(B1["ka"], 1, B1["tmp"], B1["tmp2"])
            dve.sem_inc(S["ka_roped"], 1)
            for t in range(NT):
                wd = P * (t + 1)
                pick = B1["pick"][:, t, 0:wd]
                link(V_.tensor_tensor(pick, B1["score"][:, t, 0:wd], C(f"causal{t}"), ALU.add))
                for r in range(TOPK // 8):
                    link(V_.max(tiny[:, 16:24], pick))
                    link(V_.match_replace(pick, tiny[:, 16:24], pick, PAD))
                link(V_.tensor_scalar(pick, pick, PAD, 1.0, ALU.is_equal, ALU.subtract))
                link(V_.scalar_tensor_tensor(B1["amask"][:, t, 0:wd], pick, -NEG, C(f"causal{t}"),
                                             ALU.mult, ALU.add))
            dve.sem_inc(S["dsa_mask"], 1)
            dve.wait_ge(S["glu_in"], w("glu_in"))
            link(V_.tensor_tensor(B1["u"][:, :, 30:30 + T], B1["u"][:, :, 30:30 + T], B1["ug"], ALU.mult))
            for k in range(TAPS):
                if k == TAPS_FIRST:
                    later()
                    for x in range(4):
                        nm = "qm" if x < 2 else "km"
                        scale_rs(B1[nm][:, 2 * (x % 2):2 * (x % 2) + 2, :], col("g_qm" if x < 2 else "g_km"), 2)
                    dve.sem_inc(S["qkm_normed"], 1)
                for c in range(4):
                    src, tap = B1["u"][:, c, k:k + T], taps[:, k * 4 + c:k * 4 + c + 1]
                    if k == 0:
                        step(V_.tensor_scalar(B1["y"][:, c, :], src, tap, col("conv_b", c), ALU.mult, ALU.add))
                    else:
                        later(3)
                        step(V_.scalar_tensor_tensor(B1["y"][:, c, :], src, tap, B1["y"][:, c, :],
                                                     ALU.mult, ALU.add))
            later()
            dve.sem_inc(S["conv_y"], 1)
            ps = take()
            for c in range(4):
                ins = V_.scalar_tensor_tensor(B1["y"][:, c, :], ps[:, 0:T], -1.0 / 512, B1["y"][:, c, :],
                                              ALU.mult, ALU.add)
                if c < 3:
                    step(ins)
            later()
            read(ins)
            dve.sem_inc(S["yc_ready"], 1)
            dve.wait_ge(S["rs"], w("rs"))
            for c in range(4):
                step(V_.scalar_tensor_tensor(B1["y"][:, c, :], B1["y"][:, c, :], col("ln_g", c), rsB[:, 0:T],
                                             ALU.mult, ALU.mult))
            later()
            dve.sem_inc(S["rs_used"], 1)
            dve.sem_inc(S["yn_ready"], 1)
            def merge(br, d):
                ps = take()
                g = B1["gate"][:, br * KD + d, :]
                if br == 1:
                    read(V_.tensor_tensor(B1["merged"][:, d, :], g, ps[:, 0:T], ALU.mult))
                else:
                    read(V_.tensor_tensor(B1["tmp"][:, 0:T], g, ps[:, 0:T], ALU.mult))
                    link(V_.tensor_tensor(B1["merged"][:, d, :], B1["merged"][:, d, :], B1["tmp"][:, 0:T],
                                          ALU.add))
            own = attention(GROUPS, B1["sc"], B1["pr"], 64 ** -0.5, lambda t: B1["amask"][:, t, 0:P * (t + 1)])
            mem = attention(MEM_GROUPS, B1["sc"], B1["pr"], P ** -0.5, None, mem=True)
            both = [(own, g) for g in range(len(GROUPS))] + [(mem, g) for g in range(len(MEM_GROUPS))]
            for i in range(len(both) + 2):
                if i < len(both):
                    (scaled, _), g = both[i]
                    scaled(g)
                if 1 <= i <= len(both):
                    (_, probabilities), g = both[i - 1]
                    probabilities(g)
                for d in fillers(i):
                    merge(1 if i <= len(GROUPS) else 0, d)
            for d in range(KD):
                merge(2, d)
            dve.sem_inc(S["merged"], 1)

            def residual(gate):
                for d in range(KD):
                    ps = take()
                    if gate is None:
                        read(V_.tensor_tensor(xT[:, d, :], xT[:, d, :], ps[:, 0:T], ALU.add))
                    else:
                        read(V_.scalar_tensor_tensor(xT[:, d, :], ps[:, 0:T], gate(d), xT[:, d, :],
                                                     ALU.mult, ALU.add))
                    dve.sem_inc(S["x_ready"], 1)
                w("x_ready", KD)
            at = starts.pop(0)
            split_low(0, at)
            residual(None)
            norm(xT, lambda j: col("g_ffn", j), hT, split=True)

            ps = take()
            for t in range(NT):
                link(V_.memset(route("gpad", t, 16), PAD))
                link(V_.memset(route("epad", t, 48), PAD))
                link(V_.memset(route("list1", t, 8), PAD))
                link(V_.memset(route("list2", t, 8), PAD))
                ins = V_.tensor_tensor(route("lg", t, 36), ps[:, t * 64:t * 64 + 36], bbc[:, 0:36], ALU.add)
                if t == 0:
                    link(ins)
            read(ins)
            for t in range(NT):
                r = lambda nm, n, t=t: route(nm, t, n)
                link(V_.tensor_copy(r("gpad", 4), r("lg", 4)))
                link(V_.max(r("g8", 8), r("gpad", 16)))
                link(V_.tensor_copy(r("list1", 1), r("g8", 1)))
                link(V_.tensor_scalar(r("ngmax", 1), r("g8", 1), -1.0, None, ALU.mult))
            dve.sem_inc(S["router_max"], 1)
            for t in range(NT):
                r = lambda nm, n, t=t: route(nm, t, n)
                link(V_.match_replace(r("gpad", 16), r("list1", 8), r("gpad", 16), TAKEN1))
                link(V_.tensor_scalar(r("goh", 4), r("gpad", 4), TAKEN1, None, ALU.is_equal))
                link(V_.tensor_scalar(r("gneg", 4), r("goh", 4), 1.0, -NEG, ALU.subtract, ALU.mult))
                e = r("epad", 32).rearrange("p (g e) -> p g e", g=N_GROUP)
                lg = route("lg", t, 36)[:, 4:36].rearrange("p (g e) -> p g e", g=N_GROUP)
                wide = lambda v: v.unsqueeze(2).to_broadcast([P, N_GROUP, PER_GROUP])
                link(V_.tensor_tensor(e, lg, wide(r("goh", 4)), ALU.mult))
                link(V_.tensor_tensor(e, e, wide(r("gneg", 4)), ALU.add))
                link(V_.max(r("e8", 8), r("epad", 48)))
                link(V_.tensor_scalar(r("nv1", 1), r("e8", 1), -1.0, None, ALU.mult))
            dve.sem_inc(S["router_top2"], 1)
            dve.wait_ge(S["router_exp"], w("router_exp", 2))
            for t in range(NT):
                r = lambda nm, n, t=t: route(nm, t, n)
                link(V_.tensor_copy(r("list1", 1), r("e8", 1)))
                link(V_.tensor_copy(r("list2", 1), route("e8", t, 8)[:, 1:2]))
                link(V_.match_replace(r("epad", 48), r("list1", 8), r("epad", 48), TAKEN1))
                link(V_.match_replace(r("epad", 48), r("list2", 8), r("epad", 48), TAKEN2))
                link(V_.tensor_scalar(r("d", 1), r("e21", 1), 1.0, r("gsum", 1), ALU.add, ALU.mult))
                link(V_.reciprocal(r("w1", 1), r("d", 1)))
                link(V_.tensor_tensor(r("w2", 1), r("w1", 1), r("e21", 1), ALU.mult))
                comb = tiny[:, 96 + t * N_EXP:96 + (t + 1) * N_EXP]
                link(V_.tensor_scalar(comb, r("epad", 32), TAKEN1, r("w1", 1), ALU.is_equal, ALU.mult))
                link(V_.tensor_scalar(r("epad", 32), r("epad", 32), TAKEN2, r("w2", 1), ALU.is_equal, ALU.mult))
                link(V_.tensor_tensor(comb, comb, r("epad", 32), ALU.add))
            dve.sem_inc(S["comb_ready"], 1)
            dve.wait_ge(S["comb_turned"], w("comb_turned"))
            link(V_.tensor_copy(combT[0:N_EXP, 0:T], bank[3][0:N_EXP, 0:T]))
            select(0, 0)
            dve.wait_ge(S["c_act"], w("c_act"))
            glu(at, N_EXP // 2, 0, True, None, True)

            _, _, n2 = par_at("g_ffn1_2", 0)
            for l in range(LAYERS):
                at = 72 * l
                for s, name in enumerate(("g_ffn1_2", "g_mix_2", "g_ffn2_2")):
                    tile, ga, _ = par_at(name, l)
                    link(V_.scalar_tensor_tensor(modg[:, l * 6 + s, :], ada[:, at + (3 * s + 1) * 8:at + (3 * s + 2) * 8],
                                                 1.0, tile[:, ga:ga + 8], ALU.add, ALU.mult))
                    f = 1.0 if s == 1 else 0.5
                    link(V_.tensor_scalar(modg[:, l * 6 + 3 + s, :], ada[:, at + (3 * s + 2) * 8:at + (3 * s + 3) * 8],
                                          1.0, f, ALU.add, ALU.mult))

            for l in range(LAYERS):
                V = B2
                gain = lambda s, l=l: (lambda j: modg[:, l * 6 + s, j:j + 1])
                shift = lambda s, l=l: (lambda j: ada[:, 72 * l + 3 * s * 8 + j:72 * l + 3 * s * 8 + j + 1])
                gate = lambda s, l=l: (lambda j: modg[:, l * 6 + 3 + s, j:j + 1])

                def flat(nm):
                    return V[nm].rearrange("p a b -> p (a b)")
                at = starts.pop(0)
                norm(xT, gain(0), hT, bias=shift(0), split=True)
                glu(at, 5, 1, False, gate(0), False)
                norm(xT, gain(1), hT, bias=shift(1), split=True, hi=m_hi, lo=m_lo)
                link(V_.memset(V["praw"][:, :, 0:1], 0.0))
                link(V_.memset(V["cu"][:, :, 0:2], 0.0))
                link(V_.memset(flat("state"), 0.0))
                dve.sem_inc(S["state_ready"], 1)
                dve.wait_ge(S["praw_ready"], w("praw_ready"))
                link(V_.tensor_tensor(V["ysh"], V["praw"][:, :, 0:T], V["praw"][:, :, 1:1 + T], ALU.subtract))
                for b in (6, 7, 2, 3, 0, 1, 4, 5):
                    step(V_.scalar_tensor_tensor(V["pm"][:, b, :], V["ysh"][:, b, :], col("rwkv_mu_2", b, l),
                                                 V["praw"][:, b, 1:1 + T], ALU.mult, ALU.add))
                later()
                dve.sem_inc(S["pm_ready"], 1)
                r_, k_, v_ = V["pm"][:, 0:2, :], V["pm"][:, 2:4, :], V["pm"][:, 4:6, :]
                for c in range(2):
                    step(V_.tensor_scalar(V["kk"][:, c, :], k_[:, c, :], col("rwkv_k_k_2", c, l), None, ALU.mult))
                later()
                dve.sem_inc(S["kk_raw"], 1)
                dve.wait_ge(S["sw_ready"], w("sw_ready"))
                for c in range(2):
                    step(V_.tensor_tensor_scan(V["cs"][:, c, :], C("reset"), V["sw"][:, c, :], 0.0, ALU.mult, ALU.add))
                later()
                link(V_.tensor_tensor(flat("csp"), flat("cs"), flat("sw"), ALU.subtract))
                dve.sem_inc(S["cs_ready"], 1)
                ps = take()
                read(V_.tensor_scalar(rsB[:, :], ps[:, :], 1e-24, float(2 ** KK_SHIFT), ALU.max, ALU.mult))
                dve.sem_inc(S["kk_sum"], 1)
                for c in range(2):
                    step(V_.tensor_scalar(V["ysh"][:, 2 + c, :], V["aa"][:, c, :], 1.0, col("rwkv_k_a_2", c, l),
                                          ALU.subtract, ALU.mult))
                later()
                link(V_.scalar_tensor_tensor(k_, V["ysh"][:, 2:4, :], 1.0, k_, ALU.add, ALU.mult))
                for c in range(2):
                    step(V_.scalar_tensor_tensor(V["ysh"][:, c, :], r_[:, c, :], col("rwkv_r_k_2", c, l),
                                                 k_[:, c, :], ALU.mult, ALU.mult))
                later()
                dve.sem_inc(S["bonus_in"], 1)
                dve.wait_ge(S["rs"], w("rs"))
                link(V_.tensor_tensor(flat("kk"), flat("kk"), rsB[:, :], ALU.mult))
                dve.sem_inc(S["rs_used"], 1)
                dve.wait_ge(S["w_ready"], w("w_ready"))
                step(V_.tensor_tensor(flat("al"), flat("kk"), flat("Wprev"), ALU.mult))
                step(V_.tensor_tensor(flat("csp"), flat("kk"), flat("aa"), ALU.mult))
                step(V_.tensor_tensor(V["kap"], k_, V["Winv"], ALU.mult))
                step(V_.tensor_tensor(V["rho"], r_, V["W"], ALU.mult))
                later(2)
                step(V_.tensor_tensor(flat("be"), flat("csp"), flat("Winv"), ALU.mult))
                for c in range(2):
                    for c4 in range(4):
                        step(V_.tensor_copy(tiny[:, 24 + c * 4 + c4:25 + c * 4 + c4],
                                            V["W"][:, c, (c4 + 1) * CHUNK - 1:(c4 + 1) * CHUNK]))
                later()
                dve.sem_inc(S["rwkv_in"], 1)
                for x in range(3):
                    dst = V["q"][:, 2 * x:2 * x + 2, :] if x < 2 else V["k"]
                    scale_rs(dst, col("att_q_gain_2" if x < 2 else "att_k_gain_2", 0, l), 2 if x < 2 else 1)
                dve.sem_inc(S["att_normed"], 1)
                ps = take()
                read(V_.tensor_tensor(flat("bon"), ps[:, :], v_.rearrange("p a b -> p (a b)"), ALU.mult))
                for dst, mask in (("AT", "strict"), ("BT", "strict"), ("C1T", "incl"), ("C2T", "incl")):
                    for g in range(2):
                        ps = take()
                        read(V_.tensor_tensor(V[dst][:, g, :].rearrange("p (a b) -> p a b", a=4),
                                              ps[:, :].rearrange("p (a b) -> p a b", a=4), b3(C(mask), 4), ALU.mult))
                        if dst == "AT":
                            for o in ("Tm", "TT"):
                                step(V_.tensor_copy(V[o][:, g, :].rearrange("p (a b) -> p a b", a=4), b3(C("eye"), 4)))
                            link(V_.tensor_tensor(V["off"][:, g, :].rearrange("p (a b) -> p a b", a=4),
                                                  V["AT"][:, g, :].rearrange("p (a b) -> p a b", a=4),
                                                  b3(C("level0"), 4), ALU.mult))
                            dve.sem_inc(S["off_ready"], 1)
                scaled, probabilities = attention(GROUPS, V["sc"], V["pr"], 64 ** -0.5,
                                                  lambda t: C("causal0") if t == 0 else C("window1"), sink=l)
                for lev in range(6):
                    scaled(lev)
                    for g in range(2):
                        if lev < 5:
                            ps = take()
                            read(V_.tensor_tensor(V["Tm"][:, g, :], V["Tm"][:, g, :], ps[:, :], ALU.subtract))
                        ps = take()
                        read(V_.tensor_tensor(V["TT"][:, g, :], V["TT"][:, g, :], ps[:, :], ALU.subtract))
                        if lev < 5:
                            link(V_.tensor_tensor(V["off"][:, g, :].rearrange("p (a b) -> p a b", a=4),
                                                  V["AT"][:, g, :].rearrange("p (a b) -> p a b", a=4),
                                                  b3(C(f"level{lev + 1}"), 4), ALU.mult))
                            dve.sem_inc(S["off_ready"], 1)
                    if lev == 5:
                        dve.sem_inc(S["solve_ready"], 1)
                    probabilities(lev)
                for c4 in range(4):
                    t, r0 = c4 // 2, (c4 % 2) * CHUNK
                    if 6 + c4 < len(GROUPS):
                        scaled(6 + c4)
                    ps = take()
                    read(V_.tensor_scalar(V["negU"][r0:r0 + CHUNK, t, :], ps[r0:r0 + CHUNK, 0:T], -1.0, None, ALU.mult))
                    dve.sem_inc(S["u_ready"], 1)
                    if c4 < 3:
                        ps = take()
                        read(V_.tensor_tensor(flat("state"), ps[:, 0:T], flat("state"), ALU.add))
                        for c in range(2):
                            step(V_.scalar_tensor_tensor(V["state"][:, c, :], V["state"][:, c, :],
                                                         tiny[:, 24 + c * 4 + c4:25 + c * 4 + c4], C("half"),
                                                         ALU.mult, ALU.mult))
                        later()
                        dve.sem_inc(S["state_ready"], 1)
                    if 6 + c4 < len(GROUPS):
                        probabilities(6 + c4)
                dve.wait_ge(S["sconv_in"], w("sconv_in"))
                link(V_.tensor_tensor(V["cu"][:, :, 2:2 + T], V["cc"], V["ch"], ALU.mult))
                for k in range(3):
                    for c in range(2):
                        src, tap = V["cu"][:, c, k:k + T], col("conv_w_2", 2 * k + c, l)
                        if k == 0:
                            step(V_.tensor_scalar(V["cy"][:, c, :], src, tap, None, ALU.mult))
                        else:
                            later(1)
                            step(V_.scalar_tensor_tensor(V["cy"][:, c, :], src, tap, V["cy"][:, c, :],
                                                         ALU.mult, ALU.add))
                later()
                link(V_.tensor_tensor(flat("cy"), flat("cy"), flat("cb"), ALU.mult))
                dve.sem_inc(S["conv_ready"], 1)
                dve.wait_ge(S["y_done"], w("y_done"))
                link(V_.tensor_copy(flat("W"), bank[7][:, :]))
                dve.sem_inc(S["y_ready"], 1)
                ps = take()
                read(V_.scalar_tensor_tensor(flat("W"), ps[:, :], -1.0 / 64, flat("W"), ALU.mult, ALU.add))
                dve.sem_inc(S["yc_ready"], 1)
                dve.wait_ge(S["rs"], w("rs"))
                for c in range(2):
                    step(V_.scalar_tensor_tensor(V["W"][:, c, :], V["W"][:, c, :], col("rwkv_gn_w_2", c, l),
                                                 rsB[:, c * T:(c + 1) * T], ALU.mult, ALU.mult))
                later()
                dve.sem_inc(S["rs_used"], 1)
                for c in range(2):
                    step(V_.scalar_tensor_tensor(V["W"][:, c, :], V["W"][:, c, :], col("rwkv_gn_b_2", c, l),
                                                 V["bon"][:, c, :], ALU.add, ALU.add))
                later()
                link(V_.tensor_tensor(flat("yr"), flat("W"), flat("gB"), ALU.mult))
                dve.sem_inc(S["mix_ready"], 1)
                at = starts.pop(0)
                split_low(0, at)
                split_low(1, at + 1)
                residual(gate(1))
                norm(xT, gain(2), hT, bias=shift(2), split=True)
                glu(at, 5, 1, False, gate(2), l < LAYERS - 1)
            for i in range(KD):
                dve.sem_inc(S["x_ready_pe"], 1)

        @block.sync
        def _(sp):
            w = Seen()
            n_slab = [0]

            def before(n):
                if n >= SLOTS:
                    name, k = slab_end[n - SLOTS]
                    sp.wait_ge(S[name], k)

            def load(src, view=None, first=True):
                n = n_slab[0]
                if first:
                    before(n)
                dst = slab[n % SLOTS]
                sp.dma_start(view(dst) if view else dst[:, :], src).then_inc(S[f"slab{n % SLOTS}_in"], 16)

            def done():
                n_slab[0] += 1

            def matrix(src, c0, cols, kc=KD, width=None):
                width = SLAB // kc
                for c in range(0, cols, width):
                    load(src[:, c0 + c:c0 + c + width].rearrange("(k p) c -> p k c", p=P),
                         lambda d: d[:, :].rearrange("p (k c) -> p k c", k=kc))
                    done()

            def glu_loads(w_up, w_down, f0, half, slot, waits):
                for x in range(3):
                    s = (slot + x) % SLOTS
                    if waits:
                        sp.wait_ge(S[waits[x][0]], waits[x][1])
                    if x < 2:
                        for ab in range(2):
                            src = w_up(ab * half, f0 + x * P)
                            dst = slab[s][:, :].rearrange("p (k c) -> p k c", k=KD)[:, :, ab * P:(ab + 1) * P]
                            sp.dma_start(dst, src).then_inc(S[f"slab{s}_in"], 16)
                    else:
                        sp.dma_start(slab[s][:, :].rearrange("p (j d) -> p j d", j=2), w_down(f0))\
                            .then_inc(S[f"slab{s}_in"], 16)

            def glu(turns, tail, up, down, half):
                n0 = n_slab[0]
                for u in range(2):
                    n = n0 + 3 * u
                    glu_loads(lambda ab, f, u=u: up(0, u, ab, f), lambda f, u=u: down(0, u, f), 0, half, n,
                              [slab_end[n + x - SLOTS] for x in range(3)])
                with sp.Fori(1, turns) as i:
                    for u in range(2):
                        n = n0 + 3 * u
                        waits = [(slab_end[n + x][0], (i - 1) * 2 + slab_end[n + x][1])
                                 for x in range(3)]
                        glu_loads(lambda ab, f, u=u: up(i, u, ab, f), lambda f, u=u: down(i, u, f), 0, half, n, waits)
                n_slab[0] += 6 * turns
                for u in range(tail):
                    n = n_slab[0]
                    glu_loads(lambda ab, f, u=u: up(turns, u, ab, f), lambda f, u=u: down(turns, u, f), 0, half, n,
                              [slab_end[n + x - SLOTS] for x in range(3)])
                    n_slab[0] += 3

            first_c = CW["half"][0]
            sp.dma_start(const[:, 0:first_c], a["const"][:, 0:first_c]).then_inc(S["const_in"], 16)
            sp.dma_start(xin, a["x"][0].rearrange("(t p) d -> p t d", p=P)).then_inc(S["x_in"], 16)
            w_in = a["w_in"][0]
            matrix(w_in, 768, 512)
            sp.dma_start(memin, a["mem"][0].rearrange("(t p) d -> p t d", p=P)).then_inc(S["mem_in"], 16)
            for x, (c0, cn, d0) in enumerate(((1280, 64, 0), (1280, 64, 64), (1344, 8, 128))):
                load(w_in[:, c0:c0 + cn].rearrange("(k p) c -> p k c", p=P),
                     lambda d, d0=d0, cn=cn: d[:, :].rearrange("p (k c) -> p k c", k=KD)[:, :, d0:d0 + cn], x == 0)
            done()
            matrix(w_in, 512, 256)
            sp.dma_start(const[:, first_c:], a["const"][:, first_c:]).then_inc(S["const_more"], 16)
            matrix(w_in, 0, 512)
            matrix(w_in, 1352, 1024)
            matrix(w_in, 2376, 512)
            matrix(a["w_mem_kv"][0], 0, 1024)
            matrix(w_in, 2888, 3072)
            for name in ("w_br_b", "w_br_a", "w_br_m"):
                matrix(a[name][0], 0, D, kc=4)
            matrix(a["w_o"][0], 0, D)

            def moe_up(i, u, ab, f):
                wv = a["w_up"][0].rearrange("e r c -> (e r) c")
                return wv[bass.ds(i * 2 * D + u * D, D), ab + f:ab + f + P].rearrange("(k p) c -> p k c", p=P)

            def moe_down(i, u, f):
                wv = a["w_down"][0].rearrange("e r c -> (e r) c")
                return wv[bass.ds(i * 512 + u * 256, 256), :].rearrange("(j p) d -> p j d", p=P)
            glu(N_EXP // 2, 0, moe_up, moe_down, 256)

            for l in range(LAYERS):
                def ffn(up_w, down_w):
                    def up(i, u, ab, f):
                        return up_w[:, bass.ds(i * 512 + (u * 256 + ab + f), P)].rearrange("(k p) c -> p k c", p=P)

                    def down(i, u, f):
                        rows_ = bass.ds(i * 512 + u * 256, 256)
                        return down_w[rows_, :].rearrange("(j p) d -> p j d", p=P)
                    glu(5, 1, up, down, D_FF)
                ffn(a["w_ffn1_in_2"][l], a["w_ffn1_out_2"][l])
                wm = a["w_mix_in_2"][l]
                matrix(wm, 768, 1024)
                matrix(wm, 0, 768)
                matrix(wm, 1792, 768)
                matrix(a["w_mix_out_2"][l], 0, D)
                ffn(a["w_ffn2_in_2"][l], a["w_ffn2_out_2"][l])

        @block.gpsimd
        def _(pool):
            w = Seen()
            for dst, src in other_rows():
                pool.dma_start(dst, src).then_inc(S["others_in"], 16)

            def split_low(x, n):
                pool.wait_ge(S[f"hi{x}_ready"], w(f"hi{x}_ready"))
                nc.gpsimd.tensor_tensor(w_lo[x][:, :], slab[n % SLOTS][:, :], w_hi[x][:, :].bitcast(F), ALU.subtract)\
                    .then_inc(S[f"lo{x}_ready"], 1)

            def glu(at, turns, moe):
                mine = (1, 2) if moe else (2,)
                for x in mine:
                    split_low(x, at + x)
                if not moe:
                    w("hi1_ready", 2 * turns + 1)
                loop = turns - 1 if moe else turns
                with pool.Fori(0, loop) as i:
                    w.enter(i, {f"hi{x}_ready": 2 for x in mine})
                    for u in range(2):
                        for x in mine:
                            split_low(x, at + 3 * (u + 1) + x)
                    w.leave(loop)
                if moe:
                    for x in mine:
                        split_low(x, at + 3 + x)

            low_slabs = iter(low_used)

            def split_slabs(n, w_hi):
                for k in range(n):
                    slot, _ = next(low_slabs)
                    pool.wait_ge(S["phi_ready"], w("phi_ready"))
                    nc.gpsimd.tensor_tensor(slab_low[slot][:, :], slab[slot][:, :], w_hi[k % 3][:, :].bitcast(F),
                                            ALU.subtract).then_inc(S["plo_ready"], 1)

            pool.wait_ge(S["p_high"], 1)
            nc.gpsimd.tensor_tensor(p_lo[:, :, :], hT[:, :, :], p_hi[:, :, :].bitcast(F), ALU.subtract)\
                .then_inc(S["p_split"], 1)
            split_slabs(6, early_hi)
            split_slabs(12, gates_hi)
            for n, (at, _) in enumerate(glu_starts):
                glu(at, N_EXP // 2 if n == 0 else 5, n == 0)
                if n and n % 2:
                    split_slabs(6, mix_hi)


ROW_COUNTS = [sum(n for _, n in ROWS_1), LAYERS * sum(n for _, n in ROWS_2), TAPS * 4, 72, 72,
              sum(n for _, n in ROWS_0)]

INPUTS = ["x", "mem", "g_mix", "w_in", "b_gate", "g_qa", "g_ka", "g_idx_k", "conv_w", "conv_b", "ln_g", "ln_b",
          "g_mem", "w_mem_kv", "g_qm", "g_km", "w_br_a", "w_br_b", "w_br_m", "w_o", "g_ffn", "w_rg", "b_rg",
          "w_re", "b_re", "w_up", "w_down", "c_2", "w_ada_2", "b_ada_2", "g_ffn1_2", "w_ffn1_in_2",
          "w_ffn1_out_2", "g_mix_2", "w_mix_in_2", "w_mix_out_2", "att_q_gain_2", "att_k_gain_2",
          "att_sinks_2", "rwkv_mu_2", "rwkv_w0_2", "rwkv_w_w2_2", "rwkv_a0_2", "rwkv_a_w2_2", "rwkv_g_w2_2",
          "rwkv_k_k_2", "rwkv_k_a_2", "rwkv_r_k_2", "rwkv_gn_w_2", "rwkv_gn_b_2", "conv_w_2", "g_ffn2_2",
          "w_ffn2_in_2", "w_ffn2_out_2"]


def kernel(**inputs):
    import concourse.bacc as bacc
    from concourse.bass_utils import run_bass_kernel_spmd

    nc = bacc.Bacc("TRN2", target_bir_lowering=False, num_devices=1)
    arrays, a = {}, {}
    for name in INPUTS:
        v = np.ascontiguousarray(inputs[name])
        arrays["in_" + name] = v
        a[name] = nc.dram_tensor("in_" + name, v.shape, mybir.dt.from_np(v.dtype), kind="ExternalInput").ap()
    v = _constants()[0]
    arrays["in_const"] = v
    a["const"] = nc.dram_tensor("in_const", v.shape, mybir.dt.float32, kind="ExternalInput").ap()
    out = nc.dram_tensor("out_x", (1, T, D), mybir.dt.float32, kind="ExternalOutput").ap()
    build(nc, a, out)
    r = run_bass_kernel_spmd(nc, [arrays], core_ids=[0])
    return r.results[0]["out_x"]
```
